# Optimizing a Trainium2 kernel written in Bass

```python
import math
import jax, jax.numpy as jnp
from jax import lax
import numpy as np

D_MODEL = 1024
BATCH = 1
SEQ = 1024
DEPTH = 1
DEC_BATCH = 8
DEC_SEQ = 16
PAST_LEN = 256

CHUNK = 64
Q_BLOCK = 128
RET_HEADS = 8
RET_HD = 64
FOX_HEADS = 8
FOX_HD = 64
D_RET = RET_HEADS * RET_HD
D_FOX = FOX_HEADS * FOX_HD
D_MIX = D_RET + D_FOX
IN_COLS = 4 * D_RET + 3 * D_FOX + FOX_HEADS
SPLITS = [D_RET, 2 * D_RET, 3 * D_RET, 4 * D_RET, 4 * D_RET + D_FOX, 4 * D_RET + 2 * D_FOX, 4 * D_RET + 3 * D_FOX]
ROPE_BASE = 10000.0
N_KEYS = 128
N_EXPERTS = N_KEYS * N_KEYS
PEER_HEADS = 8
PEER_DKEY = 256
PEER_HALF = PEER_DKEY // 2
PEER_TOPK = 16
PEER_BLOCK = 128
EPS = 1e-6

kernel_name = 'retention_fox_peer_streaming_step'

F32 = jnp.float32

def rms_norm(x, g):
    xf = x.astype(F32)
    y = xf * lax.rsqrt(jnp.mean(xf * xf, axis=-1, keepdims=True) + EPS)
    return (y * g.astype(F32)).astype(x.dtype)

def rotary(x, pos):
    half = x.shape[-1] // 2
    inv = ROPE_BASE ** (-jnp.arange(half, dtype=F32) / half)
    ang = pos.astype(F32)[:, None] * inv[None, :]
    cos = jnp.cos(ang)[None, :, None, :]
    sin = jnp.sin(ang)[None, :, None, :]
    x1 = x[..., :half].astype(F32)
    x2 = x[..., half:].astype(F32)
    return jnp.concatenate([x1 * cos - x2 * sin, x1 * sin + x2 * cos], axis=-1)

def project(h, w_in, b_f, fox_qn_g, fox_kn_g, pos):
    b, t, _ = h.shape
    z = jnp.einsum('btd,dc->btc', h, w_in)
    rq, rk, rv, rg, fq, fk, fv, ff = jnp.split(z, SPLITS, axis=-1)
    rq = rotary(rq.reshape(b, t, RET_HEADS, RET_HD), pos)
    rk = rotary(rk.reshape(b, t, RET_HEADS, RET_HD), pos) * (RET_HD ** -0.5)
    rv = rv.reshape(b, t, RET_HEADS, RET_HD).astype(F32)
    fq = rms_norm(fq.reshape(b, t, FOX_HEADS, FOX_HD), fox_qn_g)
    fk = rms_norm(fk.reshape(b, t, FOX_HEADS, FOX_HD), fox_kn_g)
    fv = fv.reshape(b, t, FOX_HEADS, FOX_HD)
    logf = jax.nn.log_sigmoid(ff.astype(F32) + b_f.astype(F32))
    return rq, rk, rv, rg, fq, fk, fv, logf

def retention(q, k, v, s0):
    b, t, h, _ = q.shape
    blen = min(CHUNK, t)
    n = t // blen
    lg = jnp.log1p(-(2.0 ** (-5.0 - jnp.arange(h, dtype=F32))))
    idx = jnp.arange(blen, dtype=F32)
    dist = idx[:, None] - idx[None, :]
    intra = jnp.where(dist[None] >= 0, jnp.exp(lg[:, None, None] * jnp.maximum(dist, 0.0)[None]), 0.0)
    q_dec = jnp.exp(lg[None, :] * (idx[:, None] + 1.0))
    k_dec = jnp.exp(lg[None, :] * (blen - 1.0 - idx[:, None]))
    s_dec = jnp.exp(lg * blen)

    def to_chunks(a):
        return a.reshape(b, n, blen, h, a.shape[-1]).transpose(1, 0, 2, 3, 4)

    def step(s, inp):
        qc, kc, vc = inp
        sc = jnp.einsum('blhd,bmhd->bhlm', qc, kc) * intra[None]
        o = (jnp.einsum('bhlm,bmhe->blhe', sc, vc)
             + jnp.einsum('blhd,bhde->blhe', qc, s) * q_dec[None, :, :, None])
        s = s * s_dec[None, :, None, None] + jnp.einsum('blhd,blhe->bhde', kc * k_dec[None, :, :, None], vc)
        return s, o

    s, o = lax.scan(step, s0, (to_chunks(q), to_chunks(k), to_chunks(v)))
    o = o.transpose(1, 0, 2, 3, 4).reshape(b, t, h, -1)
    return o, s

def fox_block(q, k, v, cq, ck, qpos, kpos):
    logits = jnp.einsum('bqhd,bkhd->bhqk', q, k).astype(F32) * (FOX_HD ** -0.5)
    logits = logits + (cq.transpose(0, 2, 1)[..., :, None] - ck.transpose(0, 2, 1)[..., None, :])
    mask = kpos[None, :] <= qpos[:, None]
    logits = jnp.where(mask[None, None], logits, -jnp.inf)
    p = jax.nn.softmax(logits, axis=-1)
    return jnp.einsum('bhqk,bkhd->bqhd', p.astype(v.dtype), v)

def fox_prompt(q, k, v, logf):
    b, t, h, d = q.shape
    c = jnp.cumsum(logf, axis=1)
    pos = jnp.arange(t)
    nb = t // Q_BLOCK
    qb = q.reshape(b, nb, Q_BLOCK, h, d).transpose(1, 0, 2, 3, 4)
    cqb = c.reshape(b, nb, Q_BLOCK, h).transpose(1, 0, 2, 3)
    pb = pos.reshape(nb, Q_BLOCK)
    out = lax.map(lambda a: fox_block(a[0], k, v, a[1], c, a[2], pos), (qb, cqb, pb))
    return out.transpose(1, 0, 2, 3, 4).reshape(b, t, h, d)

def fox_sample(q, k, v, logf, ck, cv, clogf):
    p = ck.shape[1]
    t = q.shape[1]
    k_all = jnp.concatenate([ck.astype(k.dtype), k], axis=1)
    v_all = jnp.concatenate([cv.astype(v.dtype), v], axis=1)
    c = jnp.cumsum(jnp.concatenate([clogf.astype(F32), logf], axis=1), axis=1)
    kpos = jnp.arange(p + t)
    qpos = p + jnp.arange(t)
    return fox_block(q, k_all, v_all, c[:, p:], c, qpos, kpos)

def combine(ro, rg, fo, ret_out_g, fox_out_g, w_out, dtype):
    b, t = rg.shape[:2]
    r = rms_norm(ro, ret_out_g).reshape(b, t, D_RET) * jax.nn.silu(rg.astype(F32))
    f = rms_norm(fo, fox_out_g).reshape(b, t, D_FOX)
    m = jnp.concatenate([r.astype(dtype), f.astype(dtype)], axis=-1)
    return jnp.einsum('btc,cd->btd', m, w_out)

def peer_tokens(x, wq, keys, u, v):
    n = x.shape[0]
    q = jnp.einsum('nd,dc->nc', x, wq).reshape(n, PEER_HEADS, 2, PEER_HALF)
    s1 = jnp.einsum('nhd,hkd->nhk', q[:, :, 0], keys[0]).astype(F32)
    s2 = jnp.einsum('nhd,hkd->nhk', q[:, :, 1], keys[1]).astype(F32)
    v1, i1 = lax.top_k(s1, PEER_TOPK)
    v2, i2 = lax.top_k(s2, PEER_TOPK)
    cand = (v1[..., :, None] + v2[..., None, :]).reshape(n, PEER_HEADS, PEER_TOPK * PEER_TOPK)
    cv, ci = lax.top_k(cand, PEER_TOPK)
    e = (jnp.take_along_axis(i1, ci // PEER_TOPK, axis=-1) * N_KEYS
         + jnp.take_along_axis(i2, ci % PEER_TOPK, axis=-1))
    g = jax.nn.softmax(cv, axis=-1)
    ue = u[e]
    ve = v[e]
    act = jax.nn.gelu(jnp.einsum('nd,nhkd->nhk', x, ue).astype(F32))
    w = (g * act).astype(x.dtype)
    return jnp.einsum('nhk,nhkd->nd', w, ve)

def peer(x, wq, keys, u, v):
    b, t, d = x.shape
    flat = x.reshape(-1, d)
    n = flat.shape[0]
    if n % PEER_BLOCK == 0 and n > PEER_BLOCK:
        blocks = flat.reshape(n // PEER_BLOCK, PEER_BLOCK, d)
        out = lax.map(lambda xb: peer_tokens(xb, wq, keys, u, v), blocks)
    else:
        out = peer_tokens(flat, wq, keys, u, v)
    return out.reshape(b, t, d)

def layer(x, pos, s0, past, norm1_g, w_in, b_f, fox_qn_g, fox_kn_g, ret_out_g, fox_out_g,
          w_out, norm2_g, peer_wq, peer_keys, peer_u, peer_v):
    h = rms_norm(x, norm1_g)
    rq, rk, rv, rg, fq, fk, fv, logf = project(h, w_in, b_f, fox_qn_g, fox_kn_g, pos)
    ro, s_new = retention(rq, rk, rv, s0)
    if past is None:
        fo = fox_prompt(fq, fk, fv, logf)
    else:
        fo = fox_sample(fq, fk, fv, logf, past[0], past[1], past[2])
    x = x + combine(ro, rg, fo, ret_out_g, fox_out_g, w_out, x.dtype)
    x = x + peer(rms_norm(x, norm2_g), peer_wq, peer_keys, peer_u, peer_v)
    return x, fk, fv, logf, s_new.astype(x.dtype)

def setup_inputs(seed: int = 0) -> dict:
    key = jax.random.key(seed)
    ks = jax.random.split(key, 20)
    nrm = jax.random.normal
    return {
        'x_prompt': nrm(ks[0], (BATCH, SEQ, D_MODEL), F32),
        'x_sample': nrm(ks[1], (DEC_BATCH, DEC_SEQ, D_MODEL), F32),
        'cache_fox_k': nrm(ks[2], (DEPTH, DEC_BATCH, PAST_LEN, FOX_HEADS, FOX_HD), F32),
        'cache_fox_v': nrm(ks[3], (DEPTH, DEC_BATCH, PAST_LEN, FOX_HEADS, FOX_HD), F32),
        'cache_fox_logf': jax.nn.log_sigmoid(2.0 + nrm(ks[4], (DEPTH, DEC_BATCH, PAST_LEN, FOX_HEADS), F32)),
        'state_ret': 0.5 * nrm(ks[5], (DEPTH, DEC_BATCH, RET_HEADS, RET_HD, RET_HD), F32),
        'norm1_g': 1.0 + 0.02 * nrm(ks[6], (DEPTH, D_MODEL), F32),
        'w_in': nrm(ks[7], (DEPTH, D_MODEL, IN_COLS), F32) * (D_MODEL ** -0.5),
        'b_f': 2.0 + 0.5 * nrm(ks[8], (DEPTH, FOX_HEADS), F32),
        'fox_qn_g': 1.0 + 0.02 * nrm(ks[9], (DEPTH, FOX_HEADS, FOX_HD), F32),
        'fox_kn_g': 1.0 + 0.02 * nrm(ks[10], (DEPTH, FOX_HEADS, FOX_HD), F32),
        'ret_out_g': 1.0 + 0.02 * nrm(ks[11], (DEPTH, RET_HEADS, RET_HD), F32),
        'fox_out_g': 1.0 + 0.02 * nrm(ks[12], (DEPTH, FOX_HEADS, FOX_HD), F32),
        'w_out': nrm(ks[13], (DEPTH, D_MIX, D_MODEL), F32) * (D_MIX ** -0.5),
        'norm2_g': 1.0 + 0.02 * nrm(ks[14], (DEPTH, D_MODEL), F32),
        'peer_wq': nrm(ks[15], (DEPTH, D_MODEL, PEER_HEADS * PEER_DKEY), F32) * (D_MODEL ** -0.5),
        'peer_keys': nrm(ks[16], (DEPTH, 2, PEER_HEADS, N_KEYS, PEER_HALF), F32) * (PEER_HALF ** -0.5),
        'peer_u': nrm(ks[17], (DEPTH, N_EXPERTS, D_MODEL), F32) * (D_MODEL ** -0.5),
        'peer_v': nrm(ks[18], (DEPTH, N_EXPERTS, D_MODEL), F32) * (PEER_HEADS ** -0.5),
    }

def reference(x_prompt, x_sample, cache_fox_k, cache_fox_v, cache_fox_logf, state_ret,
              norm1_g, w_in, b_f, fox_qn_g, fox_kn_g, ret_out_g, fox_out_g, w_out, norm2_g,
              peer_wq, peer_keys, peer_u, peer_v):
    y_p = x_prompt
    y_s = x_sample
    pos_p = jnp.arange(x_prompt.shape[1])
    pos_s = PAST_LEN + jnp.arange(x_sample.shape[1])
    kp_l, vp_l, lp_l, sp_l = [], [], [], []
    ks_l, vs_l, ls_l, ss_l = [], [], [], []
    for l in range(DEPTH):
        w = (norm1_g[l], w_in[l], b_f[l], fox_qn_g[l], fox_kn_g[l], ret_out_g[l], fox_out_g[l],
             w_out[l], norm2_g[l], peer_wq[l], peer_keys[l], peer_u[l], peer_v[l])
        s0_p = jnp.zeros((x_prompt.shape[0], RET_HEADS, RET_HD, RET_HD), F32)
        y_p, kp, vp, lp, sp = layer(y_p, pos_p, s0_p, None, *w)
        past = (cache_fox_k[l], cache_fox_v[l], cache_fox_logf[l])
        y_s, kk, vv, ll, ss = layer(y_s, pos_s, state_ret[l].astype(F32), past, *w)
        kp_l.append(kp); vp_l.append(vp); lp_l.append(lp); sp_l.append(sp)
        ks_l.append(kk); vs_l.append(vv); ls_l.append(ll); ss_l.append(ss)
    new_fox_k_p = jnp.stack(kp_l)
    new_fox_v_p = jnp.stack(vp_l)
    new_fox_logf_p = jnp.stack(lp_l)
    new_state_ret_p = jnp.stack(sp_l)
    new_fox_k_s = jnp.stack(ks_l)
    new_fox_v_s = jnp.stack(vs_l)
    new_fox_logf_s = jnp.stack(ls_l)
    new_state_ret_s = jnp.stack(ss_l)
    return (y_p, y_s, new_fox_k_p, new_fox_v_p, new_fox_logf_p, new_state_ret_p,
            new_fox_k_s, new_fox_v_s, new_fox_logf_s, new_state_ret_s)


_drawn_inputs = setup_inputs


def setup_inputs(seed=0):
    import zlib

    import numpy as np

    out = dict(_drawn_inputs(seed))
    spreads = {}
    factors = {'fox_qn_g': 3.387,
     'fox_kn_g': 2.723,
     'ret_out_g': 12.222,
     'fox_out_g': 7.645,
     'norm2_g': 7.889}
    for name, (base, spread) in spreads.items():
        noise = np.random.default_rng([zlib.crc32(name.encode()), seed]).standard_normal(out[name].shape)
        drawn = base * np.exp(spread * noise) if base else spread * noise
        out[name] = __import__('jax').numpy.asarray(drawn.astype(out[name].dtype))
    for name, factor in factors.items():
        out[name] = (out[name] * factor).astype(out[name].dtype)
    return out
```

```python
import math

import numpy as np

import concourse.bass as bass
from concourse import mybir
from contextlib import ExitStack

F32 = mybir.dt.float32
BF16 = mybir.dt.bfloat16
U32 = mybir.dt.uint32
I32 = mybir.dt.int32
ALU = mybir.AluOpType
ACT = mybir.ActivationFunctionType
AX = mybir.AxisListType

P = 128
D = 1024
KC = D // P
NP_TOK, NB, NS, PAST = 1024, 8, 16, 256
TILES = (NP_TOK + NB * NS) // P
PT = NP_TOK // P
ST = PT
NH, HD = 8, 64
GW = NH * HD
PAIRS = NH // 2
EPS = 1e-6
BIG = 1e30
TOPK, NKEY, PH = 16, 128, 8
GROUPS = TILES * PH
GELU_C = 2.0 * math.sqrt(2.0 / math.pi)


def emit(nc, a):
    ctx = ExitStack()
    with ctx:
        def sb(name, shape, dt=F32):
            return ctx.enter_context(nc.sbuf_tensor(name, shape, dt))

        def flat(name, n):
            return sb(name, [P, n])

        Hreg = flat("Hreg", KC * P * TILES)
        Wreg = flat("Wreg", 2 * KC * GW)
        Rreg = flat("Rreg", 4 * TILES * GW)
        mixo = sb("mixo", [P, TILES, 2 * GW])
        Xreg = flat("Xreg", 4384)
        hT = Hreg[:, :].rearrange("p (k n) -> p k n", k=KC)
        wbuf = Wreg[:, :].rearrange("p (s k c) -> p s k c", s=2, k=KC)
        quarter = TILES * GW
        qT = Rreg[:, 0:quarter].rearrange("p (r n) -> p r n", r=PAIRS)
        kT = Rreg[:, quarter:2 * quarter].rearrange("p (r n) -> p r n", r=PAIRS)
        vn = Rreg[:, 2 * quarter:3 * quarter].rearrange("p (t c) -> p t c", t=TILES)
        kn = Rreg[:, 3 * quarter:4 * quarter].rearrange("p (t c) -> p t c", t=TILES)

        ident = sb("ident", [P, P])
        identb = sb("identb", [P, P], BF16)
        causal = sb("causal", [P, 2, P])
        maskq = sb("maskq", [P, P], BF16)
        maskn = sb("maskn", [P, NS], BF16)
        cosn = mixo[:, 0, GW:GW + 32 * TILES].rearrange("p (t d) -> p t d", t=TILES)
        nsin = mixo[:, 1, GW:GW + 32 * TILES].rearrange("p (t d) -> p t d", t=TILES)
        psin = mixo[:, 2, GW:GW + 32 * TILES].rearrange("p (t d) -> p t d", t=TILES)
        gain_fq, gain_fk, gain_ret = (mixo[:, 3 + i, GW:] for i in range(3))
        grow1 = mixo[:, 7, :]
        dec = sb("dec", [P, 2, 2, NH])
        sdec = sb("sdec", [P, 2, PAIRS])
        bind = sb("bind", [P, NB])
        iota = sb("iota", [P, TOPK])
        nhalf = sb("nhalf", [P, NH])
        gain_fox = sb("gain_fox", [P, GW])
        grow = sb("grow", [P, D])
        bfb = sb("bfb", [P, NH])
        ffw = sb("ffw", [P, KC, NH])
        lgf = sb("lgf", [P, TILES, NH])
        lgfT = Hreg[0:NH, 7040:7040 + TILES * P]
        small = sb("small", [P, 64])

        def bc(ap, shape):
            return ap.to_broadcast(shape)

        held = ctx.enter_context(nc.semaphore("held"))

        def after(engine, semaphore, value):
            engine.wait_ge(semaphore, value)
            engine.sem_inc(held, 1)

        phases = []

        def program(body):
            phases.append(body)
            with ExitStack() as ph:
                def sem(name):
                    return ctx.enter_context(nc.semaphore(f"{name}_{len(phases)}"))

                def ps(name, shape):
                    return ph.enter_context(nc.psum_tensor(f"{name}_{len(phases)}", shape, F32))

                block = ph.enter_context(nc.Block())
                body(block, sem, ps)

        def phase_norm(block, sem, ps):
            const_in = sem("const_in")
            x_in = [sem(f"x_in{i}") for i in range(2)]
            sq_done, rs_done, xs_done = sem("sq_done"), sem("rs_done"), sem("xs_done")
            tr_done, ev_done, ev2_done = sem("tr_done"), sem("ev_done"), sem("ev2_done")
            pool_step = sem("pool_step")
            xt = Xreg[:, 0:2 * D].rearrange("p (s d) -> p s d", s=2)
            xs = Xreg[:, 2 * D:4 * D].rearrange("p (s d) -> p s d", s=2)
            junk = Rreg[:, 0:D]
            tp = [ps(f"tp{i}", [P, 4, P]) for i in range(4)]
            masks = Xreg[:, 4 * D:4 * D + P + NS]
            loads = [(ident, a["c_ident"]), (causal, a["c_causal"]), (masks, a["c_masks"]), (cosn, a["c_cos"]), (nsin, a["c_nsin"]), (psin, a["c_psin"]),
                     (dec, a["c_dec"]), (sdec, a["c_sdec"]), (bind, a["c_bind"]), (iota, a["c_iota"])]
            grows = [(gain_fq, a["fox_qn_g"]), (gain_fk, a["fox_kn_g"]), (gain_ret, a["ret_out_g"]),
                     (gain_fox[:, :], a["fox_out_g"])]
            n_const = 16 * (len(loads) + len(grows) + 2)

            def x_rows(t):
                return a["x_prompt"][0, t * P:(t + 1) * P, :] if t < PT else \
                    a["x_sample"].rearrange("b t d -> (b t) d")

            @block.sync
            def _(sp):
                for t in range(TILES):
                    if t >= 2:
                        sp.wait_ge(xs_done, t - 1)
                    sp.dma_start(xt[:, t % 2, :], x_rows(t)).then_inc(x_in[t % 2], 16)

            @block.scalar
            def _(act):
                for dst, src in loads:
                    act.dma_start(dst[tuple(slice(None) for _ in dst.shape)], src).then_inc(const_in, 16)
                for dst, g in grows:
                    act.dma_start(dst, g.rearrange("a h d -> a (h d)").partition_broadcast(P)
                                  .rearrange("p a c -> p (a c)")).then_inc(const_in, 16)
                act.dma_start(grow1, a["norm1_g"].partition_broadcast(P)
                              .rearrange("p a c -> p (a c)")).then_inc(const_in, 16)
                act.dma_start(bfb[:, :], a["b_f"].partition_broadcast(P)
                              .rearrange("p a c -> p (a c)")).then_inc(const_in, 16)

                def evacuate(t):
                    act.wait_ge(tr_done, t + 1)
                    nc.scalar.copy(hT[:, 0:4, t * P:(t + 1) * P], tp[2 * (t % 2)][:, :, :]).then_inc(ev_done, 1)

                for t in range(TILES):
                    act.wait_ge(x_in[t % 2], 16 * (t // 2 + 1))
                    nc.scalar.activation(junk, xt[:, t % 2, :], ACT.Square,
                                         accum_out=small[:, t:t + 1]).then_inc(sq_done, 1)
                    act.wait_ge(sq_done, t + 1)
                    if t >= 1:
                        evacuate(t - 1)
                evacuate(TILES - 1)

            @block.gpsimd
            def _(pool):
                nc.gpsimd.memset(nhalf[:, :], -0.5).then_inc(pool_step, 1)
                pool.wait_ge(pool_step, 1)
                for t in range(TILES):
                    pool.wait_ge(sq_done, t + 1)
                    nc.gpsimd.tensor_scalar(small[:, 16 + t:17 + t], small[:, t:t + 1], 1.0 / D, EPS,
                                            ALU.mult, ALU.add).then_inc(pool_step, 1)
                    pool.wait_ge(pool_step, t + 2)
                    nc.gpsimd.tensor_tensor(small[:, 32 + t:33 + t], small[:, 16 + t:17 + t], nhalf[:, 0:1],
                                            ALU.pow).then_inc(rs_done, 1)

            @block.vector
            def _(dve):
                dve.wait_ge(const_in, n_const)
                nc.vector.tensor_copy(identb[:, :], ident[:, :])
                nc.vector.tensor_copy(maskq[:, :], masks[:, 0:P])
                nc.vector.tensor_copy(maskn[:, :], masks[:, P:])
                for t in range(TILES + 1):
                    if t < TILES:
                        dve.wait_ge(rs_done, t + 1)
                        if t >= 2:
                            dve.wait_ge(tr_done, t - 1)
                        nc.vector.scalar_tensor_tensor(out=xs[:, t % 2, :], in0=xt[:, t % 2, :],
                                                       scalar=small[:, 32 + t:33 + t], in1=grow1,
                                                       op0=ALU.mult, op1=ALU.mult).then_inc(xs_done, 1)
                    if t >= 1:
                        dve.wait_ge(tr_done, t)
                        nc.vector.tensor_copy(hT[:, 4:8, (t - 1) * P:t * P],
                                              tp[2 * ((t - 1) % 2) + 1][:, :, :]).then_inc(ev2_done, 1)

            @block.tensor
            def _(pe):
                pe.wait_ge(const_in, n_const)
                for t in range(TILES):
                    pe.wait_ge(xs_done, t + 1)
                    if t >= 2:
                        pe.wait_ge(ev_done, t - 1)
                        pe.wait_ge(ev2_done, t - 1)
                    for k in range(KC):
                        last = nc.tensor.transpose(tp[2 * (t % 2) + k // 4][:, k % 4, :],
                                                   xs[:, t % 2, k * P:(k + 1) * P], ident[:, :])
                    last.then_inc(tr_done, 1)

        RQ, RK, RV, RG, FQ, FK, FV = range(7)

        def projection(groups):
            def body(block, sem, ps):
                steps = [(g, t) for g in groups for t in range(TILES)]
                turned = [n for n, (g, _) in enumerate(steps) if g in (RQ, RK, FQ, FK)]
                order = {n: m for m, n in enumerate(turned)}
                normed = [n for n, (g, _) in enumerate(steps) if g in (RG, FQ, FK)]
                norder = {n: m for m, n in enumerate(normed)}
                w_in = [sem(f"w_in{i}") for i in range(2)]
                w_used, z_done = sem("w_used"), sem("z_done")
                z_free = [sem(f"z_free{i}") for i in range(3)]
                rot_done, tr_done, ev_done = sem("rot_done"), sem("tr_done"), sem("ev_done")
                link_sem, v_done = sem("link_sem"), sem("v_done")
                with_ff = FV in groups
                if with_ff:
                    sq_done, ss_done, rs_done = sem("sq_done"), sem("ss_done"), sem("rs_done")
                    pool_step, gate_exp, out_done = sem("pool_step"), sem("gate_exp"), sem("out_done")
                    ff_in, ff_done, ff_z, ff_abs = sem("ff_in"), sem("ff_done"), sem("ff_z"), sem("ff_abs")
                    ff_exp, ff_e1, ff_ln, ff_log = sem("ff_exp"), sem("ff_e1"), sem("ff_ln"), sem("ff_log")
                    ffT = sem("ffT")
                z = [ps(f"z{i}", [P, GW]) for i in range(3)]
                tp = [ps(f"ztp{i}", [P, 4, P]) for i in range(2)]
                ffp = ps("ffp", [P, TILES, NH])
                ffpt = ps("ffpt", [NH, 2, 512])
                tmp = Xreg[:, 0:8 * GW].rearrange("p (s c) -> p s c", s=8)
                ffx = Xreg[:, 8 * GW:8 * GW + 4 * TILES * NH].rearrange("p (s t h) -> p s t h", s=4, t=TILES)

                def heads(ap):
                    return ap.rearrange("p (h d) -> p h d", h=NH)

                @block.sync
                def _(sp):
                    for gi, g in enumerate(groups):
                        if gi >= 2:
                            sp.wait_ge(w_used, gi - 1)
                        sp.dma_start(wbuf[:, gi % 2], a["w_in"][0, :, g * GW:(g + 1) * GW]
                                     .rearrange("(k p) c -> p k c", p=P)).then_inc(w_in[gi % 2], 16)
                    outs = 0
                    if with_ff:
                        sp.dma_start(ffw[:, :, :], a["c_wff"]).then_inc(ff_in, 16)
                    for n, (g, t) in enumerate(steps):
                        if g == FK:
                            sp.wait_ge(rot_done, order[n] + 1)
                            src, dk = kn[:, t, :], "new_fox_k"
                        elif g == FV:
                            sp.wait_ge(v_done, t + 1)
                            src, dk = vn[:, t, :], "new_fox_v"
                        else:
                            continue
                        dst = a[dk + "_p"][0, 0, t * P:(t + 1) * P].rearrange("n h d -> n (h d)") if t < PT else \
                            a[dk + "_s"][0].rearrange("b n h d -> (b n) (h d)")
                        sp.dma_start(dst, src).then_inc(out_done, 16)
                        outs += 1
                    if with_ff:
                        sp.wait_ge(ff_log, 1)
                        sp.dma_start(a["new_fox_logf_p"][0, 0].rearrange("(t p) h -> p t h", p=P),
                                     lgf[:, 0:PT, :]).then_inc(out_done, 16)
                        sp.dma_start(a["new_fox_logf_s"][0].rearrange("b n h -> (b n) h"),
                                     lgf[:, ST, :]).then_inc(out_done, 16)
                        outs += 2
                    if outs:
                        sp.wait_ge(out_done, 16 * outs)

                @block.tensor
                def _(pe):
                    def turn(n):
                        m = order[n]
                        g, t = steps[n]
                        pe.wait_ge(rot_done, m + 1)
                        if m >= 2:
                            pe.wait_ge(ev_done, m - 1)
                        src = tmp[:, 6 + m % 2, :] if g in (RQ, FQ) else kn[:, t, :]
                        for r in range(PAIRS):
                            last = nc.tensor.transpose(tp[m % 2][:, r, :], src[:, r * P:(r + 1) * P], ident[:, :])
                        last.then_inc(tr_done, 1)

                    for n, (g, t) in enumerate(steps):
                        gi = n // TILES
                        if t == 0:
                            pe.wait_ge(w_in[gi % 2], 16 * (gi // 2 + 1))
                        if n >= 3:
                            pe.wait_ge(z_free[n % 3], n // 3)
                        for k in range(KC):
                            last = nc.tensor.matmul(z[n % 3][:, :], hT[:, k, t * P:(t + 1) * P],
                                                    wbuf[:, gi % 2, k, :], start=(k == 0), stop=(k == KC - 1))
                        last.then_inc(z_done, 1)
                        if t == TILES - 1:
                            pe.wait_ge(z_done, n + 1)
                            pe.sem_inc(w_used, 1)
                        if n - 1 in order:
                            turn(n - 1)
                    if len(steps) - 1 in order:
                        turn(len(steps) - 1)
                    if with_ff:
                        pe.wait_ge(ff_in, 16)
                        for t in range(TILES):
                            for k in range(KC):
                                last = nc.tensor.matmul(ffp[:, t, :], hT[:, k, t * P:(t + 1) * P], ffw[:, k, :],
                                                        start=(k == 0), stop=(k == KC - 1))
                        last.then_inc(ff_done, 1)
                        pe.wait_ge(ff_log, 1)
                        for t in range(TILES):
                            if t == PT:
                                pe.wait_ge(ffT, 1)
                            last = nc.tensor.transpose(ffpt[:, (t // 4) % 2, (t % 4) * P:(t % 4 + 1) * P],
                                                       lgf[:, t, :], ident[:, :])
                            if t == PT - 1 or t == ST:
                                last.then_inc(tr_done, 1)

                @block.scalar
                def _(act):
                    def evacuate(n):
                        m = order[n]
                        g, t = steps[n]
                        act.wait_ge(tr_done, m + 1)
                        dst = qT if g in (RQ, FQ) else kT
                        nc.scalar.copy(dst[:, :, t * P:(t + 1) * P], tp[m % 2][:, :, :]).then_inc(ev_done, 1)

                    for n, (g, t) in enumerate(steps):
                        if g in (RV, FV):
                            act.wait_ge(z_done, n + 1)
                            nc.scalar.copy(vn[:, t, :], z[n % 3][:, :]).then_inc(z_free[n % 3], 1)
                            act.wait_ge(z_free[n % 3], n // 3 + 1)
                            act.sem_inc(v_done, 1)
                        if g in (FQ, FK):
                            m = norder[n]
                            act.wait_ge(z_done, n + 1)
                            if m >= 2:
                                act.wait_ge(ss_done, m - 1)
                            nc.scalar.activation(tmp[:, m % 2, :], z[n % 3][:, :], ACT.Square).then_inc(sq_done, 1)
                        if g == RG:
                            m = norder[n]
                            if m >= 2:
                                act.wait_ge(ss_done, m - 1)
                            nc.scalar.activation(tmp[:, m % 2, :], mixo[:, t, 0:GW], ACT.Square).then_inc(sq_done, 1)
                            act.wait_ge(z_done, n + 1)
                            if n >= 2:
                                act.wait_ge(z_free[(n - 2) % 3], (n - 2) // 3 + 1)
                            nc.scalar.activation(tmp[:, 2 + m % 2, :], z[n % 3][:, :], ACT.Exp,
                                                 scale=-1.0).then_inc(gate_exp, 1)
                        if n - 1 in order:
                            evacuate(n - 1)
                    if len(steps) - 1 in order:
                        evacuate(len(steps) - 1)
                    if with_ff:
                        act.wait_ge(ff_z, 1)
                        nc.scalar.activation(ffx[:, 1], ffx[:, 0], ACT.Abs).then_inc(ff_abs, 1)
                        act.wait_ge(ff_abs, 1)
                        nc.scalar.activation(ffx[:, 2], ffx[:, 1], ACT.Exp, scale=-1.0).then_inc(ff_exp, 1)
                        act.wait_ge(ff_e1, 1)
                        nc.scalar.activation(ffx[:, 1], ffx[:, 3], ACT.Ln).then_inc(ff_ln, 1)
                        act.wait_ge(tr_done, len(order) + 1)
                        nc.scalar.copy(lgfT[:, 0:NP_TOK], ffpt[:, :, :].rearrange("h a n -> h (a n)")).then_inc(ffT, 1)
                        act.wait_ge(tr_done, len(order) + 2)
                        nc.scalar.copy(lgfT[:, NP_TOK:], ffpt[:, 0, 0:P])

                @block.gpsimd
                def _(pool):
                    steps_done = 0
                    for m, n in enumerate(normed):
                        g, t = steps[n]
                        o = 8 * (m % 2)
                        pool.wait_ge(ss_done, m + 1)
                        nc.gpsimd.tensor_scalar(small[:, 16 + o:24 + o], small[:, o:o + 8], 1.0 / HD, EPS,
                                                ALU.mult, ALU.add).then_inc(pool_step, 1)
                        steps_done += 1
                        pool.wait_ge(pool_step, steps_done)
                        ins = nc.gpsimd.tensor_tensor(small[:, 32 + o:40 + o], small[:, 16 + o:24 + o],
                                                      nhalf[:, :], ALU.pow)
                        if g == FQ:
                            ins.then_inc(pool_step, 1)
                            steps_done += 1
                            pool.wait_ge(pool_step, steps_done)
                            ins = nc.gpsimd.tensor_scalar(small[:, 32 + o:40 + o], small[:, 32 + o:40 + o],
                                                          -(HD ** -0.5), None, ALU.mult)
                        ins.then_inc(rs_done, 1)

                @block.vector
                def _(dve):
                    count = [0]

                    def link(ins):
                        count[0] += 1
                        ins.then_inc(link_sem, 1)
                        dve.wait_ge(link_sem, count[0])

                    for n, (g, t) in enumerate(steps):
                        zn = z[n % 3][:, :]
                        kind = 0 if t < PT else 1
                        if g in (RQ, RK):
                            m = order[n]
                            dve.wait_ge(z_done, n + 1)
                            z4 = zn.rearrange("p (h a d) -> p h a d", h=NH, a=2)
                            A = tmp[:, 2, :].rearrange("p (h a d) -> p h a d", h=NH, a=2)
                            B = tmp[:, 3, :].rearrange("p (h a d) -> p h a d", h=NH, a=2)
                            cs = bc(cosn[:, t, :].unsqueeze(1).unsqueeze(1), [P, NH, 2, 32])
                            nc.vector.tensor_tensor(A, z4, cs, ALU.mult)
                            nc.vector.tensor_tensor(B[:, :, 0, :], z4[:, :, 1, :],
                                                    bc(nsin[:, t, :].unsqueeze(1), [P, NH, 32]), ALU.mult)
                            count[0] += 1
                            nc.vector.tensor_tensor(B[:, :, 1, :], z4[:, :, 0, :],
                                                    bc(psin[:, t, :].unsqueeze(1), [P, NH, 32]),
                                                    ALU.mult).then_inc(link_sem, 1)
                            dve.wait_ge(link_sem, count[0])
                            dve.sem_inc(z_free[n % 3], 1)
                            link(nc.vector.tensor_tensor(tmp[:, 4, :], tmp[:, 2, :], tmp[:, 3, :], ALU.add))
                            if g == RQ:
                                if m >= 2:
                                    dve.wait_ge(tr_done, m - 1)
                                dst = tmp[:, 6 + m % 2, :]
                            else:
                                dst = kn[:, t, :]
                            nc.vector.tensor_tensor(
                                heads(dst), heads(tmp[:, 4, :]),
                                bc(dec[:, 0 if g == RQ else 1, kind, :].unsqueeze(2), [P, NH, HD]),
                                ALU.mult).then_inc(rot_done, 1)
                        if g in (RG, FQ, FK):
                            m = norder[n]
                            o = 8 * (m % 2)
                            dve.wait_ge(sq_done, m + 1)
                            nc.vector.tensor_reduce(small[:, o:o + 8], heads(tmp[:, m % 2, :]), AX.X,
                                                    ALU.add).then_inc(ss_done, 1)
                            if g == RG:
                                dve.wait_ge(gate_exp, m + 1)
                                link(nc.vector.tensor_scalar_add(tmp[:, 4, :], tmp[:, 2 + m % 2, :], 1.0))
                                link(nc.vector.reciprocal(tmp[:, 5, :], tmp[:, 4, :]))
                                link(nc.vector.tensor_tensor(tmp[:, 4, :], zn, tmp[:, 5, :], ALU.mult))
                                dve.sem_inc(z_free[n % 3], 1)
                                link(nc.vector.tensor_tensor(tmp[:, 5, :], tmp[:, 4, :], gain_ret, ALU.mult))
                                link(nc.vector.tensor_tensor(tmp[:, 4, :], tmp[:, 5, :], mixo[:, t, 0:GW], ALU.mult))
                                dve.wait_ge(rs_done, m + 1)
                                link(nc.vector.tensor_tensor(heads(mixo[:, t, 0:GW]), heads(tmp[:, 4, :]),
                                                             bc(small[:, 32 + o:40 + o].unsqueeze(2), [P, NH, HD]),
                                                             ALU.mult))
                            else:
                                mt = order[n]
                                dve.wait_ge(rs_done, m + 1)
                                link(nc.vector.tensor_tensor(heads(tmp[:, 4, :]), heads(zn),
                                                             bc(small[:, 32 + o:40 + o].unsqueeze(2), [P, NH, HD]),
                                                             ALU.mult))
                                dve.sem_inc(z_free[n % 3], 1)
                                if g == FQ:
                                    if mt >= 2:
                                        dve.wait_ge(tr_done, mt - 1)
                                    dst = tmp[:, 6 + mt % 2, :]
                                else:
                                    dst = kn[:, t, :]
                                nc.vector.tensor_tensor(dst, tmp[:, 4, :], gain_fq if g == FQ else gain_fk,
                                                        ALU.mult).then_inc(rot_done, 1)
                    if with_ff:
                        dve.wait_ge(ff_done, 1)
                        nc.vector.tensor_tensor(ffx[:, 0], ffp[:, :, :], bc(bfb[:, :].unsqueeze(1), [P, TILES, NH]),
                                                ALU.add).then_inc(ff_z, 1)
                        dve.wait_ge(ff_exp, 1)
                        nc.vector.tensor_scalar_add(ffx[:, 3], ffx[:, 2], 1.0).then_inc(ff_e1, 1)
                        dve.wait_ge(ff_ln, 1)
                        nc.vector.scalar_tensor_tensor(out=lgf[:, :, :], in0=ffx[:, 0], scalar=0.0, in1=ffx[:, 1],
                                                       op0=ALU.min, op1=ALU.subtract).then_inc(ff_log, 1)
            return body

        def phase_retention(block, sem, ps):
            st = Wreg[:, 0:PAIRS * HD].rearrange("p (r e) -> p r e", r=PAIRS)
            stt = Wreg[:, 256:512].rearrange("p (r e) -> p r e", r=PAIRS)
            sT = Wreg[:, 512:512 + 2 * NH * P].rearrange("p (s q r l) -> p s q r l", s=2, q=2, r=PAIRS)
            s0 = Wreg[:, 2560:2560 + 2048].rearrange("p (r b e) -> p r b e", r=PAIRS, b=NB)
            vbd = Wreg[:, 4608:4608 + 2 * GW].rearrange("p (s b e) -> p s b e", s=2, b=NB)
            sadd = Wreg[:, 5632:5632 + 2048].rearrange("p (r b e) -> p r b e", r=PAIRS, b=NB)
            oT = Wreg[:, 7680:7680 + GW].rearrange("p (r l) -> p r l", r=PAIRS)
            sc = [ps(f"sc{i}", [P, 4, P]) for i in range(2)]
            op_all = [[ps(f"op{i}{j}", [P, GW]) for j in range(2)] for i in range(2)]
            op = [[b[:, 0:PAIRS * HD].rearrange("p (r e) -> p r e", r=PAIRS) for b in row] for row in op_all]
            up_all = ps("up", [P, GW])
            up = up_all[:, 0:PAIRS * HD].rearrange("p (r e) -> p r e", r=PAIRS)
            opT = ps("opT", [P, PAIRS, P])
            snew = [op_all[i][0][:, :].rearrange("p (b e) -> p b e", b=NB) for i in range(2)]
            sc_done, mask_done, o_done, oev = sem("sc_done"), sem("mask_done"), sem("o_done"), sem("oev")
            up_done, st_done, link_sem = sem("up_done"), sem("st_done"), sem("link_sem")
            s0_in, oT_done, oTc, vb_done = sem("s0_in"), sem("oT_done"), sem("oTc"), sem("vb_done")
            sn_done, sn_out, out_done, oTt = sem("sn_done"), sem("sn_out"), sem("out_done"), sem("oTt")

            @block.sync
            def _(sp):
                for par in range(2):
                    for r in range(PAIRS):
                        sp.dma_start(s0[64 * par:64 * par + 64, r],
                                     a["state_ret"][0, :, 2 * r + par].rearrange("b d e -> d b e")).then_inc(s0_in, 16)
                sp.wait_ge(st_done, PT)
                for par in range(2):
                    sp.dma_start(a["new_state_ret_p"][0, 0].rearrange("(r q) d e -> q d r e", q=2)[par],
                                 st[64 * par:64 * par + 64]).then_inc(out_done, 16)
                for r in range(PAIRS):
                    sp.wait_ge(sn_out, r + 1)
                    for par in range(2):
                        sp.dma_start(a["new_state_ret_s"][0, :, 2 * r + par].rearrange("b d e -> d b e"),
                                     sadd[64 * par:64 * par + 64, r]).then_inc(out_done, 16)
                sp.wait_ge(out_done, 16 * (2 + 2 * PAIRS))

            @block.tensor
            def _(pe):
                def scores(t):
                    for half in range(2):
                        if t >= 1:
                            pe.wait_ge(mask_done, 2 * (t - 1) + half + 1)
                        for r in range(PAIRS):
                            b0 = 64 * half
                            last = nc.tensor.matmul(sc[half][:, r, :], kT[b0:b0 + 64, r, t * P:(t + 1) * P],
                                                    qT[b0:b0 + 64, r, t * P:(t + 1) * P], start=True, stop=True)
                        last.then_inc(sc_done, 1)

                def outputs(t):
                    if t >= 2:
                        pe.wait_ge(oev, t - 1)
                    if t >= 1:
                        pe.wait_ge(st_done, t)
                    for h in range(NH):
                        if h < 2:
                            pe.wait_ge(mask_done, 2 * t + h + 1)
                        b0, r = 64 * (h % 2), h // 2
                        o = op[h % 2][t % 2][:, r, :]
                        last = nc.tensor.matmul(o, sT[:, t % 2, h % 2, r, :], vn[:, t, h * HD:(h + 1) * HD],
                                                start=True, stop=(t == 0))
                        if t:
                            last = nc.tensor.matmul(o, qT[b0:b0 + 64, r, t * P:(t + 1) * P],
                                                    st[b0:b0 + 64, r, :], start=False, stop=True)
                    last.then_inc(o_done, 1)
                    for h in range(NH):
                        b0, r = 64 * (h % 2), h // 2
                        last = nc.tensor.matmul(up[b0:b0 + 64, r, :], kn[:, t, h * HD:(h + 1) * HD],
                                                vn[:, t, h * HD:(h + 1) * HD], start=True, stop=True)
                    last.then_inc(up_done, 1)

                scores(0)
                for t in range(PT):
                    scores(t + 1)
                    outputs(t)
                pe.wait_ge(s0_in, 16 * NH)
                pe.wait_ge(mask_done, 2 * TILES)
                for h in range(NH):
                    b0, r = 64 * (h % 2), h // 2
                    nc.tensor.matmul(opT[b0:b0 + 64, r, :], vn[:, ST, h * HD:(h + 1) * HD], sT[:, ST % 2, h % 2, r, :],
                                     start=True, stop=False)
                    for b in range(NB):
                        c = NP_TOK + b * NS
                        last = nc.tensor.matmul(opT[b0:b0 + 64, r, b * NS:(b + 1) * NS], s0[b0:b0 + 64, r, b, :],
                                                qT[b0:b0 + 64, r, c:c + NS], start=False, stop=(b == NB - 1))
                last.then_inc(oT_done, 1)
                pe.wait_ge(oev, PT)
                for h in range(NH):
                    b0, r = 64 * (h % 2), h // 2
                    pe.wait_ge(vb_done, h + 1)
                    if h % 2 == 0 and r >= 2:
                        pe.wait_ge(sn_out, r - 1)
                    last = nc.tensor.matmul(snew[r % 2][b0:b0 + 64].rearrange("p b e -> p (b e)"),
                                            kn[:, ST, h * HD:(h + 1) * HD],
                                            vbd[:, h % 2].rearrange("p b e -> p (b e)"), start=True, stop=True)
                    last.then_inc(sn_done, 1)
                pe.wait_ge(oTc, 1)
                pe.wait_ge(st_done, PT)
                for r in range(PAIRS):
                    last = nc.tensor.transpose(up_all[:, r * P:(r + 1) * P], oT[:, r, :], ident[:, :])
                last.then_inc(oTt, 1)

            @block.vector
            def _(dve):
                count = [0]

                def link(ins):
                    count[0] += 1
                    ins.then_inc(link_sem, 1)
                    dve.wait_ge(link_sem, count[0])

                def mask(t):
                    for half in range(2):
                        dve.wait_ge(sc_done, 2 * t + half + 1)
                        if t >= 2:
                            dve.wait_ge(o_done, t - 1)
                        nc.vector.tensor_tensor(sT[:, t % 2, half], sc[half][:, :, :],
                                                bc(causal[:, 0 if t < PT else 1, :].unsqueeze(1), [P, 4, P]),
                                                ALU.mult).then_inc(mask_done, 1)

                for t in range(PT):
                    mask(t)
                    dve.wait_ge(up_done, t + 1)
                    sd = bc(sdec[:, 0, :].unsqueeze(2), [P, PAIRS, HD])
                    if t == 0:
                        nc.vector.tensor_tensor(st, up, sd, ALU.mult).then_inc(st_done, 1)
                    else:
                        link(nc.vector.tensor_tensor(stt, up, st, ALU.add))
                        nc.vector.tensor_tensor(st, stt, sd, ALU.mult).then_inc(st_done, 1)
                    dve.wait_ge(st_done, t + 1)
                mask(ST)
                dve.wait_ge(s0_in, 16 * NH)

                def spread(h):
                    if h >= 2:
                        dve.wait_ge(sn_done, h - 1)
                    nc.vector.tensor_tensor(vbd[:, h % 2],
                                            bc(vn[:, ST, h * HD:(h + 1) * HD].unsqueeze(1), [P, NB, HD]),
                                            bc(bind[:, :].unsqueeze(2), [P, NB, HD]), ALU.mult).then_inc(vb_done, 1)

                for r in range(PAIRS):
                    spread(2 * r)
                    spread(2 * r + 1)
                    dve.wait_ge(sn_done, 2 * r + 2)
                    link(nc.vector.tensor_tensor(sadd[:, r], snew[r % 2], s0[:, r], ALU.add))
                    nc.vector.tensor_scalar(sadd[:, r], sadd[:, r], sdec[:, 1, r:r + 1], None,
                                            ALU.mult).then_inc(sn_out, 1)

            @block.scalar
            def _(act):
                for t in range(PT):
                    act.wait_ge(o_done, t + 1)
                    for par in range(2):
                        last = nc.scalar.copy(
                            mixo[:, t, 0:GW].rearrange("p (r q e) -> p q r e", q=2, e=HD)[:, par],
                            op[par][t % 2])
                    last.then_inc(oev, 1)
                act.wait_ge(oT_done, 1)
                nc.scalar.copy(oT, opT[:, :, :]).then_inc(oTc, 1)
                act.wait_ge(oTt, 1)
                nc.scalar.copy(mixo[:, ST, 0:GW], up_all[:, :])

        def phase_fox(block, sem, ps):
            cB = Hreg[:, 0:2 * NP_TOK].rearrange("p (s n) -> p s n", s=2)
            sN = Hreg[:, 2048:4096].rearrange("p (s n) -> p s n", s=2)
            pr = Hreg[:, 4096:6144].rearrange("p (s n) -> p s n", s=2)
            pT = Hreg[:, 6144:8192].rearrange("p (s j q) -> p s j q", s=2, j=8)
            ones = Hreg[:, 8192:9216]
            csum = Rreg[0:NH, 3 * quarter:3 * quarter + NP_TOK]
            e8 = Rreg[0:NH, 3 * quarter + 1024:3 * quarter + 2048].rearrange("p (h m) -> p h m", h=NH)
            e64 = Rreg[0:64, 3 * quarter + 2048:3 * quarter + 3072].rearrange("p (b m) -> p b m", b=NB)
            lfs = Rreg[0:64, 3 * quarter + 3072:3 * quarter + 3344]
            cs = Rreg[0:64, 3 * quarter + 3344:3 * quarter + 3616]
            mn = sb("mn", [P, 2, 3])
            ck = Wreg[:, 0:2048].rearrange("p (s j c) -> p s j c", s=2, j=2)
            cv = Wreg[:, 2048:4096].rearrange("p (s j c) -> p s j c", s=2, j=2)
            vnew = Wreg[0:NS, 4096:8192].rearrange("p (b c) -> p b c", b=NB)
            qbd = Xreg[:, 0:1024].rearrange("p (r b a q) -> p r b a q", r=PAIRS, b=NB, a=2)
            ckT = Xreg[:, 1024:3072].rearrange("p (s r n) -> p s r n", s=2, r=PAIRS) if False else \
                Xreg[:, 1024:2048].rearrange("p (r n) -> p r n", r=PAIRS)
            pn = Xreg[:, 2048:2048 + 272]
            pns = Xreg[:, 2320:2320 + 272]
            psT = Xreg[:, 2592:2592 + 384].rearrange("p (j m) -> p j m", j=3)
            foT = Xreg[:, 2976:2976 + 512].rearrange("p (r n) -> p r n", r=PAIRS)
            sp_ = [ps(f"s{i}", [P, NP_TOK]) for i in range(2)]
            tpp = ps("tpp", [P, 8, P])
            ov = ps("ov", [P, HD])
            cbp = ps("cbp", [P, 512])

            e_in, lf_in, vn_in = sem("e_in"), sem("lf_in"), sem("vn_in")
            ones_set, c_done, cs_done = sem("ones_set"), sem("c_done"), sem("cs_done")
            cb_mm, cb_ev = sem("cb_mm"), sem("cb_ev")
            s_done, ttr_done, exp_done, t_done = sem("s_done"), sem("ttr_done"), sem("exp_done"), sem("t_done")
            pta, ptb, pv_done, norm_done, rl_done = sem("pta"), sem("ptb"), sem("pv_done"), sem("norm_done"), sem("rl_done")
            kv_in = [sem(f"kv_in{i}") for i in range(2)]
            kv_used, qb_done, qz = sem("kv_used"), sem("qb_done"), sem("qz")
            kt_mm, kt_ev, ss_done, smin, sexp, spn = (sem(x) for x in ("kt_mm", "kt_ev", "ss_done", "smin", "sexp", "spn"))
            st_mm, st_ev, so_mm, so_ev, srl, fT_mm = (sem(x) for x in ("st_mm", "st_ev", "so_mm", "so_ev", "srl", "fT_mm"))
            NSTEP = NH * PT

            @block.sync
            def _(sp):
                sp.dma_start(e8, a["c_e8"]).then_inc(e_in, 16)
                sp.dma_start(e64, a["c_e64"]).then_inc(e_in, 16)
                sp.dma_start(lfs[:, 0:PAST], a["cache_lf_t"]).then_inc(lf_in, 16)
                for b in range(NB):
                    sp.dma_start(lfs[b * NH:(b + 1) * NH, PAST:PAST + NS],
                                 lgfT[:, NP_TOK + b * NS:NP_TOK + (b + 1) * NS]).then_inc(lf_in, 16)
                    sp.dma_start(vnew[:, b, :], vn[b * NS:(b + 1) * NS, ST, :]).then_inc(vn_in, 16)
                for b in range(NB):
                    if b >= 2:
                        sp.wait_ge(kv_used, b - 1)
                    sp.dma_start(ck[:, b % 2], a["cache_fox_k"][0, b].rearrange("(j p) h d -> p j (h d)", p=P)
                                 ).then_inc(kv_in[b % 2], 16)
                    sp.dma_start(cv[:, b % 2], a["cache_fox_v"][0, b].rearrange("(j p) h d -> p j (h d)", p=P)
                                 ).then_inc(kv_in[b % 2], 16)

            @block.tensor
            def _(pe):
                def decay_rows(h):
                    for half in range(2):
                        m = 2 * h + half
                        if m >= 1:
                            pe.wait_ge(cb_ev, m)
                        nc.tensor.matmul(cbp[:, :], e8[:, h, :], csum[:, 512 * half:512 * half + 512],
                                         start=True, stop=True).then_inc(cb_mm, 1)

                def scores(n):
                    h, i = n // PT, n % PT
                    b0, r = 64 * (h % 2), h // 2
                    if n >= 2:
                        pe.wait_ge(ttr_done, n - 1)
                    width = (i + 1) * P
                    for c in range(0, width, 512):
                        w = min(512, width - c)
                        final = c + w == width
                        nc.tensor.matmul(sp_[n % 2][:, c:c + w], qT[b0:b0 + 64, r, i * P:(i + 1) * P],
                                         kT[b0:b0 + 64, r, c:c + w], start=True, stop=not final)
                    nc.tensor.matmul(sp_[n % 2][:, i * P:width], identb[:, :], maskq[:, :],
                                     start=False, stop=True).then_inc(s_done, 1)

                def turn(n):
                    i = n % PT
                    pe.wait_ge(exp_done, n + 1)
                    for j in range(i + 1):
                        last = nc.tensor.transpose(tpp[:, j, :], pr[:, n % 2, j * P:(j + 1) * P], ident[:, :])
                    last.then_inc(t_done, 1)

                def values(n):
                    h, i = n // PT, n % PT
                    pe.wait_ge(pta, n + 1)
                    pe.wait_ge(ptb, 4 * h + max(0, i - 3))
                    if n >= 1:
                        pe.wait_ge(norm_done, n)
                    for j in range(i + 1):
                        last = nc.tensor.matmul(ov[:, :], pT[:, n % 2, j, :], vn[:, j, h * HD:(h + 1) * HD],
                                                start=(j == 0), stop=(j == i))
                    last.then_inc(pv_done, 1)

                pe.wait_ge(e_in, 32)
                pe.wait_ge(c_done, 1)
                decay_rows(0)
                for n in range(NSTEP + 2):
                    if n < NSTEP:
                        scores(n)
                        if n % PT == 4 and n // PT < NH - 1:
                            decay_rows(n // PT + 1)
                    if n >= 2:
                        values(n - 2)
                    if 1 <= n <= NSTEP:
                        turn(n - 1)
                pe.wait_ge(cs_done, 1)
                pe.wait_ge(qb_done, 2)
                pe.wait_ge(vn_in, 16 * NB)
                kTp = sp_[0][:, :].rearrange("p (r n) -> p r n", r=PAIRS)
                pe.wait_ge(ttr_done, NSTEP)
                for b in range(NB):
                    pe.wait_ge(kv_in[b % 2], 32 * (b // 2 + 1))
                    if b >= 1:
                        pe.wait_ge(kt_ev, b)
                    for r in range(PAIRS):
                        for j in range(2):
                            last = nc.tensor.transpose(kTp[:, r, j * P:(j + 1) * P], ck[:, b % 2, j, r * P:(r + 1) * P],
                                                       ident[:, :])
                    last.then_inc(kt_mm, 1)
                    S = sp_[1][:, 0:272]
                    if b >= 1:
                        pe.wait_ge(sexp, b)
                    nc.tensor.matmul(S, e64[:, b, :], cs, start=True, stop=False, skip_group_check=True)
                    nc.tensor.matmul(S[:, PAST:PAST + NS], identb[:, :], maskn[:, :], start=False, stop=False,
                                     skip_group_check=True)
                    pe.wait_ge(kt_ev, b + 1)
                    for r in range(PAIRS):
                        o = 32 * r
                        lhs = qbd[:, r, b].rearrange("p a q -> p (a q)")
                        nc.tensor.matmul(S[o:o + 32, 0:PAST], lhs, ckT[:, r, :], start=False, stop=False,
                                         skip_group_check=True)
                        last = nc.tensor.matmul(S[o:o + 32, PAST:PAST + NS], lhs,
                                                kT[:, r, NP_TOK + b * NS:NP_TOK + (b + 1) * NS],
                                                start=False, stop=True, skip_group_check=True)
                    last.then_inc(ss_done, 1)
                    pe.wait_ge(spn, b + 1)
                    if b >= 1:
                        pe.wait_ge(st_ev, 2 * b)
                    for j in range(2):
                        nc.tensor.transpose(tpp[:, j, :], pns[:, j * P:(j + 1) * P], ident[:, :])
                    nc.tensor.transpose(tpp[0:NS, 2, :], pns[:, PAST:PAST + NS], ident[:, :]).then_inc(st_mm, 1)
                    pe.wait_ge(st_ev, 2 * b + 2)
                    if b >= 1:
                        pe.wait_ge(so_ev, 2 * b)
                    for r in range(PAIRS):
                        o = cbp[:, 32 * r:32 * r + 32]
                        for j in range(2):
                            nc.tensor.matmul(o, cv[:, b % 2, j, r * P:(r + 1) * P], psT[:, j, 32 * r:32 * r + 32],
                                             start=(j == 0), stop=False)
                        last = nc.tensor.matmul(o, vnew[:, b, r * P:(r + 1) * P], psT[0:NS, 2, 32 * r:32 * r + 32],
                                                start=False, stop=True)
                    last.then_inc(so_mm, 1)
                    pe.wait_ge(so_mm, b + 1)
                    pe.sem_inc(kv_used, 1)
                pe.wait_ge(so_ev, 2 * NB)
                for r in range(PAIRS):
                    last = nc.tensor.transpose(tpp[:, r, :], foT[:, r, :], ident[:, :])
                last.then_inc(fT_mm, 1)

            @block.scalar
            def _(act):
                def rows(m):
                    act.wait_ge(cb_mm, m + 1)
                    h, half = m // 2, m % 2
                    if h >= 2:
                        act.wait_ge(ttr_done, PT * (h - 1))
                    nc.scalar.copy(cB[:, h % 2, 512 * half:512 * half + 512], cbp[:, :]).then_inc(cb_ev, 1)

                act.wait_ge(lf_in, 16 * (NB + 1))
                rows(0)
                rows(1)
                for n in range(NSTEP + 1):
                    if n < NSTEP:
                        w = (n % PT + 1) * P
                        act.wait_ge(ttr_done, n + 1)
                        if n >= 2:
                            act.wait_ge(t_done, n - 1)
                            act.wait_ge(rl_done, n - 1)
                        nc.scalar.activation(pr[:, n % 2, 0:w], sN[:, n % 2, 0:w], ACT.Exp, bias=mn[:, n % 2, 0:1],
                                             scale=-1.0, accum_out=mn[:, n % 2, 1:2]).then_inc(exp_done, 1)
                    if n < NSTEP and n % PT == 4 and n // PT < NH - 1:
                        rows(2 * (n // PT) + 2)
                        rows(2 * (n // PT) + 3)
                    if n >= 1:
                        act.wait_ge(t_done, n)
                        j = min(4, (n - 1) % PT + 1)
                        if n >= 3:
                            act.wait_ge(pv_done, n - 2)
                        nc.scalar.copy(pT[:, (n - 1) % 2, 0:j, :], tpp[:, 0:j, :]).then_inc(pta, 1)
                for b in range(NB):
                    act.wait_ge(kt_mm, b + 1)
                    if b >= 1:
                        act.wait_ge(ss_done, b)
                    nc.scalar.copy(ckT, sp_[0][:, :].rearrange("p (r n) -> p r n", r=PAIRS)).then_inc(kt_ev, 1)
                    act.wait_ge(smin, b + 1)
                    if b >= 1:
                        act.wait_ge(spn, b)
                    nc.scalar.activation(pn, sp_[1][:, 0:272], ACT.Exp, bias=mn[:, 0, 0:1], scale=-1.0,
                                         accum_out=mn[:, 0, 1:2]).then_inc(sexp, 1)
                    act.wait_ge(st_mm, b + 1)
                    if b >= 1:
                        act.wait_ge(so_mm, b)
                    nc.scalar.copy(psT[:, 0:2, :], tpp[:, 0:2, :]).then_inc(st_ev, 1)
                    nc.scalar.copy(psT[0:NS, 2, :], tpp[0:NS, 2, :]).then_inc(st_ev, 1)
                act.wait_ge(fT_mm, 1)
                nc.scalar.copy(mixo[:, ST, GW:], tpp[:, 0:4, :].rearrange("p r e -> p (r e)"))

            @block.gpsimd
            def _(pool):
                nc.gpsimd.memset(ones, 1.0).then_inc(ones_set, 1)
                nc.gpsimd.memset(Xreg[:, 0:1024], 0.0).then_inc(qz, 1)

            @block.vector
            def _(dve):
                dve.wait_ge(ones_set, 1)
                nc.vector.tensor_tensor_scan(out=csum, data0=ones[0:NH, :], data1=lgfT[:, 0:NP_TOK],
                                             initial=0.0, op0=ALU.mult, op1=ALU.add).then_inc(c_done, 1)
                dve.wait_ge(lf_in, 16 * (NB + 1))
                nc.vector.tensor_tensor_scan(out=cs, data0=ones[0:64, 0:272], data1=lfs,
                                             initial=0.0, op0=ALU.mult, op1=ALU.add).then_inc(cs_done, 1)
                dve.wait_ge(qz, 1)
                for par in range(2):
                    o = 64 * par
                    nc.vector.tensor_copy(qbd[o:o + 64, :, :, par, :].rearrange("p r b q -> p (r b) q"),
                                          qT[o:o + 64, :, NP_TOK:].rearrange("p r (b q) -> p r b q", q=NS)
                                          ).then_inc(qb_done, 1) if False else \
                        [nc.vector.tensor_copy(qbd[o:o + 64, r, :, par, :],
                                               qT[o:o + 64, r, NP_TOK:].rearrange("p (b q) -> p b q", q=NS))
                         for r in range(PAIRS)][-1].then_inc(qb_done, 1)

                for n in range(NSTEP + 2):
                    if n < NSTEP:
                        h, w = n // PT, (n % PT + 1) * P
                        if n % PT == 0:
                            dve.wait_ge(cb_ev, 2 * h + 2)
                        dve.wait_ge(s_done, n + 1)
                        if n >= 2:
                            dve.wait_ge(exp_done, n - 1)
                        nc.vector.tensor_tensor_reduce(out=sN[:, n % 2, 0:w], in0=sp_[n % 2][:, 0:w],
                                                       in1=cB[:, h % 2, 0:w], scale=1.0, scalar=3e38,
                                                       op0=ALU.add, op1=ALU.min,
                                                       accum_out=mn[:, n % 2, 0:1]).then_inc(ttr_done, 1)
                    if 1 <= n <= NSTEP:
                        m = n - 1
                        dve.wait_ge(exp_done, m + 1)
                        if m >= 2:
                            dve.wait_ge(norm_done, m - 1)
                        nc.vector.reciprocal(mn[:, m % 2, 2:3], mn[:, m % 2, 1:2]).then_inc(rl_done, 1)
                        if m % PT >= 4:
                            j = m % PT + 1
                            dve.wait_ge(t_done, m + 1)
                            if m >= 2:
                                dve.wait_ge(pv_done, m - 1)
                            nc.vector.tensor_copy(pT[:, m % 2, 4:j, :], tpp[:, 4:j, :]).then_inc(ptb, 1)
                    if n >= 2:
                        m = n - 2
                        h, i = m // PT, m % PT
                        dve.wait_ge(pv_done, m + 1)
                        dve.wait_ge(rl_done, m + 1)
                        nc.vector.tensor_scalar(mixo[:, i, GW + h * HD:GW + (h + 1) * HD], ov[:, :],
                                                mn[:, m % 2, 2:3], None, ALU.mult).then_inc(norm_done, 1)
                for b in range(NB):
                    dve.wait_ge(ss_done, b + 1)
                    nc.vector.tensor_reduce(mn[:, 0, 0:1], sp_[1][:, 0:272], AX.X, ALU.min).then_inc(smin, 1)
                    dve.wait_ge(sexp, b + 1)
                    nc.vector.reciprocal(mn[:, 0, 2:3], mn[:, 0, 1:2]).then_inc(srl, 1)
                    dve.wait_ge(srl, b + 1)
                    if b >= 1:
                        dve.wait_ge(st_mm, b)
                    nc.vector.tensor_scalar(pns, pn, mn[:, 0, 2:3], None, ALU.mult).then_inc(spn, 1)
                    dve.wait_ge(so_mm, b + 1)
                    for par in range(2):
                        o = 64 * par
                        nc.vector.tensor_copy(foT[o:o + 64, :, b * NS:(b + 1) * NS],
                                              cbp[o:o + 64, 0:P].rearrange("p (r a q) -> p r a q", r=PAIRS, a=2)
                                              [:, :, par, :]).then_inc(so_ev, 1)

        idx_all = Xreg[:, 0:GROUPS * TOPK].bitcast(I32)
        gate_all = Xreg[:, GROUPS * TOPK:2 * GROUPS * TOPK]
        wout = Wreg[:, :].rearrange("p (k c) -> p k c", k=KC)
        wq = Rreg[:, 0:KC * 2048].rearrange("p (k c) -> p k c", k=KC)

        def phase_route(block, sem, ps):
            NSEG = 2 * PH
            keysT = Rreg[:, 16384:18432].rearrange("p (s n) -> p s n", s=NSEG)
            mixs, xt, x1, xns = (Hreg[:, i * D:(i + 1) * D] for i in range(4))
            mT = Hreg[:, 4096:5120].rearrange("p (k n) -> p k n", k=KC)
            qTs = Hreg[:, 5120:7168].rearrange("p (s n) -> p s n", s=NSEG)
            sc = Hreg[:, 7168:9216].rearrange("p (s n) -> p s n", s=NSEG)
            sc2 = qTs
            cand = Hreg[:, 0:2048].rearrange("p (h n) -> p h n", h=PH)
            X0 = 2 * GROUPS * TOPK
            vals = Xreg[:, X0:X0 + 256].rearrange("p (s n) -> p s n", s=NSEG)
            idx = Xreg[:, X0 + 256:X0 + 512].bitcast(U32).rearrange("p (s n) -> p s n", s=NSEG)
            fidx = Xreg[:, X0 + 512:X0 + 768].rearrange("p (s n) -> p s n", s=NSEG)
            cval = Xreg[:, X0 + 768:X0 + 896].rearrange("p (h n) -> p h n", h=PH)
            ci = Xreg[:, X0 + 896:X0 + 1024].bitcast(U32).rearrange("p (h n) -> p h n", h=PH)
            cia = Xreg[:, X0 + 1024:X0 + 1152].bitcast(U32)
            cif = Xreg[:, X0 + 1152:X0 + 1408].rearrange("p (a n) -> p a n", a=2)
            sel = Xreg[:, X0 + 1408:X0 + 1664].rearrange("p (a n) -> p a n", a=2)
            ef = Xreg[:, X0 + 1664:X0 + 1792].rearrange("p (h n) -> p h n", h=PH)
            ssum = Xreg[:, X0 + 1792:X0 + 1808]
            sq = sc2.rearrange("p s n -> p (s n)")[:, 0:D]
            tp = ps("btp", [P, 8, P])
            yp = ps("yp", [P, D])
            qp = [ps(f"qp{i}", [P, 4, P]) for i in range(2)]
            spp = [ps(f"spp{i}", [P, 4, P]) for i in range(2)]

            names = ("w_in", "x_in", "fsq", "fss", "frs", "mix_done", "mt_mm", "mt_a", "mt_v", "y_mm", "x1_done",
                     "xsq", "xrs", "xn_done", "xt_mm", "q_mm", "q_ev", "s_mm", "s_ev", "route_done", "xcopy",
                     "x_out", "gexp", "csub", "pstep", "vlink", "g2_in")
            S = {n: sem("r_" + n) for n in names}
            LINKS = 23

            @block.sync
            def _(sp):
                sp.dma_start(wout, a["w_out"][0].rearrange("(k p) c -> p k c", p=P)).then_inc(S["w_in"], 16)
                sp.dma_start(grow[:, :], a["norm2_g"].partition_broadcast(P)
                             .rearrange("p a c -> p (a c)")).then_inc(S["g2_in"], 16)
                for k in range(KC):
                    sp.dma_start(wq[:, k, :], a["peer_wq"][0, k * P:(k + 1) * P, :]).then_inc(S["w_in"], 16)
                sp.dma_start(keysT, a["keys_t"]).then_inc(S["w_in"], 16)

                def load(src, t):
                    sp.dma_start(xt, src).then_inc(S["x_in"], 16)
                    after(sp, S["x1_done"], t + 1)
                    sp.dma_start(a["x1"][t], x1).then_inc(S["x_out"], 16)
                    after(sp, S["route_done"], t + 1)

                with sp.Fori(0, PT) as t:
                    load(a["x_prompt"][0, bass.ds(t * P, P), :], t)
                load(a["x_sample"].rearrange("b t d -> (b t) d"), PT)
                sp.wait_ge(S["x_out"], 16 * TILES)

            @block.tensor
            def _(pe):
                pe.wait_ge(S["w_in"], 16 * (2 + KC))
                with pe.Fori(0, TILES) as t:
                    pe.wait_ge(S["mix_done"], t + 1)
                    for k in range(KC):
                        last = nc.tensor.transpose(tp[:, k, :], mixs[:, k * P:(k + 1) * P], ident[:, :])
                    last.then_inc(S["mt_mm"], 1)
                    pe.wait_ge(S["mt_a"], 2 * t + 1)
                    pe.wait_ge(S["mt_v"], 2 * t + 1)
                    for c in range(2):
                        for k in range(KC):
                            last = nc.tensor.matmul(yp[:, 512 * c:512 * c + 512], mT[:, k, :],
                                                    wout[:, k, 512 * c:512 * c + 512],
                                                    start=(k == 0), stop=(k == KC - 1))
                    last.then_inc(S["y_mm"], 1)
                    pe.wait_ge(S["xn_done"], t + 1)
                    for k in range(KC):
                        last = nc.tensor.transpose(tp[:, k, :], xns[:, k * P:(k + 1) * P], ident[:, :])
                    last.then_inc(S["xt_mm"], 1)
                    pe.wait_ge(S["mt_a"], 2 * t + 2)
                    pe.wait_ge(S["mt_v"], 2 * t + 2)
                    for b in range(4):
                        if b >= 2:
                            pe.wait_ge(S["q_ev"], 4 * t + b - 1)
                        for i in range(4):
                            s = 4 * b + i
                            for k in range(KC):
                                last = nc.tensor.matmul(qp[b % 2][:, i, :], wq[:, k, s * P:(s + 1) * P], mT[:, k, :],
                                                        start=(k == 0), stop=(k == KC - 1))
                        last.then_inc(S["q_mm"], 1)
                    for b in range(4):
                        pe.wait_ge(S["q_ev"], 4 * t + b + 1)
                        if b >= 2:
                            pe.wait_ge(S["s_ev"], 4 * t + b - 1)
                        for i in range(4):
                            s = 4 * b + i
                            last = nc.tensor.matmul(spp[b % 2][:, i, :], qTs[:, s, :], keysT[:, s, :],
                                                    start=True, stop=True)
                        last.then_inc(S["s_mm"], 1)
                    pe.wait_ge(S["s_ev"], 4 * t + 4)

            @block.scalar
            def _(act):
                with act.Fori(0, TILES) as t:
                    if True:
                        nc.scalar.activation(sq[:, 0:GW], mixo[:, bass.ds(t, 1), GW:].rearrange("p a c -> p (a c)"),
                                             ACT.Square).then_inc(S["fsq"], 1)
                    after(act, S["mt_mm"], t + 1)
                    nc.scalar.copy(mT[:, 0:4, :], tp[:, 0:4, :]).then_inc(S["mt_a"], 1)
                    after(act, S["x1_done"], t + 1)
                    nc.scalar.activation(sq, x1, ACT.Square, accum_out=ssum[:, 8:9]).then_inc(S["xsq"], 1)
                    after(act, S["xt_mm"], t + 1)
                    nc.scalar.copy(mT[:, 0:4, :], tp[:, 0:4, :]).then_inc(S["mt_a"], 1)
                    for b in range(4):
                        after(act, S["q_mm"], 4 * t + b + 1)
                        nc.scalar.copy(qTs[:, 4 * b:4 * b + 4, :], qp[b % 2][:, :, :]).then_inc(S["q_ev"], 1)
                    for b in range(4):
                        after(act, S["s_mm"], 4 * t + b + 1)
                        nc.scalar.copy(sc[:, 4 * b:4 * b + 4, :], spp[b % 2][:, :, :]).then_inc(S["s_ev"], 1)
                    after(act, S["csub"], t + 1)
                    nc.scalar.activation(ef, ef, ACT.Exp).then_inc(S["gexp"], 1)
                    after(act, S["route_done"], t + 1)

            @block.gpsimd
            def _(pool):
                with pool.Fori(0, TILES) as t:
                    after(pool, S["fss"], t + 1)
                    nc.gpsimd.tensor_scalar(small[:, 16:24], small[:, 0:8], 1.0 / HD, EPS,
                                            ALU.mult, ALU.add).then_inc(S["pstep"], 1)
                    after(pool, S["pstep"], 2 * t + 1)
                    nc.gpsimd.tensor_tensor(small[:, 32:40], small[:, 16:24], nhalf[:, :], ALU.pow
                                            ).then_inc(S["frs"], 1)
                    after(pool, S["xsq"], t + 1)
                    nc.gpsimd.tensor_scalar(ssum[:, 9:10], ssum[:, 8:9], 1.0 / D, EPS,
                                            ALU.mult, ALU.add).then_inc(S["pstep"], 1)
                    after(pool, S["pstep"], 2 * t + 2)
                    nc.gpsimd.tensor_tensor(ssum[:, 10:11], ssum[:, 9:10], nhalf[:, 0:1], ALU.pow
                                            ).then_inc(S["xrs"], 1)
                    after(pool, S["xn_done"], t + 1)
                    nc.gpsimd.tensor_copy(mixo[:, bass.ds(t, 1), :].rearrange("p a c -> p (a c)"), xns
                                          ).then_inc(S["xcopy"], 1)
                    after(pool, S["xcopy"], t + 1)

            @block.vector
            def _(dve):
                dve.wait_ge(S["g2_in"], 16)
                with dve.Fori(0, TILES) as t:
                    count = [0]

                    def link(ins):
                        count[0] += 1
                        ins.then_inc(S["vlink"], 1)
                        after(dve, S["vlink"], LINKS * t + count[0])

                    def mixt(lo, hi):
                        return mixo[:, bass.ds(t, 1), lo:hi].rearrange("p a c -> p (a c)")

                    def heads(ap):
                        return ap.rearrange("p (h d) -> p h d", h=NH)

                    after(dve, S["fsq"], t + 1)
                    nc.vector.tensor_reduce(small[:, 0:8], heads(sq[:, 0:GW]), AX.X, ALU.add).then_inc(S["fss"], 1)
                    nc.vector.tensor_copy(mixs[:, 0:GW], mixt(0, GW))
                    after(dve, S["frs"], t + 1)
                    link(nc.vector.tensor_tensor(heads(mixs[:, GW:]), heads(mixt(GW, D)),
                                                 bc(small[:, 32:40].unsqueeze(2), [P, NH, HD]), ALU.mult))
                    nc.vector.tensor_tensor(mixs[:, GW:], mixs[:, GW:], gain_fox[:, :], ALU.mult
                                            ).then_inc(S["mix_done"], 1)
                    after(dve, S["mt_mm"], t + 1)
                    nc.vector.tensor_copy(mT[:, 4:8, :], tp[:, 4:8, :]).then_inc(S["mt_v"], 1)
                    after(dve, S["y_mm"], t + 1)
                    after(dve, S["x_in"], 16 * t + 16)
                    nc.vector.tensor_tensor(x1, yp[:, :], xt, ALU.add).then_inc(S["x1_done"], 1)
                    after(dve, S["xrs"], t + 1)
                    nc.vector.scalar_tensor_tensor(out=xns, in0=x1, scalar=ssum[:, 10:11], in1=grow[:, :],
                                                   op0=ALU.mult, op1=ALU.mult).then_inc(S["xn_done"], 1)
                    after(dve, S["xt_mm"], t + 1)
                    nc.vector.tensor_copy(mT[:, 4:8, :], tp[:, 4:8, :]).then_inc(S["mt_v"], 1)
                    after(dve, S["s_ev"], 4 * t + 4)
                    for s in range(NSEG):
                        last = nc.vector.max(vals[:, s, 0:8], sc[:, s, :])
                    link(last)
                    for s in range(NSEG):
                        nc.vector.max_index(idx[:, s, 0:8], vals[:, s, 0:8], sc[:, s, :])
                        last = nc.vector.match_replace(sc2[:, s, :], vals[:, s, 0:8], sc[:, s, :], -3e38)
                    link(last)
                    for s in range(NSEG):
                        last = nc.vector.max(vals[:, s, 8:16], sc2[:, s, :])
                    link(last)
                    for s in range(NSEG):
                        last = nc.vector.max_index(idx[:, s, 8:16], vals[:, s, 8:16], sc2[:, s, :])
                    link(last)
                    v4 = vals.rearrange("p (h a) n -> p h a n", a=2)
                    f4 = fidx.rearrange("p (h a) n -> p h a n", a=2)
                    nc.vector.tensor_copy(fidx, idx)
                    link(nc.vector.tensor_tensor(cand.rearrange("p h (i j) -> p h i j", i=TOPK),
                                                 bc(v4[:, :, 0, :].unsqueeze(3), [P, PH, TOPK, TOPK]),
                                                 bc(v4[:, :, 1, :].unsqueeze(2), [P, PH, TOPK, TOPK]), ALU.add))
                    cand2 = sc2.rearrange("p (h a) n -> p h (a n)", a=2)
                    for h in range(PH):
                        last = nc.vector.max(cval[:, h, 0:8], cand[:, h, :])
                    link(last)
                    for h in range(PH):
                        nc.vector.max_index(ci[:, h, 0:8], cval[:, h, 0:8], cand[:, h, :])
                        last = nc.vector.match_replace(cand2[:, h, :], cval[:, h, 0:8], cand[:, h, :], -3e38)
                    link(last)
                    for h in range(PH):
                        last = nc.vector.max(cval[:, h, 8:16], cand2[:, h, :])
                    link(last)
                    for h in range(PH):
                        last = nc.vector.max_index(ci[:, h, 8:16], cval[:, h, 8:16], cand2[:, h, :])
                    link(last)
                    cflat = ci.rearrange("p h n -> p (h n)")
                    link(nc.vector.tensor_scalar(cia, cflat, 4, None, ALU.logical_shift_right))
                    link(nc.vector.tensor_copy(cif[:, 0, :], cia))
                    link(nc.vector.tensor_scalar(cia, cflat, 15, None, ALU.bitwise_and))
                    link(nc.vector.tensor_copy(cif[:, 1, :], cia))
                    for half in range(2):
                        oh = sc.rearrange("p s n -> p (s n)").rearrange("p (k j) -> p k j", j=TOPK)
                        link(nc.vector.tensor_tensor(oh, bc(cif[:, half, :].unsqueeze(2), [P, P, TOPK]),
                                                     bc(iota[:, :].unsqueeze(1), [P, P, TOPK]), ALU.is_equal))
                        oh4 = oh.rearrange("p (h k) j -> p h k j", h=PH)
                        link(nc.vector.tensor_tensor(oh4, oh4,
                                                     bc(f4[:, :, half, :].unsqueeze(2), [P, PH, TOPK, TOPK]),
                                                     ALU.mult))
                        link(nc.vector.tensor_reduce(sel[:, half, :], oh, AX.X, ALU.add))
                    nc.vector.scalar_tensor_tensor(out=idx_all[:, bass.ds(t * P, P)], in0=sel[:, 0, :],
                                                   scalar=float(NKEY), in1=sel[:, 1, :], op0=ALU.mult, op1=ALU.add)
                    nc.vector.tensor_tensor(ef, cval, bc(cval[:, :, 0:1], [P, PH, TOPK]), ALU.subtract
                                            ).then_inc(S["csub"], 1)
                    after(dve, S["gexp"], t + 1)
                    link(nc.vector.tensor_reduce(ssum[:, 0:8], ef, AX.X, ALU.add))
                    link(nc.vector.reciprocal(small[:, 48:56], ssum[:, 0:8]))
                    after(dve, S["x_out"], 16 * t + 16)
                    after(dve, S["xcopy"], t + 1)
                    link(nc.vector.tensor_tensor(gate_all[:, bass.ds(t * P, P)].rearrange("p (h n) -> p h n", h=PH),
                                                 ef, bc(small[:, 48:56].unsqueeze(2), [P, PH, TOPK]), ALU.mult))
                    assert count[0] == LINKS, count[0]
                    dve.sem_inc(S["route_done"], 1)

        def phase_experts(block, sem, ps):
            NU = NV = 8
            ub = Rreg[:, 0:NU * D].rearrange("p (s d) -> p s d", s=NU)
            vb = Rreg[:, NU * D:(NU + NV) * D].rearrange("p (s d) -> p s d", s=NV)
            acc = Hreg[:, 0:2 * D].rearrange("p (s d) -> p s d", s=2)
            junk = Hreg[:, 2 * D:3 * D]
            islot = sb("islot", [P, 2, TOPK], I32)
            dots = sb("dots", [P, 2, TOPK])
            gw = sb("gw", [P, 2, TOPK])
            g1, g2 = sb("g1", [P, TOPK]), sb("g2", [P, TOPK])
            u_in = [sem(f"u_in{i}") for i in range(NU)]
            v_in = [sem(f"v_in{i}") for i in range(NV)]
            u_used, v_used = sem("u_used"), sem("v_used")
            idx_done, dots_done = sem("idx_done"), sem("dots_done")
            gel1, gel2, gw_done = sem("gel1"), sem("gel2"), sem("gw_done")
            acc_in, acc_out, vlink = sem("acc_in"), sem("acc_out"), sem("vlink")
            u_tab, v_tab = a["peer_u"][0], a["peer_v"][0]
            E1 = 7

            def up(g, i):
                return g * TOPK + i

            @block.gpsimd
            def _(pool):
                def load_index(g):
                    nc.gpsimd.tensor_copy(islot[:, bass.ds(g % 2, 1), :].rearrange("p a n -> p (a n)"),
                                          idx_all[:, bass.ds(g * TOPK, TOPK)]).then_inc(idx_done, 1)
                    after(pool, idx_done, g + 1)

                def gather_u(g, par):
                    for i in range(TOPK):
                        s = i % NU
                        if isinstance(g, int) and g == 0 and i < NU:
                            pass
                        else:
                            after(pool, u_used, up(g, i) - NU + 1)
                        nc.gpsimd.indirect_dma_start(
                            ub[:, s, :], None, u_tab,
                            bass.IndirectOffsetOnAxis(ap=islot[:, par, i:i + 1], axis=0)).then_inc(u_in[s], 16)

                def gather_v(g, par):
                    for i in range(TOPK):
                        s = i % NV
                        if isinstance(g, int) and g == 0 and i < NV:
                            pass
                        else:
                            after(pool, v_used, up(g, i) - NV + 1)
                        nc.gpsimd.indirect_dma_start(
                            vb[:, s, :], None, v_tab,
                            bass.IndirectOffsetOnAxis(ap=islot[:, par, i:i + 1], axis=0)).then_inc(v_in[s], 16)

                load_index(0)
                gather_u(0, 0)
                load_index(1)
                gather_u(1, 1)
                gather_v(0, 0)
                with pool.Fori(1, GROUPS // 2) as j:
                    for par in range(2):
                        g = 2 * j + par
                        for s in range(NV):
                            after(pool, v_in[s], 32 * (g - 1))
                        load_index(g)
                        gather_u(g, par)
                        gather_v(g - 1, 1 - par)
                gather_v(GROUPS - 1, 1)

            @block.sync
            def _(sp):
                def out_rows(t):
                    return a["y_prompt"][0, bass.ds(t * P, P), :]

                for t in range(2):
                    sp.dma_start(acc[:, t, :], a["x1"][t]).then_inc(acc_in, 16)
                def store(t):
                    after(sp, v_used, (t + 1) * P)
                    sp.dma_start(out_rows(t), acc[:, bass.ds(t % 2, 1), :].rearrange("p a d -> p (a d)")
                                 ).then_inc(acc_out, 16)

                with sp.Fori(0, PT - 1) as t:
                    store(t)
                    after(sp, acc_out, 16 * t + 16)
                    sp.dma_start(acc[:, bass.ds(t % 2, 1), :].rearrange("p a d -> p (a d)"),
                                 a["x1"][bass.ds(t + 2, 1)].rearrange("a p d -> (a p) d")).then_inc(acc_in, 16)
                store(PT - 1)
                sp.wait_ge(v_used, TILES * P)
                sp.dma_start(a["y_sample"].rearrange("b t d -> (b t) d"), acc[:, ST % 2, :]).then_inc(acc_out, 16)
                sp.wait_ge(acc_out, 16 * TILES)
                sp.wait_ge(acc_in, 16 * TILES)

            @block.scalar
            def _(act):
                with act.Fori(0, GROUPS) as g:
                    after(act, gel1, g + 1)
                    nc.scalar.activation(g2[:, :], g1[:, :], ACT.Exp, scale=-1.0).then_inc(gel2, 1)

            @block.vector
            def _(dve):
                count = [0]

                def dot(g, par):
                    for i in range(TOPK):
                        s = i % NU
                        after(dve, u_in[s], 32 * g + 16 * (i // NU) + 16)
                        nc.vector.scalar_tensor_tensor(
                            out=junk, in0=ub[:, s, :], scalar=1.0,
                            in1=mixo[:, bass.ds(g // PH, 1), :].rearrange("p a d -> p (a d)"),
                            op0=ALU.mult, op1=ALU.mult,
                            accum_out=dots[:, par, i:i + 1]).then_inc(u_used, 1)
                        after(dve, u_used, up(g, i) + 1)

                def weights(g, par):
                    x = dots[:, par, :]
                    base = E1 * g
                    k = [0]

                    def link(ins):
                        k[0] += 1
                        ins.then_inc(vlink, 1)
                        after(dve, vlink, base + k[0])

                    link(nc.vector.tensor_tensor(g1[:, :], x, x, ALU.mult))
                    link(nc.vector.tensor_scalar(g1[:, :], g1[:, :], GELU_C * 0.044715, GELU_C, ALU.mult, ALU.add))
                    link(nc.vector.tensor_tensor(g1[:, :], g1[:, :], x, ALU.mult))
                    nc.vector.tensor_scalar_max(g1[:, :], g1[:, :], -80.0).then_inc(gel1, 1)
                    after(dve, gel2, g + 1)
                    link(nc.vector.tensor_scalar_add(g1[:, :], g2[:, :], 1.0))
                    link(nc.vector.reciprocal(g1[:, :], g1[:, :]))
                    link(nc.vector.tensor_tensor(g1[:, :], g1[:, :], x, ALU.mult))
                    link(nc.vector.tensor_tensor(gw[:, par, :], g1[:, :], gate_all[:, bass.ds(g * TOPK, TOPK)],
                                                 ALU.mult))

                def add(g, par):
                    for i in range(TOPK):
                        s = i % NV
                        after(dve, v_in[s], 32 * g + 16 * (i // NV) + 16)
                        ac = acc[:, bass.ds((g // PH) % 2, 1), :].rearrange("p a d -> p (a d)")
                        nc.vector.scalar_tensor_tensor(out=ac, in0=vb[:, s, :], scalar=gw[:, par, i:i + 1], in1=ac,
                                                       op0=ALU.mult, op1=ALU.add).then_inc(v_used, 1)
                        after(dve, v_used, up(g, i) + 1)

                dve.wait_ge(acc_in, 32)
                dot(0, 0)
                weights(0, 0)
                dot(1, 1)
                add(0, 0)
                weights(1, 1)
                with dve.Fori(1, GROUPS // 2) as j:
                    for par in range(2):
                        g = 2 * j + par
                        dot(g, par)
                        dve.wait_ge(acc_in, 16 * ((g - 1) // PH) + 16)
                        add(g - 1, 1 - par)
                        weights(g, par)
                add(GROUPS - 1, 1)

        program(phase_norm)
        program(projection([RQ, RK, RV]))
        program(phase_retention)
        program(projection([RG, FQ, FK, FV]))
        program(phase_fox)
        program(phase_route)
        program(phase_experts)


def shape_constants():
    f = np.float32
    n = np.arange(P)
    pos = np.empty((P, TILES), np.float64)
    for t in range(PT):
        pos[:, t] = t * P + n
    pos[:, ST] = PAST + n % NS
    inv = (10000.0 ** (-np.arange(32, dtype=f) / 32)).astype(f)
    ang = (pos.astype(f)[:, :, None] * inv[None, None, :]).astype(f).astype(np.float64)
    lg = np.log1p(-(2.0 ** (-5.0 - np.arange(NH))))
    step = np.stack([n + 1.0, n % NS + 1.0])
    grown = lg[None, None, :] * step[:, :, None]
    dec = np.stack([np.exp(grown), np.exp(-grown) * HD ** -0.5])
    span = np.array([P, NS])
    sdec = np.empty((P, 2, PAIRS))
    for par in range(2):
        for r in range(PAIRS):
            sdec[64 * par:64 * par + 64, :, r] = np.exp(lg[2 * r + par] * span)[None, :]
    same = (n[:, None] // NS) == (n[None, :] // NS)
    later = n[:, None] <= n[None, :]
    causal = np.stack([later, later & same], axis=1)
    maskq = np.where(n[None, :] > n[:, None], BIG, 0.0)
    maskn = np.where(np.arange(NS)[None, :] > (n % NS)[:, None], BIG, 0.0)
    e8 = np.zeros((NH, NH, P))
    e8[np.arange(NH), np.arange(NH), :] = 1.0
    e64 = np.zeros((NB * NH, NB, P))
    for b in range(NB):
        for m in range(P):
            e64[b * NH + m // NS, b, m] = 1.0
    return {
        "c_ident": np.eye(P, dtype=f), 
        "c_causal": causal.astype(f), "c_masks": np.concatenate([maskq, maskn], axis=1).astype(f),
         "c_cos": np.cos(ang).astype(f),
        "c_nsin": (-np.sin(ang)).astype(f), "c_psin": np.sin(ang).astype(f),
        "c_dec": np.ascontiguousarray(dec.transpose(2, 0, 1, 3)).astype(f), "c_sdec": sdec.astype(f),
        "c_bind": (n[:, None] // NS == np.arange(NB)[None, :]).astype(f),
        "c_iota": np.broadcast_to(np.arange(TOPK, dtype=f), (P, TOPK)).copy(),
        "c_e8": e8.astype(f), "c_e64": e64.astype(f),
    }


_DIRECT = ["x_prompt", "x_sample", "cache_fox_k", "cache_fox_v", "state_ret", "norm1_g", "w_in", "b_f", "fox_qn_g",
           "fox_kn_g", "ret_out_g", "fox_out_g", "w_out", "norm2_g", "peer_wq", "peer_u", "peer_v"]
_OUTS = [("y_prompt", (1, NP_TOK, D)), ("y_sample", (NB, NS, D)),
         ("new_fox_k_p", (1, 1, NP_TOK, NH, HD)), ("new_fox_v_p", (1, 1, NP_TOK, NH, HD)),
         ("new_fox_logf_p", (1, 1, NP_TOK, NH)), ("new_state_ret_p", (1, 1, NH, HD, HD)),
         ("new_fox_k_s", (1, NB, NS, NH, HD)), ("new_fox_v_s", (1, NB, NS, NH, HD)),
         ("new_fox_logf_s", (1, NB, NS, NH)), ("new_state_ret_s", (1, NB, NH, HD, HD))]


def kernel(**inputs):
    import concourse.bacc as _bacc
    from concourse.bass_utils import run_bass_kernel_spmd as _run

    nc = _bacc.Bacc("TRN2", target_bir_lowering=False, num_devices=1)
    data = {n: np.ascontiguousarray(inputs[n]) for n in _DIRECT}
    data["cache_lf_t"] = np.ascontiguousarray(
        np.asarray(inputs["cache_fox_logf"])[0].transpose(0, 2, 1).reshape(NB * NH, PAST))
    data["keys_t"] = np.ascontiguousarray(
        np.asarray(inputs["peer_keys"])[0].transpose(3, 1, 0, 2).reshape(P, 2 * PH, NKEY))
    data["c_wff"] = np.ascontiguousarray(
        np.asarray(inputs["w_in"])[0, :, 7 * GW:].reshape(KC, P, NH).transpose(1, 0, 2))
    data.update(shape_constants())
    arrays, a = {}, {}
    for name, v in data.items():
        arrays[f"in_{name}"] = v
        a[name] = nc.dram_tensor(f"in_{name}", v.shape, mybir.dt.from_np(v.dtype), kind="ExternalInput").ap()
    for name, shape in _OUTS:
        a[name] = nc.dram_tensor(f"out_{name}", shape, F32, kind="ExternalOutput").ap()
    a["x1"] = nc.dram_tensor("x1_scratch", (TILES, P, D), F32, kind="Internal").ap()
    emit(nc, a)
    r = _run(nc, [arrays], core_ids=[0])
    return tuple(r.results[0][f"out_{name}"] for name, _ in _OUTS)
```

```python
import math

import numpy as np

import concourse.bass as bass
from concourse import mybir
from contextlib import ExitStack

F32 = mybir.dt.float32
BF16 = mybir.dt.bfloat16
U32 = mybir.dt.uint32
I32 = mybir.dt.int32
ALU = mybir.AluOpType
ACT = mybir.ActivationFunctionType
AX = mybir.AxisListType

P = 128
D = 1024
KC = D // P
NP_TOK, NB, NS, PAST = 1024, 8, 16, 256
TILES = (NP_TOK + NB * NS) // P
PT = NP_TOK // P
ST = PT
NH, HD = 8, 64
GW = NH * HD
PAIRS = NH // 2
EPS = 1e-6
BIG = 1e30
TOPK, NKEY, PH = 16, 128, 8
GELU_C = 2.0 * math.sqrt(2.0 / math.pi)


def emit(nc, a):
    ctx = ExitStack()
    with ctx:
        def sb(name, shape, dt=F32):
            return ctx.enter_context(nc.sbuf_tensor(name, shape, dt))

        def flat(name, n):
            return sb(name, [P, n])

        Hreg = flat("Hreg", KC * P * TILES)
        Wreg = flat("Wreg", 2 * KC * GW)
        Rreg = flat("Rreg", 4 * TILES * GW)
        mixo = sb("mixo", [P, TILES, 2 * GW])
        Xreg = flat("Xreg", 4384)
        hT = Hreg[:, :].rearrange("p (k n) -> p k n", k=KC)
        wbuf = Wreg[:, :].rearrange("p (s k c) -> p s k c", s=2, k=KC)
        quarter = TILES * GW
        qT = Rreg[:, 0:quarter].rearrange("p (r n) -> p r n", r=PAIRS)
        kT = Rreg[:, quarter:2 * quarter].rearrange("p (r n) -> p r n", r=PAIRS)
        vn = Rreg[:, 2 * quarter:3 * quarter].rearrange("p (t c) -> p t c", t=TILES)
        kn = Rreg[:, 3 * quarter:4 * quarter].rearrange("p (t c) -> p t c", t=TILES)

        ident = sb("ident", [P, P])
        identb = sb("identb", [P, P], BF16)
        causal = sb("causal", [P, 2, P])
        maskq = sb("maskq", [P, P], BF16)
        maskn = sb("maskn", [P, NS], BF16)
        cosn = mixo[:, 0, GW:GW + 32 * TILES].rearrange("p (t d) -> p t d", t=TILES)
        nsin = mixo[:, 1, GW:GW + 32 * TILES].rearrange("p (t d) -> p t d", t=TILES)
        psin = mixo[:, 2, GW:GW + 32 * TILES].rearrange("p (t d) -> p t d", t=TILES)
        gain_fq, gain_fk, gain_ret = (mixo[:, 3 + i, GW:] for i in range(3))
        grow1 = mixo[:, 7, :]
        dec = sb("dec", [P, 2, 2, NH])
        sdec = sb("sdec", [P, 2, PAIRS])
        bind = sb("bind", [P, NB])
        iota = sb("iota", [P, TOPK])
        nhalf = sb("nhalf", [P, NH])
        gain_fox = sb("gain_fox", [P, GW])
        grow = sb("grow", [P, D])
        bfb = sb("bfb", [P, NH])
        ffw = sb("ffw", [P, KC, NH])
        lgf = sb("lgf", [P, TILES, NH])
        lgfT = Hreg[0:NH, 7040:7040 + TILES * P]
        small = sb("small", [P, 64])

        def bc(ap, shape):
            return ap.to_broadcast(shape)

        held = ctx.enter_context(nc.semaphore("held"))

        def after(engine, semaphore, value):
            engine.wait_ge(semaphore, value)
            engine.sem_inc(held, 1)

        phases, used = [], []

        def recycle():
            nc.clear_and_free_semaphores(used)
            used.clear()
            nc.all_engine_barrier()

        def program(body):
            phases.append(body)
            with ExitStack() as ph:
                def sem(name):
                    used.append(nc.alloc_semaphore(f"{name}_{len(phases)}"))
                    return used[-1]

                def ps(name, shape):
                    return ph.enter_context(nc.psum_tensor(f"{name}_{len(phases)}", shape, F32))

                block = ph.enter_context(nc.Block())
                body(block, sem, ps)

        def phase_norm(block, sem, ps):
            const_in = sem("const_in")
            x_in = [sem(f"x_in{i}") for i in range(2)]
            sq_done, rs_done, xs_done = sem("sq_done"), sem("rs_done"), sem("xs_done")
            tr_done, ev_done, ev2_done = sem("tr_done"), sem("ev_done"), sem("ev2_done")
            pool_step = sem("pool_step")
            xt = Xreg[:, 0:2 * D].rearrange("p (s d) -> p s d", s=2)
            xs = Xreg[:, 2 * D:4 * D].rearrange("p (s d) -> p s d", s=2)
            junk = Rreg[:, 0:D]
            tp = [ps(f"tp{i}", [P, 4, P]) for i in range(4)]
            masks = Xreg[:, 4 * D:4 * D + P + NS]
            loads = [(ident, a["c_ident"]), (causal, a["c_causal"]), (masks, a["c_masks"]), (cosn, a["c_cos"]), (nsin, a["c_nsin"]), (psin, a["c_psin"]),
                     (dec, a["c_dec"]), (sdec, a["c_sdec"]), (bind, a["c_bind"]), (iota, a["c_iota"])]
            grows = [(gain_fq, a["fox_qn_g"]), (gain_fk, a["fox_kn_g"]), (gain_ret, a["ret_out_g"]),
                     (gain_fox[:, :], a["fox_out_g"])]
            n_const = 16 * (len(loads) + len(grows) + 2)

            def x_rows(t):
                return a["x_prompt"][0, t * P:(t + 1) * P, :] if t < PT else \
                    a["x_sample"].rearrange("b t d -> (b t) d")

            @block.sync
            def _(sp):
                for t in range(TILES):
                    if t >= 2:
                        sp.wait_ge(xs_done, t - 1)
                    sp.dma_start(xt[:, t % 2, :], x_rows(t)).then_inc(x_in[t % 2], 16)

            @block.scalar
            def _(act):
                for dst, src in loads:
                    act.dma_start(dst[tuple(slice(None) for _ in dst.shape)], src).then_inc(const_in, 16)
                for dst, g in grows:
                    act.dma_start(dst, g.rearrange("a h d -> a (h d)").partition_broadcast(P)
                                  .rearrange("p a c -> p (a c)")).then_inc(const_in, 16)
                act.dma_start(grow1, a["norm1_g"].partition_broadcast(P)
                              .rearrange("p a c -> p (a c)")).then_inc(const_in, 16)
                act.dma_start(bfb[:, :], a["b_f"].partition_broadcast(P)
                              .rearrange("p a c -> p (a c)")).then_inc(const_in, 16)

                def evacuate(t):
                    act.wait_ge(tr_done, t + 1)
                    nc.scalar.copy(hT[:, 0:4, t * P:(t + 1) * P], tp[2 * (t % 2)][:, :, :]).then_inc(ev_done, 1)

                for t in range(TILES):
                    act.wait_ge(x_in[t % 2], 16 * (t // 2 + 1))
                    nc.scalar.activation(junk, xt[:, t % 2, :], ACT.Square,
                                         accum_out=small[:, t:t + 1]).then_inc(sq_done, 1)
                    act.wait_ge(sq_done, t + 1)
                    if t >= 1:
                        evacuate(t - 1)
                evacuate(TILES - 1)

            @block.gpsimd
            def _(pool):
                nc.gpsimd.memset(nhalf[:, :], -0.5).then_inc(pool_step, 1)
                pool.wait_ge(pool_step, 1)
                for t in range(TILES):
                    pool.wait_ge(sq_done, t + 1)
                    nc.gpsimd.tensor_scalar(small[:, 16 + t:17 + t], small[:, t:t + 1], 1.0 / D, EPS,
                                            ALU.mult, ALU.add).then_inc(pool_step, 1)
                    pool.wait_ge(pool_step, t + 2)
                    nc.gpsimd.tensor_tensor(small[:, 32 + t:33 + t], small[:, 16 + t:17 + t], nhalf[:, 0:1],
                                            ALU.pow).then_inc(rs_done, 1)

            @block.vector
            def _(dve):
                dve.wait_ge(const_in, n_const)
                nc.vector.tensor_copy(identb[:, :], ident[:, :])
                nc.vector.tensor_copy(maskq[:, :], masks[:, 0:P])
                nc.vector.tensor_copy(maskn[:, :], masks[:, P:])
                for t in range(TILES + 1):
                    if t < TILES:
                        dve.wait_ge(rs_done, t + 1)
                        if t >= 2:
                            dve.wait_ge(tr_done, t - 1)
                        nc.vector.scalar_tensor_tensor(out=xs[:, t % 2, :], in0=xt[:, t % 2, :],
                                                       scalar=small[:, 32 + t:33 + t], in1=grow1,
                                                       op0=ALU.mult, op1=ALU.mult).then_inc(xs_done, 1)
                    if t >= 1:
                        dve.wait_ge(tr_done, t)
                        nc.vector.tensor_copy(hT[:, 4:8, (t - 1) * P:t * P],
                                              tp[2 * ((t - 1) % 2) + 1][:, :, :]).then_inc(ev2_done, 1)

            @block.tensor
            def _(pe):
                pe.wait_ge(const_in, n_const)
                for t in range(TILES):
                    pe.wait_ge(xs_done, t + 1)
                    if t >= 2:
                        pe.wait_ge(ev_done, t - 1)
                        pe.wait_ge(ev2_done, t - 1)
                    for k in range(KC):
                        last = nc.tensor.transpose(tp[2 * (t % 2) + k // 4][:, k % 4, :],
                                                   xs[:, t % 2, k * P:(k + 1) * P], ident[:, :])
                    last.then_inc(tr_done, 1)

        RQ, RK, RV, RG, FQ, FK, FV = range(7)

        def projection(groups):
            def body(block, sem, ps):
                steps = [(g, t) for g in groups for t in range(TILES)]
                turned = [n for n, (g, _) in enumerate(steps) if g in (RQ, RK, FQ, FK)]
                order = {n: m for m, n in enumerate(turned)}
                normed = [n for n, (g, _) in enumerate(steps) if g in (RG, FQ, FK)]
                norder = {n: m for m, n in enumerate(normed)}
                w_in = [sem(f"w_in{i}") for i in range(2)]
                w_used, z_done = sem("w_used"), sem("z_done")
                z_free = [sem(f"z_free{i}") for i in range(3)]
                rot_done, tr_done, ev_done = sem("rot_done"), sem("tr_done"), sem("ev_done")
                link_sem, v_done = sem("link_sem"), sem("v_done")
                with_ff = FV in groups
                if with_ff:
                    sq_done, ss_done, rs_done = sem("sq_done"), sem("ss_done"), sem("rs_done")
                    pool_step, gate_exp, out_done = sem("pool_step"), sem("gate_exp"), sem("out_done")
                    ff_in, ff_done, ff_z, ff_abs = sem("ff_in"), sem("ff_done"), sem("ff_z"), sem("ff_abs")
                    ff_exp, ff_e1, ff_ln, ff_log = sem("ff_exp"), sem("ff_e1"), sem("ff_ln"), sem("ff_log")
                    ffT = sem("ffT")
                z = [ps(f"z{i}", [P, GW]) for i in range(3)]
                tp = [ps(f"ztp{i}", [P, 4, P]) for i in range(2)]
                ffp = ps("ffp", [P, TILES, NH])
                ffpt = ps("ffpt", [NH, 2, 512])
                tmp = Xreg[:, 0:8 * GW].rearrange("p (s c) -> p s c", s=8)
                ffx = Xreg[:, 8 * GW:8 * GW + 4 * TILES * NH].rearrange("p (s t h) -> p s t h", s=4, t=TILES)

                def heads(ap):
                    return ap.rearrange("p (h d) -> p h d", h=NH)

                @block.sync
                def _(sp):
                    for gi, g in enumerate(groups):
                        if gi >= 2:
                            sp.wait_ge(w_used, gi - 1)
                        sp.dma_start(wbuf[:, gi % 2], a["w_in"][0, :, g * GW:(g + 1) * GW]
                                     .rearrange("(k p) c -> p k c", p=P)).then_inc(w_in[gi % 2], 16)
                    outs = 0
                    if with_ff:
                        sp.dma_start(ffw[:, :, :], a["c_wff"]).then_inc(ff_in, 16)
                    for n, (g, t) in enumerate(steps):
                        if g == FK:
                            sp.wait_ge(rot_done, order[n] + 1)
                            src, dk = kn[:, t, :], "new_fox_k"
                        elif g == FV:
                            sp.wait_ge(v_done, t + 1)
                            src, dk = vn[:, t, :], "new_fox_v"
                        else:
                            continue
                        dst = a[dk + "_p"][0, 0, t * P:(t + 1) * P].rearrange("n h d -> n (h d)") if t < PT else \
                            a[dk + "_s"][0].rearrange("b n h d -> (b n) (h d)")
                        sp.dma_start(dst, src).then_inc(out_done, 16)
                        outs += 1
                    if with_ff:
                        sp.wait_ge(ff_log, 1)
                        sp.dma_start(a["new_fox_logf_p"][0, 0].rearrange("(t p) h -> p t h", p=P),
                                     lgf[:, 0:PT, :]).then_inc(out_done, 16)
                        sp.dma_start(a["new_fox_logf_s"][0].rearrange("b n h -> (b n) h"),
                                     lgf[:, ST, :]).then_inc(out_done, 16)
                        outs += 2
                    if outs:
                        sp.wait_ge(out_done, 16 * outs)

                @block.tensor
                def _(pe):
                    def turn(n):
                        m = order[n]
                        g, t = steps[n]
                        pe.wait_ge(rot_done, m + 1)
                        if m >= 2:
                            pe.wait_ge(ev_done, m - 1)
                        src = tmp[:, 6 + m % 2, :] if g in (RQ, FQ) else kn[:, t, :]
                        for r in range(PAIRS):
                            last = nc.tensor.transpose(tp[m % 2][:, r, :], src[:, r * P:(r + 1) * P], ident[:, :])
                        last.then_inc(tr_done, 1)

                    for n, (g, t) in enumerate(steps):
                        gi = n // TILES
                        if t == 0:
                            pe.wait_ge(w_in[gi % 2], 16 * (gi // 2 + 1))
                        if n >= 3:
                            pe.wait_ge(z_free[n % 3], n // 3)
                        for k in range(KC):
                            last = nc.tensor.matmul(z[n % 3][:, :], hT[:, k, t * P:(t + 1) * P],
                                                    wbuf[:, gi % 2, k, :], start=(k == 0), stop=(k == KC - 1))
                        last.then_inc(z_done, 1)
                        if t == TILES - 1:
                            pe.wait_ge(z_done, n + 1)
                            pe.sem_inc(w_used, 1)
                        if n - 1 in order:
                            turn(n - 1)
                    if len(steps) - 1 in order:
                        turn(len(steps) - 1)
                    if with_ff:
                        pe.wait_ge(ff_in, 16)
                        for t in range(TILES):
                            for k in range(KC):
                                last = nc.tensor.matmul(ffp[:, t, :], hT[:, k, t * P:(t + 1) * P], ffw[:, k, :],
                                                        start=(k == 0), stop=(k == KC - 1))
                        last.then_inc(ff_done, 1)
                        pe.wait_ge(ff_log, 1)
                        for t in range(TILES):
                            if t == PT:
                                pe.wait_ge(ffT, 1)
                            last = nc.tensor.transpose(ffpt[:, (t // 4) % 2, (t % 4) * P:(t % 4 + 1) * P],
                                                       lgf[:, t, :], ident[:, :])
                            if t == PT - 1 or t == ST:
                                last.then_inc(tr_done, 1)

                @block.scalar
                def _(act):
                    def evacuate(n):
                        m = order[n]
                        g, t = steps[n]
                        act.wait_ge(tr_done, m + 1)
                        dst = qT if g in (RQ, FQ) else kT
                        nc.scalar.copy(dst[:, :, t * P:(t + 1) * P], tp[m % 2][:, :, :]).then_inc(ev_done, 1)

                    for n, (g, t) in enumerate(steps):
                        if g in (RV, FV):
                            act.wait_ge(z_done, n + 1)
                            nc.scalar.copy(vn[:, t, :], z[n % 3][:, :]).then_inc(z_free[n % 3], 1)
                            act.wait_ge(z_free[n % 3], n // 3 + 1)
                            act.sem_inc(v_done, 1)
                        if g in (FQ, FK):
                            m = norder[n]
                            act.wait_ge(z_done, n + 1)
                            if m >= 2:
                                act.wait_ge(ss_done, m - 1)
                            nc.scalar.activation(tmp[:, m % 2, :], z[n % 3][:, :], ACT.Square).then_inc(sq_done, 1)
                        if g == RG:
                            m = norder[n]
                            if m >= 2:
                                act.wait_ge(ss_done, m - 1)
                            nc.scalar.activation(tmp[:, m % 2, :], mixo[:, t, 0:GW], ACT.Square).then_inc(sq_done, 1)
                            act.wait_ge(z_done, n + 1)
                            if n >= 2:
                                act.wait_ge(z_free[(n - 2) % 3], (n - 2) // 3 + 1)
                            nc.scalar.activation(tmp[:, 2 + m % 2, :], z[n % 3][:, :], ACT.Exp,
                                                 scale=-1.0).then_inc(gate_exp, 1)
                        if n - 1 in order:
                            evacuate(n - 1)
                    if len(steps) - 1 in order:
                        evacuate(len(steps) - 1)
                    if with_ff:
                        act.wait_ge(ff_z, 1)
                        nc.scalar.activation(ffx[:, 1], ffx[:, 0], ACT.Abs).then_inc(ff_abs, 1)
                        act.wait_ge(ff_abs, 1)
                        nc.scalar.activation(ffx[:, 2], ffx[:, 1], ACT.Exp, scale=-1.0).then_inc(ff_exp, 1)
                        act.wait_ge(ff_e1, 1)
                        nc.scalar.activation(ffx[:, 1], ffx[:, 3], ACT.Ln).then_inc(ff_ln, 1)
                        act.wait_ge(tr_done, len(order) + 1)
                        nc.scalar.copy(lgfT[:, 0:NP_TOK], ffpt[:, :, :].rearrange("h a n -> h (a n)")).then_inc(ffT, 1)
                        act.wait_ge(tr_done, len(order) + 2)
                        nc.scalar.copy(lgfT[:, NP_TOK:], ffpt[:, 0, 0:P])

                @block.gpsimd
                def _(pool):
                    steps_done = 0
                    for m, n in enumerate(normed):
                        g, t = steps[n]
                        o = 8 * (m % 2)
                        pool.wait_ge(ss_done, m + 1)
                        nc.gpsimd.tensor_scalar(small[:, 16 + o:24 + o], small[:, o:o + 8], 1.0 / HD, EPS,
                                                ALU.mult, ALU.add).then_inc(pool_step, 1)
                        steps_done += 1
                        pool.wait_ge(pool_step, steps_done)
                        ins = nc.gpsimd.tensor_tensor(small[:, 32 + o:40 + o], small[:, 16 + o:24 + o],
                                                      nhalf[:, :], ALU.pow)
                        if g == FQ:
                            ins.then_inc(pool_step, 1)
                            steps_done += 1
                            pool.wait_ge(pool_step, steps_done)
                            ins = nc.gpsimd.tensor_scalar(small[:, 32 + o:40 + o], small[:, 32 + o:40 + o],
                                                          -(HD ** -0.5), None, ALU.mult)
                        ins.then_inc(rs_done, 1)

                @block.vector
                def _(dve):
                    count = [0]

                    def link(ins):
                        count[0] += 1
                        ins.then_inc(link_sem, 1)
                        dve.wait_ge(link_sem, count[0])

                    for n, (g, t) in enumerate(steps):
                        zn = z[n % 3][:, :]
                        kind = 0 if t < PT else 1
                        if g in (RQ, RK):
                            m = order[n]
                            dve.wait_ge(z_done, n + 1)
                            z4 = zn.rearrange("p (h a d) -> p h a d", h=NH, a=2)
                            A = tmp[:, 2, :].rearrange("p (h a d) -> p h a d", h=NH, a=2)
                            B = tmp[:, 3, :].rearrange("p (h a d) -> p h a d", h=NH, a=2)
                            cs = bc(cosn[:, t, :].unsqueeze(1).unsqueeze(1), [P, NH, 2, 32])
                            nc.vector.tensor_tensor(A, z4, cs, ALU.mult)
                            nc.vector.tensor_tensor(B[:, :, 0, :], z4[:, :, 1, :],
                                                    bc(nsin[:, t, :].unsqueeze(1), [P, NH, 32]), ALU.mult)
                            count[0] += 1
                            nc.vector.tensor_tensor(B[:, :, 1, :], z4[:, :, 0, :],
                                                    bc(psin[:, t, :].unsqueeze(1), [P, NH, 32]),
                                                    ALU.mult).then_inc(link_sem, 1)
                            dve.wait_ge(link_sem, count[0])
                            dve.sem_inc(z_free[n % 3], 1)
                            link(nc.vector.tensor_tensor(tmp[:, 4, :], tmp[:, 2, :], tmp[:, 3, :], ALU.add))
                            if g == RQ:
                                if m >= 2:
                                    dve.wait_ge(tr_done, m - 1)
                                dst = tmp[:, 6 + m % 2, :]
                            else:
                                dst = kn[:, t, :]
                            nc.vector.tensor_tensor(
                                heads(dst), heads(tmp[:, 4, :]),
                                bc(dec[:, 0 if g == RQ else 1, kind, :].unsqueeze(2), [P, NH, HD]),
                                ALU.mult).then_inc(rot_done, 1)
                        if g in (RG, FQ, FK):
                            m = norder[n]
                            o = 8 * (m % 2)
                            dve.wait_ge(sq_done, m + 1)
                            nc.vector.tensor_reduce(small[:, o:o + 8], heads(tmp[:, m % 2, :]), AX.X,
                                                    ALU.add).then_inc(ss_done, 1)
                            if g == RG:
                                dve.wait_ge(gate_exp, m + 1)
                                link(nc.vector.tensor_scalar_add(tmp[:, 4, :], tmp[:, 2 + m % 2, :], 1.0))
                                link(nc.vector.reciprocal(tmp[:, 5, :], tmp[:, 4, :]))
                                link(nc.vector.tensor_tensor(tmp[:, 4, :], zn, tmp[:, 5, :], ALU.mult))
                                dve.sem_inc(z_free[n % 3], 1)
                                link(nc.vector.tensor_tensor(tmp[:, 5, :], tmp[:, 4, :], gain_ret, ALU.mult))
                                link(nc.vector.tensor_tensor(tmp[:, 4, :], tmp[:, 5, :], mixo[:, t, 0:GW], ALU.mult))
                                dve.wait_ge(rs_done, m + 1)
                                link(nc.vector.tensor_tensor(heads(mixo[:, t, 0:GW]), heads(tmp[:, 4, :]),
                                                             bc(small[:, 32 + o:40 + o].unsqueeze(2), [P, NH, HD]),
                                                             ALU.mult))
                            else:
                                mt = order[n]
                                dve.wait_ge(rs_done, m + 1)
                                link(nc.vector.tensor_tensor(heads(tmp[:, 4, :]), heads(zn),
                                                             bc(small[:, 32 + o:40 + o].unsqueeze(2), [P, NH, HD]),
                                                             ALU.mult))
                                dve.sem_inc(z_free[n % 3], 1)
                                if g == FQ:
                                    if mt >= 2:
                                        dve.wait_ge(tr_done, mt - 1)
                                    dst = tmp[:, 6 + mt % 2, :]
                                else:
                                    dst = kn[:, t, :]
                                nc.vector.tensor_tensor(dst, tmp[:, 4, :], gain_fq if g == FQ else gain_fk,
                                                        ALU.mult).then_inc(rot_done, 1)
                    if with_ff:
                        dve.wait_ge(ff_done, 1)
                        nc.vector.tensor_tensor(ffx[:, 0], ffp[:, :, :], bc(bfb[:, :].unsqueeze(1), [P, TILES, NH]),
                                                ALU.add).then_inc(ff_z, 1)
                        dve.wait_ge(ff_exp, 1)
                        nc.vector.tensor_scalar_add(ffx[:, 3], ffx[:, 2], 1.0).then_inc(ff_e1, 1)
                        dve.wait_ge(ff_ln, 1)
                        nc.vector.scalar_tensor_tensor(out=lgf[:, :, :], in0=ffx[:, 0], scalar=0.0, in1=ffx[:, 1],
                                                       op0=ALU.min, op1=ALU.subtract).then_inc(ff_log, 1)
            return body

        def phase_retention(block, sem, ps):
            st = Wreg[:, 0:PAIRS * HD].rearrange("p (r e) -> p r e", r=PAIRS)
            stt = Wreg[:, 256:512].rearrange("p (r e) -> p r e", r=PAIRS)
            sT = Wreg[:, 512:512 + 2 * NH * P].rearrange("p (s q r l) -> p s q r l", s=2, q=2, r=PAIRS)
            s0 = Wreg[:, 2560:2560 + 2048].rearrange("p (r b e) -> p r b e", r=PAIRS, b=NB)
            vbd = Wreg[:, 4608:4608 + 2 * GW].rearrange("p (s b e) -> p s b e", s=2, b=NB)
            sadd = Wreg[:, 5632:5632 + 2048].rearrange("p (r b e) -> p r b e", r=PAIRS, b=NB)
            oT = Wreg[:, 7680:7680 + GW].rearrange("p (r l) -> p r l", r=PAIRS)
            sc = [ps(f"sc{i}", [P, 4, P]) for i in range(2)]
            op_all = [[ps(f"op{i}{j}", [P, GW]) for j in range(2)] for i in range(2)]
            op = [[b[:, 0:PAIRS * HD].rearrange("p (r e) -> p r e", r=PAIRS) for b in row] for row in op_all]
            up_all = ps("up", [P, GW])
            up = up_all[:, 0:PAIRS * HD].rearrange("p (r e) -> p r e", r=PAIRS)
            opT = ps("opT", [P, PAIRS, P])
            snew = [op_all[i][0][:, :].rearrange("p (b e) -> p b e", b=NB) for i in range(2)]
            sc_done, mask_done, o_done, oev = sem("sc_done"), sem("mask_done"), sem("o_done"), sem("oev")
            up_done, st_done, link_sem = sem("up_done"), sem("st_done"), sem("link_sem")
            s0_in, oT_done, oTc, vb_done = sem("s0_in"), sem("oT_done"), sem("oTc"), sem("vb_done")
            sn_done, sn_out, out_done, oTt = sem("sn_done"), sem("sn_out"), sem("out_done"), sem("oTt")

            @block.sync
            def _(sp):
                for par in range(2):
                    for r in range(PAIRS):
                        sp.dma_start(s0[64 * par:64 * par + 64, r],
                                     a["state_ret"][0, :, 2 * r + par].rearrange("b d e -> d b e")).then_inc(s0_in, 16)
                sp.wait_ge(st_done, PT)
                for par in range(2):
                    sp.dma_start(a["new_state_ret_p"][0, 0].rearrange("(r q) d e -> q d r e", q=2)[par],
                                 st[64 * par:64 * par + 64]).then_inc(out_done, 16)
                for r in range(PAIRS):
                    sp.wait_ge(sn_out, r + 1)
                    for par in range(2):
                        sp.dma_start(a["new_state_ret_s"][0, :, 2 * r + par].rearrange("b d e -> d b e"),
                                     sadd[64 * par:64 * par + 64, r]).then_inc(out_done, 16)
                sp.wait_ge(out_done, 16 * (2 + 2 * PAIRS))

            @block.tensor
            def _(pe):
                def scores(t):
                    for half in range(2):
                        if t >= 1:
                            pe.wait_ge(mask_done, 2 * (t - 1) + half + 1)
                        for r in range(PAIRS):
                            b0 = 64 * half
                            last = nc.tensor.matmul(sc[half][:, r, :], kT[b0:b0 + 64, r, t * P:(t + 1) * P],
                                                    qT[b0:b0 + 64, r, t * P:(t + 1) * P], start=True, stop=True)
                        last.then_inc(sc_done, 1)

                def outputs(t):
                    if t >= 2:
                        pe.wait_ge(oev, t - 1)
                    if t >= 1:
                        pe.wait_ge(st_done, t)
                    for h in range(NH):
                        if h < 2:
                            pe.wait_ge(mask_done, 2 * t + h + 1)
                        b0, r = 64 * (h % 2), h // 2
                        o = op[h % 2][t % 2][:, r, :]
                        last = nc.tensor.matmul(o, sT[:, t % 2, h % 2, r, :], vn[:, t, h * HD:(h + 1) * HD],
                                                start=True, stop=(t == 0))
                        if t:
                            last = nc.tensor.matmul(o, qT[b0:b0 + 64, r, t * P:(t + 1) * P],
                                                    st[b0:b0 + 64, r, :], start=False, stop=True)
                    last.then_inc(o_done, 1)
                    for h in range(NH):
                        b0, r = 64 * (h % 2), h // 2
                        last = nc.tensor.matmul(up[b0:b0 + 64, r, :], kn[:, t, h * HD:(h + 1) * HD],
                                                vn[:, t, h * HD:(h + 1) * HD], start=True, stop=True)
                    last.then_inc(up_done, 1)

                scores(0)
                for t in range(PT):
                    scores(t + 1)
                    outputs(t)
                pe.wait_ge(s0_in, 16 * NH)
                pe.wait_ge(mask_done, 2 * TILES)
                for h in range(NH):
                    b0, r = 64 * (h % 2), h // 2
                    nc.tensor.matmul(opT[b0:b0 + 64, r, :], vn[:, ST, h * HD:(h + 1) * HD], sT[:, ST % 2, h % 2, r, :],
                                     start=True, stop=False)
                    for b in range(NB):
                        c = NP_TOK + b * NS
                        last = nc.tensor.matmul(opT[b0:b0 + 64, r, b * NS:(b + 1) * NS], s0[b0:b0 + 64, r, b, :],
                                                qT[b0:b0 + 64, r, c:c + NS], start=False, stop=(b == NB - 1))
                last.then_inc(oT_done, 1)
                pe.wait_ge(oev, PT)
                for h in range(NH):
                    b0, r = 64 * (h % 2), h // 2
                    pe.wait_ge(vb_done, h + 1)
                    if h % 2 == 0 and r >= 2:
                        pe.wait_ge(sn_out, r - 1)
                    last = nc.tensor.matmul(snew[r % 2][b0:b0 + 64].rearrange("p b e -> p (b e)"),
                                            kn[:, ST, h * HD:(h + 1) * HD],
                                            vbd[:, h % 2].rearrange("p b e -> p (b e)"), start=True, stop=True)
                    last.then_inc(sn_done, 1)
                pe.wait_ge(oTc, 1)
                pe.wait_ge(st_done, PT)
                for r in range(PAIRS):
                    last = nc.tensor.transpose(up_all[:, r * P:(r + 1) * P], oT[:, r, :], ident[:, :])
                last.then_inc(oTt, 1)

            @block.vector
            def _(dve):
                count = [0]

                def link(ins):
                    count[0] += 1
                    ins.then_inc(link_sem, 1)
                    dve.wait_ge(link_sem, count[0])

                def mask(t):
                    for half in range(2):
                        dve.wait_ge(sc_done, 2 * t + half + 1)
                        if t >= 2:
                            dve.wait_ge(o_done, t - 1)
                        nc.vector.tensor_tensor(sT[:, t % 2, half], sc[half][:, :, :],
                                                bc(causal[:, 0 if t < PT else 1, :].unsqueeze(1), [P, 4, P]),
                                                ALU.mult).then_inc(mask_done, 1)

                for t in range(PT):
                    mask(t)
                    dve.wait_ge(up_done, t + 1)
                    sd = bc(sdec[:, 0, :].unsqueeze(2), [P, PAIRS, HD])
                    if t == 0:
                        nc.vector.tensor_tensor(st, up, sd, ALU.mult).then_inc(st_done, 1)
                    else:
                        link(nc.vector.tensor_tensor(stt, up, st, ALU.add))
                        nc.vector.tensor_tensor(st, stt, sd, ALU.mult).then_inc(st_done, 1)
                    dve.wait_ge(st_done, t + 1)
                mask(ST)
                dve.wait_ge(s0_in, 16 * NH)

                def spread(h):
                    if h >= 2:
                        dve.wait_ge(sn_done, h - 1)
                    nc.vector.tensor_tensor(vbd[:, h % 2],
                                            bc(vn[:, ST, h * HD:(h + 1) * HD].unsqueeze(1), [P, NB, HD]),
                                            bc(bind[:, :].unsqueeze(2), [P, NB, HD]), ALU.mult).then_inc(vb_done, 1)

                for r in range(PAIRS):
                    spread(2 * r)
                    spread(2 * r + 1)
                    dve.wait_ge(sn_done, 2 * r + 2)
                    link(nc.vector.tensor_tensor(sadd[:, r], snew[r % 2], s0[:, r], ALU.add))
                    nc.vector.tensor_scalar(sadd[:, r], sadd[:, r], sdec[:, 1, r:r + 1], None,
                                            ALU.mult).then_inc(sn_out, 1)

            @block.scalar
            def _(act):
                for t in range(PT):
                    act.wait_ge(o_done, t + 1)
                    for par in range(2):
                        last = nc.scalar.copy(
                            mixo[:, t, 0:GW].rearrange("p (r q e) -> p q r e", q=2, e=HD)[:, par],
                            op[par][t % 2])
                    last.then_inc(oev, 1)
                act.wait_ge(oT_done, 1)
                nc.scalar.copy(oT, opT[:, :, :]).then_inc(oTc, 1)
                act.wait_ge(oTt, 1)
                nc.scalar.copy(mixo[:, ST, 0:GW], up_all[:, :])

        def phase_fox(block, sem, ps):
            cB = Hreg[:, 0:2 * NP_TOK].rearrange("p (s n) -> p s n", s=2)
            sN = Hreg[:, 2048:4096].rearrange("p (s n) -> p s n", s=2)
            pr = Hreg[:, 4096:6144].rearrange("p (s n) -> p s n", s=2)
            pT = Hreg[:, 6144:8192].rearrange("p (s j q) -> p s j q", s=2, j=8)
            ones = Hreg[:, 8192:9216]
            csum = Rreg[0:NH, 3 * quarter:3 * quarter + NP_TOK]
            e8 = Rreg[0:NH, 3 * quarter + 1024:3 * quarter + 2048].rearrange("p (h m) -> p h m", h=NH)
            e64 = Rreg[0:64, 3 * quarter + 2048:3 * quarter + 3072].rearrange("p (b m) -> p b m", b=NB)
            lfs = Rreg[0:64, 3 * quarter + 3072:3 * quarter + 3344]
            cs = Rreg[0:64, 3 * quarter + 3344:3 * quarter + 3616]
            mn = sb("mn", [P, 2, 3])
            ck = Wreg[:, 0:2048].rearrange("p (s j c) -> p s j c", s=2, j=2)
            cv = Wreg[:, 2048:4096].rearrange("p (s j c) -> p s j c", s=2, j=2)
            vnew = Wreg[0:NS, 4096:8192].rearrange("p (b c) -> p b c", b=NB)
            qbd = Xreg[:, 0:1024].rearrange("p (r b a q) -> p r b a q", r=PAIRS, b=NB, a=2)
            ckT = Xreg[:, 1024:3072].rearrange("p (s r n) -> p s r n", s=2, r=PAIRS) if False else \
                Xreg[:, 1024:2048].rearrange("p (r n) -> p r n", r=PAIRS)
            pn = Xreg[:, 2048:2048 + 272]
            pns = Xreg[:, 2320:2320 + 272]
            psT = Xreg[:, 2592:2592 + 384].rearrange("p (j m) -> p j m", j=3)
            foT = Xreg[:, 2976:2976 + 512].rearrange("p (r n) -> p r n", r=PAIRS)
            sp_ = [ps(f"s{i}", [P, NP_TOK]) for i in range(2)]
            tpp = ps("tpp", [P, 8, P])
            ov = ps("ov", [P, HD])
            cbp = ps("cbp", [P, 512])

            e_in, lf_in, vn_in = sem("e_in"), sem("lf_in"), sem("vn_in")
            ones_set, c_done, cs_done = sem("ones_set"), sem("c_done"), sem("cs_done")
            cb_mm, cb_ev = sem("cb_mm"), sem("cb_ev")
            s_done, ttr_done, exp_done, t_done = sem("s_done"), sem("ttr_done"), sem("exp_done"), sem("t_done")
            pta, ptb, pv_done, norm_done, rl_done = sem("pta"), sem("ptb"), sem("pv_done"), sem("norm_done"), sem("rl_done")
            kv_in = [sem(f"kv_in{i}") for i in range(2)]
            kv_used, qb_done, qz = sem("kv_used"), sem("qb_done"), sem("qz")
            kt_mm, kt_ev, ss_done, smin, sexp, spn = (sem(x) for x in ("kt_mm", "kt_ev", "ss_done", "smin", "sexp", "spn"))
            st_mm, st_ev, so_mm, so_ev, srl, fT_mm = (sem(x) for x in ("st_mm", "st_ev", "so_mm", "so_ev", "srl", "fT_mm"))
            NSTEP = NH * PT

            @block.sync
            def _(sp):
                sp.dma_start(e8, a["c_e8"]).then_inc(e_in, 16)
                sp.dma_start(e64, a["c_e64"]).then_inc(e_in, 16)
                sp.dma_start(lfs[:, 0:PAST], a["cache_lf_t"]).then_inc(lf_in, 16)
                for b in range(NB):
                    sp.dma_start(lfs[b * NH:(b + 1) * NH, PAST:PAST + NS],
                                 lgfT[:, NP_TOK + b * NS:NP_TOK + (b + 1) * NS]).then_inc(lf_in, 16)
                    sp.dma_start(vnew[:, b, :], vn[b * NS:(b + 1) * NS, ST, :]).then_inc(vn_in, 16)
                for b in range(NB):
                    if b >= 2:
                        sp.wait_ge(kv_used, b - 1)
                    sp.dma_start(ck[:, b % 2], a["cache_fox_k"][0, b].rearrange("(j p) h d -> p j (h d)", p=P)
                                 ).then_inc(kv_in[b % 2], 16)
                    sp.dma_start(cv[:, b % 2], a["cache_fox_v"][0, b].rearrange("(j p) h d -> p j (h d)", p=P)
                                 ).then_inc(kv_in[b % 2], 16)

            @block.tensor
            def _(pe):
                def decay_rows(h):
                    for half in range(2):
                        m = 2 * h + half
                        if m >= 1:
                            pe.wait_ge(cb_ev, m)
                        nc.tensor.matmul(cbp[:, :], e8[:, h, :], csum[:, 512 * half:512 * half + 512],
                                         start=True, stop=True).then_inc(cb_mm, 1)

                def scores(n):
                    h, i = n // PT, n % PT
                    b0, r = 64 * (h % 2), h // 2
                    if n >= 2:
                        pe.wait_ge(ttr_done, n - 1)
                    width = (i + 1) * P
                    for c in range(0, width, 512):
                        w = min(512, width - c)
                        final = c + w == width
                        nc.tensor.matmul(sp_[n % 2][:, c:c + w], qT[b0:b0 + 64, r, i * P:(i + 1) * P],
                                         kT[b0:b0 + 64, r, c:c + w], start=True, stop=not final)
                    nc.tensor.matmul(sp_[n % 2][:, i * P:width], identb[:, :], maskq[:, :],
                                     start=False, stop=True).then_inc(s_done, 1)

                def turn(n):
                    i = n % PT
                    pe.wait_ge(exp_done, n + 1)
                    for j in range(i + 1):
                        last = nc.tensor.transpose(tpp[:, j, :], pr[:, n % 2, j * P:(j + 1) * P], ident[:, :])
                    last.then_inc(t_done, 1)

                def values(n):
                    h, i = n // PT, n % PT
                    pe.wait_ge(pta, n + 1)
                    pe.wait_ge(ptb, 4 * h + max(0, i - 3))
                    if n >= 1:
                        pe.wait_ge(norm_done, n)
                    for j in range(i + 1):
                        last = nc.tensor.matmul(ov[:, :], pT[:, n % 2, j, :], vn[:, j, h * HD:(h + 1) * HD],
                                                start=(j == 0), stop=(j == i))
                    last.then_inc(pv_done, 1)

                pe.wait_ge(e_in, 32)
                pe.wait_ge(c_done, 1)
                decay_rows(0)
                for n in range(NSTEP + 2):
                    if n < NSTEP:
                        scores(n)
                        if n % PT == 4 and n // PT < NH - 1:
                            decay_rows(n // PT + 1)
                    if n >= 2:
                        values(n - 2)
                    if 1 <= n <= NSTEP:
                        turn(n - 1)
                pe.wait_ge(cs_done, 1)
                pe.wait_ge(qb_done, 2)
                pe.wait_ge(vn_in, 16 * NB)
                kTp = sp_[0][:, :].rearrange("p (r n) -> p r n", r=PAIRS)
                pe.wait_ge(ttr_done, NSTEP)
                for b in range(NB):
                    pe.wait_ge(kv_in[b % 2], 32 * (b // 2 + 1))
                    if b >= 1:
                        pe.wait_ge(kt_ev, b)
                    for r in range(PAIRS):
                        for j in range(2):
                            last = nc.tensor.transpose(kTp[:, r, j * P:(j + 1) * P], ck[:, b % 2, j, r * P:(r + 1) * P],
                                                       ident[:, :])
                    last.then_inc(kt_mm, 1)
                    S = sp_[1][:, 0:272]
                    if b >= 1:
                        pe.wait_ge(sexp, b)
                    nc.tensor.matmul(S, e64[:, b, :], cs, start=True, stop=False, skip_group_check=True)
                    nc.tensor.matmul(S[:, PAST:PAST + NS], identb[:, :], maskn[:, :], start=False, stop=False,
                                     skip_group_check=True)
                    pe.wait_ge(kt_ev, b + 1)
                    for r in range(PAIRS):
                        o = 32 * r
                        lhs = qbd[:, r, b].rearrange("p a q -> p (a q)")
                        nc.tensor.matmul(S[o:o + 32, 0:PAST], lhs, ckT[:, r, :], start=False, stop=False,
                                         skip_group_check=True)
                        last = nc.tensor.matmul(S[o:o + 32, PAST:PAST + NS], lhs,
                                                kT[:, r, NP_TOK + b * NS:NP_TOK + (b + 1) * NS],
                                                start=False, stop=True, skip_group_check=True)
                    last.then_inc(ss_done, 1)
                    pe.wait_ge(spn, b + 1)
                    if b >= 1:
                        pe.wait_ge(st_ev, 2 * b)
                    for j in range(2):
                        nc.tensor.transpose(tpp[:, j, :], pns[:, j * P:(j + 1) * P], ident[:, :])
                    nc.tensor.transpose(tpp[0:NS, 2, :], pns[:, PAST:PAST + NS], ident[:, :]).then_inc(st_mm, 1)
                    pe.wait_ge(st_ev, 2 * b + 2)
                    if b >= 1:
                        pe.wait_ge(so_ev, 2 * b)
                    for r in range(PAIRS):
                        o = cbp[:, 32 * r:32 * r + 32]
                        for j in range(2):
                            nc.tensor.matmul(o, cv[:, b % 2, j, r * P:(r + 1) * P], psT[:, j, 32 * r:32 * r + 32],
                                             start=(j == 0), stop=False)
                        last = nc.tensor.matmul(o, vnew[:, b, r * P:(r + 1) * P], psT[0:NS, 2, 32 * r:32 * r + 32],
                                                start=False, stop=True)
                    last.then_inc(so_mm, 1)
                    pe.wait_ge(so_mm, b + 1)
                    pe.sem_inc(kv_used, 1)
                pe.wait_ge(so_ev, 2 * NB)
                for r in range(PAIRS):
                    last = nc.tensor.transpose(tpp[:, r, :], foT[:, r, :], ident[:, :])
                last.then_inc(fT_mm, 1)

            @block.scalar
            def _(act):
                def rows(m):
                    act.wait_ge(cb_mm, m + 1)
                    h, half = m // 2, m % 2
                    if h >= 2:
                        act.wait_ge(ttr_done, PT * (h - 1))
                    nc.scalar.copy(cB[:, h % 2, 512 * half:512 * half + 512], cbp[:, :]).then_inc(cb_ev, 1)

                act.wait_ge(lf_in, 16 * (NB + 1))
                rows(0)
                rows(1)
                for n in range(NSTEP + 1):
                    if n < NSTEP:
                        w = (n % PT + 1) * P
                        act.wait_ge(ttr_done, n + 1)
                        if n >= 2:
                            act.wait_ge(t_done, n - 1)
                            act.wait_ge(rl_done, n - 1)
                        nc.scalar.activation(pr[:, n % 2, 0:w], sN[:, n % 2, 0:w], ACT.Exp, bias=mn[:, n % 2, 0:1],
                                             scale=-1.0, accum_out=mn[:, n % 2, 1:2]).then_inc(exp_done, 1)
                    if n < NSTEP and n % PT == 4 and n // PT < NH - 1:
                        rows(2 * (n // PT) + 2)
                        rows(2 * (n // PT) + 3)
                    if n >= 1:
                        act.wait_ge(t_done, n)
                        j = min(4, (n - 1) % PT + 1)
                        if n >= 3:
                            act.wait_ge(pv_done, n - 2)
                        nc.scalar.copy(pT[:, (n - 1) % 2, 0:j, :], tpp[:, 0:j, :]).then_inc(pta, 1)
                for b in range(NB):
                    act.wait_ge(kt_mm, b + 1)
                    if b >= 1:
                        act.wait_ge(ss_done, b)
                    nc.scalar.copy(ckT, sp_[0][:, :].rearrange("p (r n) -> p r n", r=PAIRS)).then_inc(kt_ev, 1)
                    act.wait_ge(smin, b + 1)
                    if b >= 1:
                        act.wait_ge(spn, b)
                    nc.scalar.activation(pn, sp_[1][:, 0:272], ACT.Exp, bias=mn[:, 0, 0:1], scale=-1.0,
                                         accum_out=mn[:, 0, 1:2]).then_inc(sexp, 1)
                    act.wait_ge(st_mm, b + 1)
                    if b >= 1:
                        act.wait_ge(so_mm, b)
                    nc.scalar.copy(psT[:, 0:2, :], tpp[:, 0:2, :]).then_inc(st_ev, 1)
                    nc.scalar.copy(psT[0:NS, 2, :], tpp[0:NS, 2, :]).then_inc(st_ev, 1)
                act.wait_ge(fT_mm, 1)
                nc.scalar.copy(mixo[:, ST, GW:], tpp[:, 0:4, :].rearrange("p r e -> p (r e)"))

            @block.gpsimd
            def _(pool):
                nc.gpsimd.memset(ones, 1.0).then_inc(ones_set, 1)
                nc.gpsimd.memset(Xreg[:, 0:1024], 0.0).then_inc(qz, 1)

            @block.vector
            def _(dve):
                dve.wait_ge(ones_set, 1)
                nc.vector.tensor_tensor_scan(out=csum, data0=ones[0:NH, :], data1=lgfT[:, 0:NP_TOK],
                                             initial=0.0, op0=ALU.mult, op1=ALU.add).then_inc(c_done, 1)
                dve.wait_ge(lf_in, 16 * (NB + 1))
                nc.vector.tensor_tensor_scan(out=cs, data0=ones[0:64, 0:272], data1=lfs,
                                             initial=0.0, op0=ALU.mult, op1=ALU.add).then_inc(cs_done, 1)
                dve.wait_ge(qz, 1)
                for par in range(2):
                    o = 64 * par
                    nc.vector.tensor_copy(qbd[o:o + 64, :, :, par, :].rearrange("p r b q -> p (r b) q"),
                                          qT[o:o + 64, :, NP_TOK:].rearrange("p r (b q) -> p r b q", q=NS)
                                          ).then_inc(qb_done, 1) if False else \
                        [nc.vector.tensor_copy(qbd[o:o + 64, r, :, par, :],
                                               qT[o:o + 64, r, NP_TOK:].rearrange("p (b q) -> p b q", q=NS))
                         for r in range(PAIRS)][-1].then_inc(qb_done, 1)

                for n in range(NSTEP + 2):
                    if n < NSTEP:
                        h, w = n // PT, (n % PT + 1) * P
                        if n % PT == 0:
                            dve.wait_ge(cb_ev, 2 * h + 2)
                        dve.wait_ge(s_done, n + 1)
                        if n >= 2:
                            dve.wait_ge(exp_done, n - 1)
                        nc.vector.tensor_tensor_reduce(out=sN[:, n % 2, 0:w], in0=sp_[n % 2][:, 0:w],
                                                       in1=cB[:, h % 2, 0:w], scale=1.0, scalar=3e38,
                                                       op0=ALU.add, op1=ALU.min,
                                                       accum_out=mn[:, n % 2, 0:1]).then_inc(ttr_done, 1)
                    if 1 <= n <= NSTEP:
                        m = n - 1
                        dve.wait_ge(exp_done, m + 1)
                        if m >= 2:
                            dve.wait_ge(norm_done, m - 1)
                        nc.vector.reciprocal(mn[:, m % 2, 2:3], mn[:, m % 2, 1:2]).then_inc(rl_done, 1)
                        if m % PT >= 4:
                            j = m % PT + 1
                            dve.wait_ge(t_done, m + 1)
                            if m >= 2:
                                dve.wait_ge(pv_done, m - 1)
                            nc.vector.tensor_copy(pT[:, m % 2, 4:j, :], tpp[:, 4:j, :]).then_inc(ptb, 1)
                    if n >= 2:
                        m = n - 2
                        h, i = m // PT, m % PT
                        dve.wait_ge(pv_done, m + 1)
                        dve.wait_ge(rl_done, m + 1)
                        nc.vector.tensor_scalar(mixo[:, i, GW + h * HD:GW + (h + 1) * HD], ov[:, :],
                                                mn[:, m % 2, 2:3], None, ALU.mult).then_inc(norm_done, 1)
                for b in range(NB):
                    dve.wait_ge(ss_done, b + 1)
                    nc.vector.tensor_reduce(mn[:, 0, 0:1], sp_[1][:, 0:272], AX.X, ALU.min).then_inc(smin, 1)
                    dve.wait_ge(sexp, b + 1)
                    nc.vector.reciprocal(mn[:, 0, 2:3], mn[:, 0, 1:2]).then_inc(srl, 1)
                    dve.wait_ge(srl, b + 1)
                    if b >= 1:
                        dve.wait_ge(st_mm, b)
                    nc.vector.tensor_scalar(pns, pn, mn[:, 0, 2:3], None, ALU.mult).then_inc(spn, 1)
                    dve.wait_ge(so_mm, b + 1)
                    for par in range(2):
                        o = 64 * par
                        nc.vector.tensor_copy(foT[o:o + 64, :, b * NS:(b + 1) * NS],
                                              cbp[o:o + 64, 0:P].rearrange("p (r a q) -> p r a q", r=PAIRS, a=2)
                                              [:, :, par, :]).then_inc(so_ev, 1)

        wout = Wreg[:, :].rearrange("p (k c) -> p k c", k=KC)
        NSEG = 2 * PH
        wq = Rreg[:, 0:KC * 2048].rearrange("p (k c) -> p k c", k=KC)
        keysT = Rreg[:, 16384:18432].rearrange("p (s n) -> p s n", s=NSEG)

        def phase_out(block, sem, ps):
            mixs = [Hreg[:, i * D:(i + 1) * D] for i in range(2)]
            xt = [Hreg[:, (2 + i) * D:(3 + i) * D] for i in range(2)]
            mT = [Hreg[:, (4 + i) * D:(5 + i) * D].rearrange("p (k n) -> p k n", k=KC) for i in range(2)]
            sq = Hreg[:, 6 * D:7 * D].rearrange("p (s c) -> p s c", s=2)
            xn = [Hreg[:, (7 + i) * D:(8 + i) * D] for i in range(2)]
            tp = ps("otp", [P, 8, P])
            yp = [ps(f"oyp{i}", [P, D]) for i in range(2)]
            w_in, x_in, wq_in = sem("w_in"), [sem("x_in0"), sem("x_in1")], sem("wq_in")
            sq_done, ss_done, rs_done, mix_done = sem("sq_done"), sem("ss_done"), sem("rs_done"), sem("mix_done")
            t_mm, ev_a, ev_v, y_mm, x1_done = sem("t_mm"), sem("ev_a"), sem("ev_v"), sem("y_mm"), sem("x1_done")
            x1_out, pstep, vlink = [sem("x1_out0"), sem("x1_out1")], sem("pstep"), sem("vlink")
            g2_in, xsq, xrs, xn_done = sem("g2_in"), sem("xsq"), sem("xrs"), sem("xn_done")
            xn_out = [sem("xn_out0"), sem("xn_out1")]

            @block.sync
            def _(sp):
                sp.dma_start(wout, a["w_out"][0].rearrange("(k p) c -> p k c", p=P)).then_inc(w_in, 16)
                for t in range(2):
                    sp.dma_start(xt[t], a["x_prompt"][0, t * P:(t + 1) * P, :]).then_inc(x_in[t], 16)
                sp.dma_start(grow[:, :], a["norm2_g"].partition_broadcast(P)
                             .rearrange("p a c -> p (a c)")).then_inc(g2_in, 16)
                for k in range(KC):
                    sp.dma_start(wq[:, k, :], a["peer_wq"][0, k * P:(k + 1) * P, :]).then_inc(wq_in, 16)
                sp.dma_start(keysT, a["keys_t"]).then_inc(wq_in, 16)
                for t in range(TILES):
                    sp.wait_ge(x1_done, t + 1)
                    sp.dma_start(a["x1"][t], xt[t % 2]).then_inc(x1_out[t % 2], 16)
                    sp.wait_ge(xn_done, t + 1)
                    sp.dma_start(a["xn"][t], xn[t % 2]).then_inc(xn_out[t % 2], 16)
                    if t + 2 < TILES:
                        sp.wait_ge(x1_out[t % 2], 16 * (t // 2 + 1))
                        src = a["x_prompt"][0, (t + 2) * P:(t + 3) * P, :] if t + 2 < PT else \
                            a["x_sample"].rearrange("b t d -> (b t) d")
                        sp.dma_start(xt[t % 2], src).then_inc(x_in[t % 2], 16)
                sp.wait_ge(wq_in, 16 * (KC + 1))
                sp.wait_ge(xn_out[0], 16 * 5)
                sp.wait_ge(xn_out[1], 16 * 4)
                sp.wait_ge(x1_out[0], 16 * 5)
                sp.wait_ge(x1_out[1], 16 * 4)

            @block.scalar
            def _(act):
                def square(t):
                    act.wait_ge(x1_done, t + 1)
                    if t >= 2:
                        act.wait_ge(xn_out[t % 2], 16 * (t // 2))
                    if t >= 1:
                        act.wait_ge(xrs, t)
                    nc.scalar.activation(xn[t % 2], xt[t % 2], ACT.Square, accum_out=small[:, 48:49]).then_inc(xsq, 1)

                for t in range(TILES + 1):
                    if t < TILES:
                        if t >= 2:
                            act.wait_ge(ss_done, t - 1)
                        nc.scalar.activation(sq[:, t % 2, :], mixo[:, t, GW:], ACT.Square).then_inc(sq_done, 1)
                    if t >= 1:
                        act.wait_ge(t_mm, t)
                        if t >= 3:
                            act.wait_ge(y_mm, t - 2)
                        nc.scalar.copy(mT[(t - 1) % 2][:, 0:4, :], tp[:, 0:4, :]).then_inc(ev_a, 1)
                    if t >= 2:
                        square(t - 2)
                square(TILES - 1)

            @block.gpsimd
            def _(pool):
                steps_done = [0]

                def rsqrt(out, tmp, ssq, scale, half, done):
                    nc.gpsimd.tensor_scalar(tmp, ssq, scale, EPS, ALU.mult, ALU.add).then_inc(pstep, 1)
                    steps_done[0] += 1
                    pool.wait_ge(pstep, steps_done[0])
                    nc.gpsimd.tensor_tensor(out, tmp, half, ALU.pow).then_inc(done, 1)

                for t in range(TILES + 2):
                    if t < TILES:
                        o = 8 * (t % 2)
                        pool.wait_ge(ss_done, t + 1)
                        rsqrt(small[:, 32 + o:40 + o], small[:, 16 + o:24 + o], small[:, o:o + 8], 1.0 / HD,
                              nhalf[:, :], rs_done)
                    if t >= 2:
                        pool.wait_ge(xsq, t - 1)
                        rsqrt(small[:, 52:53], small[:, 50:51], small[:, 48:49], 1.0 / D, nhalf[:, 0:1], xrs)

            @block.vector
            def _(dve):
                def heads(ap):
                    return ap.rearrange("p (h d) -> p h d", h=NH)

                for t in range(TILES + 2):
                    if t < TILES:
                        o = 8 * (t % 2)
                        dve.wait_ge(sq_done, t + 1)
                        nc.vector.tensor_reduce(small[:, o:o + 8], heads(sq[:, t % 2, :]), AX.X,
                                                ALU.add).then_inc(ss_done, 1)
                        if t >= 2:
                            dve.wait_ge(t_mm, t - 1)
                        nc.vector.tensor_copy(mixs[t % 2][:, 0:GW], mixo[:, t, 0:GW])
                        dve.wait_ge(rs_done, t + 1)
                        nc.vector.tensor_tensor(heads(mixs[t % 2][:, GW:]), heads(mixo[:, t, GW:]),
                                                bc(small[:, 32 + o:40 + o].unsqueeze(2), [P, NH, HD]),
                                                ALU.mult).then_inc(vlink, 1)
                        dve.wait_ge(vlink, t + 1)
                        nc.vector.tensor_tensor(mixs[t % 2][:, GW:], mixs[t % 2][:, GW:], gain_fox[:, :],
                                                ALU.mult).then_inc(mix_done, 1)
                    if 1 <= t <= TILES:
                        dve.wait_ge(t_mm, t)
                        if t >= 3:
                            dve.wait_ge(y_mm, t - 2)
                        nc.vector.tensor_copy(mT[(t - 1) % 2][:, 4:8, :], tp[:, 4:8, :]).then_inc(ev_v, 1)
                    if t >= 2:
                        m = t - 2
                        dve.wait_ge(y_mm, m + 1)
                        dve.wait_ge(x_in[m % 2], 16 * (m // 2 + 1))
                        nc.vector.tensor_tensor(xt[m % 2], yp[m % 2][:, :], xt[m % 2], ALU.add).then_inc(x1_done, 1)
                        dve.wait_ge(xrs, m + 1)
                        if m == 0:
                            dve.wait_ge(g2_in, 16)
                        nc.vector.scalar_tensor_tensor(out=xn[m % 2], in0=xt[m % 2], scalar=small[:, 52:53],
                                                       in1=grow[:, :], op0=ALU.mult, op1=ALU.mult).then_inc(xn_done, 1)

            @block.tensor
            def _(pe):
                def turn(t):
                    pe.wait_ge(mix_done, t + 1)
                    if t >= 1:
                        pe.wait_ge(ev_a, t)
                        pe.wait_ge(ev_v, t)
                    for k in range(KC):
                        last = nc.tensor.transpose(tp[:, k, :], mixs[t % 2][:, k * P:(k + 1) * P], ident[:, :])
                    last.then_inc(t_mm, 1)

                turn(0)
                pe.wait_ge(w_in, 16)
                for t in range(TILES):
                    pe.wait_ge(ev_a, t + 1)
                    pe.wait_ge(ev_v, t + 1)
                    if t + 1 < TILES:
                        turn(t + 1)
                    if t >= 2:
                        pe.wait_ge(x1_done, t - 1)
                    for c in range(2):
                        for k in range(KC):
                            last = nc.tensor.matmul(yp[t % 2][:, 512 * c:512 * c + 512], mT[t % 2][:, k, :],
                                                    wout[:, k, 512 * c:512 * c + 512],
                                                    start=(k == 0), stop=(k == KC - 1))
                    last.then_inc(y_mm, 1)

        def phase_peer(block, sem, ps):
            NU = NV = 8
            NI, ND = 4, 4
            xns, xcur, xb = (Hreg[:, i * D:(i + 1) * D] for i in (0, 1, 3))
            xT = Hreg[:, 4096:5120].rearrange("p (k n) -> p k n", k=KC)
            qTs = Hreg[:, 5120:7168].rearrange("p (s n) -> p s n", s=NSEG)
            sc = Hreg[:, 7168:9216].rearrange("p (s n) -> p s n", s=NSEG)
            sc2 = qTs
            mflat = mixo[:, :, :].rearrange("p t c -> p (t c)")
            vb = mflat[:, 0:NV * D].rearrange("p (s d) -> p s d", s=NV)
            junk = mflat[:, NV * D:(NV + 1) * D]
            ub = Wreg[:, 0:NU * D].rearrange("p (s d) -> p s d", s=NU)
            idx2 = Xreg[:, 0:2 * P].bitcast(I32)
            gate2 = Xreg[:, 2 * P:4 * P]
            X0 = 4 * P
            vals = Xreg[:, X0:X0 + 256].rearrange("p (s n) -> p s n", s=NSEG)
            idx = Xreg[:, X0 + 256:X0 + 512].bitcast(U32).rearrange("p (s n) -> p s n", s=NSEG)
            fidx = Xreg[:, X0 + 512:X0 + 768].rearrange("p (s n) -> p s n", s=NSEG)
            cval = Xreg[:, X0 + 768:X0 + 896].rearrange("p (h n) -> p h n", h=PH)
            ci = Xreg[:, X0 + 896:X0 + 1024].bitcast(U32).rearrange("p (h n) -> p h n", h=PH)
            cia = Xreg[:, X0 + 1024:X0 + 1152].bitcast(U32)
            cif = Xreg[:, X0 + 1152:X0 + 1408].rearrange("p (a n) -> p a n", a=2)
            sel = Xreg[:, X0 + 1408:X0 + 1664].rearrange("p (a n) -> p a n", a=2)
            ef = Xreg[:, X0 + 1664:X0 + 1792].rearrange("p (h n) -> p h n", h=PH)
            ssum = Xreg[:, X0 + 1792:X0 + 1808]
            cand = Xreg[:, X0 + 1808:X0 + 3856].rearrange("p (h n) -> p h n", h=PH)
            islot = sb("islot", [P, NI, TOPK], I32)
            dots, gw = sb("dots", [P, 2, TOPK]), sb("gw", [P, 2, TOPK])
            g1, g2 = sb("g1", [P, TOPK]), sb("g2", [P, TOPK])
            diag = sb("diag", [P, ND, P])
            tp = ps("btp", [P, 8, P])
            qp = [ps(f"qp{i}", [P, 4, P]) for i in range(2)]
            spp = [ps(f"spp{i}", [P, 4, P]) for i in range(2)] + qp
            yp = ps("yp", [P, D])

            u_in = [sem(f"u_in{i}") for i in range(NU)]
            v_in = [sem(f"v_in{i}") for i in range(NV)]
            u_used, v_used, idx_done = sem("u_used"), sem("v_used"), sem("idx_done")
            gel1, gel2, gw_done, diag_done, elink = (sem(x) for x in ("gel1", "gel2", "gw_done", "diag_done", "elink"))
            xcopy, y_out, xb_in, out_done = sem("xcopy"), sem("y_out"), sem("xb_in"), sem("out_done")
            names = ("xn_in", "xt_mm", "xt_ev", "q_mm", "q_ev", "s_mm", "s_ev",
                     "csub", "gexp", "rlink", "route_done")
            R = {n: sem("r_" + n) for n in names}
            RLINKS, ELINKS = 22, 6
            u_tab, v_tab = a["peer_u"][0], a["peer_v"][0]

            def turns(engine, first, inner, last):
                first(0)
                with engine.Fori(1, TILES - 1) as t:
                    inner(t)
                last(TILES - 1)

            def wait(engine, semaphore, value):
                if isinstance(value, int):
                    engine.wait_ge(semaphore, value)
                else:
                    after(engine, semaphore, value)

            @block.sync
            def _(sp):
                def load_route(t):
                    wait(sp, R["xt_mm"], t)
                    wait(sp, xcopy, t)
                    sp.dma_start(xns, a["xn"][bass.ds(t, 1)].rearrange("a p d -> (a p) d")).then_inc(R["xn_in"], 16)

                def store(t):
                    wait(sp, y_out, t + 1)
                    dst = a["y_sample"].rearrange("b t d -> (b t) d") if isinstance(t, int) and t == ST else \
                        a["y_prompt"][0, bass.ds(t * P, P), :]
                    sp.dma_start(dst, xb).then_inc(out_done, 16)
                    wait(sp, out_done, 16 * t + 16)

                def load_final(t):
                    sp.dma_start(xb, a["x1"][bass.ds(t, 1)].rearrange("a p d -> (a p) d")).then_inc(xb_in, 16)

                sp.dma_start(xns, a["xn"][0]).then_inc(R["xn_in"], 16)
                sp.dma_start(xb, a["x1"][0]).then_inc(xb_in, 16)

                def turn0(t):
                    load_route(t + 1)

                def turn(t):
                    load_route(t + 1)
                    store(t - 1)
                    load_final(t)

                def turn_last(t):
                    store(t - 1)
                    load_final(t)
                    store(t)

                turns(sp, turn0, turn, turn_last)

            @block.gpsimd
            def _(pool):
                def load_numbers(t, h):
                    g = t * PH + h
                    if h == 0:
                        wait(pool, R["route_done"], t + 1)
                    if not (isinstance(g, int) and g < NI):
                        wait(pool, v_used, (g - NI + 1) * TOPK)
                    nc.gpsimd.tensor_copy(islot[:, h % NI, :],
                                          idx2[:, bass.ds((t % 2) * P + h * TOPK, TOPK)]).then_inc(idx_done, 1)
                    wait(pool, idx_done, g + 1)

                def gather_u(t, h, i):
                    g = t * PH + h
                    if not (isinstance(g, int) and g == 0 and i < NU):
                        wait(pool, u_used, g * TOPK + i - NU + 1)
                    nc.gpsimd.indirect_dma_start(
                        ub[:, i % NU, :], None, u_tab,
                        bass.IndirectOffsetOnAxis(ap=islot[:, h % NI, i:i + 1], axis=0)).then_inc(u_in[i % NU], 16)

                def gather_v(t, h, i):
                    g = t * PH + h
                    if not (isinstance(g, int) and g == 0 and i < NV):
                        wait(pool, v_used, g * TOPK + i - NV + 1)
                    nc.gpsimd.indirect_dma_start(
                        vb[:, i % NV, :], None, v_tab,
                        bass.IndirectOffsetOnAxis(ap=islot[:, h % NI, i:i + 1], axis=0)).then_inc(v_in[i % NV], 16)

                def turn(t, first=False, last=False):
                    for h in range(PH):
                        load_numbers(t, h)
                        for i in range(TOPK):
                            gather_u(t, h, i)
                            if h:
                                gather_v(t, h - 1, i)
                            elif not first:
                                gather_v(t - 1, PH - 1, i)

                turns(pool, lambda t: turn(t, first=True), turn, turn)
                for i in range(TOPK):
                    gather_v(TILES - 1, PH - 1, i)

            @block.scalar
            def _(act):
                def evacuate_x(t):
                    wait(act, R["xt_mm"], t + 1)
                    nc.scalar.copy(xT[:, 0:4, :], tp[:, 0:4, :])
                    nc.scalar.copy(xT[:, 4:8, :], tp[:, 4:8, :]).then_inc(R["xt_ev"], 1)

                def evacuate_q(t, b):
                    wait(act, R["q_mm"], 4 * t + b + 1)
                    nc.scalar.copy(qTs[:, 4 * b:4 * b + 4, :], qp[b % 2][:, :, :]).then_inc(R["q_ev"], 1)

                def evacuate_s(t, b):
                    wait(act, R["s_mm"], 4 * t + b + 1)
                    nc.scalar.copy(sc[:, 4 * b:4 * b + 4, :], spp[b][:, :, :]).then_inc(R["s_ev"], 1)

                def gate_exp(t):
                    wait(act, R["csub"], t + 1)
                    nc.scalar.activation(ef, ef, ACT.Exp).then_inc(R["gexp"], 1)

                def gelu_exp(t, h):
                    wait(act, gel1, t * PH + h + 1)
                    nc.scalar.activation(g2[:, :], g1[:, :], ACT.Exp, scale=-1.0).then_inc(gel2, 1)

                def diagonals(t, h):
                    g = t * PH + h
                    wait(act, gw_done, g + 1)
                    for i in range(TOPK):
                        if not (isinstance(g, int) and g == 0 and i < ND):
                            wait(act, v_used, g * TOPK + i - ND + 1)
                        nc.scalar.activation(diag[:, i % ND, :], ident[:, :], ACT.Copy,
                                             scale=gw[:, h % 2, i:i + 1]).then_inc(diag_done, 1)

                def turn(t, first=False, last=False):
                    for h in range(PH):
                        if h:
                            diagonals(t, h - 1)
                        elif not first:
                            diagonals(t - 1, PH - 1)
                        gelu_exp(t, h)
                        if not last:
                            if h == 0:
                                evacuate_x(t + 1)
                            elif h in (1, 2):
                                evacuate_q(t + 1, 2 * h - 2)
                                evacuate_q(t + 1, 2 * h - 1)
                            elif h == 3:
                                for b in range(4):
                                    evacuate_s(t + 1, b)
                            elif h == 6:
                                gate_exp(t + 1)

                evacuate_x(0)
                for b in range(4):
                    evacuate_q(0, b)
                for b in range(4):
                    evacuate_s(0, b)
                gate_exp(0)
                turns(act, lambda t: turn(t, first=True), turn, lambda t: turn(t, last=True))
                diagonals(TILES - 1, PH - 1)

            @block.tensor
            def _(pe):
                def turn_x(t):
                    pe.wait_ge(R["xn_in"], 16 * t + 16)
                    for k in range(KC):
                        last = nc.tensor.transpose(tp[:, k, :], xns[:, k * P:(k + 1) * P], ident[:, :])
                    last.then_inc(R["xt_mm"], 1)

                def queries(t, b):
                    if b == 0:
                        pe.wait_ge(R["xt_ev"], t + 1)
                    if b >= 2:
                        pe.wait_ge(R["q_ev"], 4 * t + b - 1)
                    elif not (isinstance(t, int) and t == 0):
                        pe.wait_ge(R["s_ev"], 4 * t)
                    for i in range(4):
                        s = 4 * b + i
                        for k in range(KC):
                            last = nc.tensor.matmul(qp[b % 2][:, i, :], wq[:, k, s * P:(s + 1) * P], xT[:, k, :],
                                                    start=(k == 0), stop=(k == KC - 1))
                    last.then_inc(R["q_mm"], 1)

                def key_scores(t):
                    for b in range(4):
                        pe.wait_ge(R["q_ev"], 4 * t + b + 1)
                        for i in range(4):
                            s = 4 * b + i
                            last = nc.tensor.matmul(spp[b][:, i, :], qTs[:, s, :], keysT[:, s, :],
                                                    start=True, stop=True)
                        last.then_inc(R["s_mm"], 1)

                def add_v(t, h):
                    g = t * PH + h
                    if h == 0 and not (isinstance(t, int) and t == 0):
                        pe.wait_ge(y_out, t)
                    for i in range(TOPK):
                        pe.wait_ge(v_in[i % NV], 32 * g + 16 * (i // NV) + 16)
                        pe.wait_ge(diag_done, g * TOPK + i + 1)
                        for c in range(2):
                            last = nc.tensor.matmul(yp[:, 512 * c:512 * c + 512], diag[:, i % ND, :],
                                                    vb[:, i % NV, 512 * c:512 * c + 512],
                                                    start=(h == 0 and i == 0), stop=(h == PH - 1 and i == TOPK - 1))
                        last.then_inc(v_used, 1)

                def turn(t, first=False, last=False):
                    for h in range(PH):
                        if h:
                            add_v(t, h - 1)
                        elif not first:
                            add_v(t - 1, PH - 1)
                        if not last:
                            if h == 0:
                                turn_x(t + 1)
                            elif h in (1, 2):
                                queries(t + 1, 2 * h - 2)
                                queries(t + 1, 2 * h - 1)
                            elif h == 3:
                                key_scores(t + 1)

                turn_x(0)
                for b in range(4):
                    queries(0, b)
                key_scores(0)
                turns(pe, lambda t: turn(t, first=True), turn, lambda t: turn(t, last=True))
                add_v(TILES - 1, PH - 1)

            @block.vector
            def _(dve):
                def dot(t, h, between):
                    g = t * PH + h
                    for i in range(TOPK):
                        if i in between:
                            between[i]()
                        wait(dve, u_in[i % NU], 32 * g + 16 * (i // NU) + 16)
                        nc.vector.scalar_tensor_tensor(out=junk, in0=ub[:, i % NU, :], scalar=1.0, in1=xcur,
                                                       op0=ALU.mult, op1=ALU.mult,
                                                       accum_out=dots[:, h % 2, i:i + 1]).then_inc(u_used, 1)
                        wait(dve, u_used, g * TOPK + i + 1)

                def weights(t, h):
                    g = t * PH + h
                    x = dots[:, h % 2, :]
                    k = [0]

                    def link(ins):
                        k[0] += 1
                        ins.then_inc(elink, 1)
                        wait(dve, elink, ELINKS * g + k[0])

                    link(nc.vector.tensor_tensor(g1[:, :], x, x, ALU.mult))
                    link(nc.vector.tensor_scalar(g1[:, :], g1[:, :], GELU_C * 0.044715, GELU_C, ALU.mult, ALU.add))
                    link(nc.vector.tensor_tensor(g1[:, :], g1[:, :], x, ALU.mult))
                    nc.vector.tensor_scalar_max(g1[:, :], g1[:, :], -80.0).then_inc(gel1, 1)
                    wait(dve, gel2, g + 1)
                    link(nc.vector.tensor_scalar_add(g1[:, :], g2[:, :], 1.0))
                    link(nc.vector.reciprocal(g1[:, :], g1[:, :]))
                    link(nc.vector.tensor_tensor(g1[:, :], g1[:, :], x, ALU.mult))
                    if not (isinstance(g, int) and g < 2):
                        wait(dve, diag_done, (g - 1) * TOPK)
                    nc.vector.tensor_tensor(gw[:, h % 2, :], g1[:, :],
                                            gate2[:, bass.ds((t % 2) * P + h * TOPK, TOPK)],
                                            ALU.mult).then_inc(gw_done, 1)
                    assert k[0] == ELINKS

                def finish(t):
                    wait(dve, v_used, (t + 1) * P)
                    wait(dve, xb_in, 16 * t + 16)
                    nc.vector.tensor_tensor(xb, yp[:, :], xb, ALU.add).then_inc(y_out, 1)

                rcount = [0]

                def rlink(t, ins):
                    rcount[0] += 1
                    ins.then_inc(R["rlink"], 1)
                    wait(dve, R["rlink"], RLINKS * t + rcount[0])

                def keep_x(t):
                    wait(dve, R["xn_in"], 16 * t + 16)
                    nc.vector.tensor_copy(xcur, xns).then_inc(xcopy, 1)
                    wait(dve, xcopy, t + 1)

                def top_keys(t, part):
                    if part == 0:
                        wait(dve, R["s_ev"], 4 * t + 4)
                        for s in range(NSEG):
                            last = nc.vector.max(vals[:, s, 0:8], sc[:, s, :])
                        rlink(t, last)
                        for s in range(NSEG):
                            nc.vector.max_index(idx[:, s, 0:8], vals[:, s, 0:8], sc[:, s, :])
                            last = nc.vector.match_replace(sc2[:, s, :], vals[:, s, 0:8], sc[:, s, :], -3e38)
                        rlink(t, last)
                    else:
                        for s in range(NSEG):
                            last = nc.vector.max(vals[:, s, 8:16], sc2[:, s, :])
                        rlink(t, last)
                        for s in range(NSEG):
                            last = nc.vector.max_index(idx[:, s, 8:16], vals[:, s, 8:16], sc2[:, s, :])
                        rlink(t, last)

                def top_sums(t, part):
                    cand2 = sc2.rearrange("p (h a) n -> p h (a n)", a=2)
                    if part == 0:
                        v4 = vals.rearrange("p (h a) n -> p h a n", a=2)
                        nc.vector.tensor_copy(fidx, idx)
                        rlink(t, nc.vector.tensor_tensor(cand.rearrange("p h (i j) -> p h i j", i=TOPK),
                                                         bc(v4[:, :, 0, :].unsqueeze(3), [P, PH, TOPK, TOPK]),
                                                         bc(v4[:, :, 1, :].unsqueeze(2), [P, PH, TOPK, TOPK]),
                                                         ALU.add))
                        for h in range(PH):
                            last = nc.vector.max(cval[:, h, 0:8], cand[:, h, :])
                        rlink(t, last)
                    elif part == 1:
                        for h in range(PH):
                            nc.vector.max_index(ci[:, h, 0:8], cval[:, h, 0:8], cand[:, h, :])
                            last = nc.vector.match_replace(cand2[:, h, :], cval[:, h, 0:8], cand[:, h, :], -3e38)
                        rlink(t, last)
                        for h in range(PH):
                            last = nc.vector.max(cval[:, h, 8:16], cand2[:, h, :])
                        rlink(t, last)
                    else:
                        for h in range(PH):
                            last = nc.vector.max_index(ci[:, h, 8:16], cval[:, h, 8:16], cand2[:, h, :])
                        rlink(t, last)
                        cflat = ci.rearrange("p h n -> p (h n)")
                        rlink(t, nc.vector.tensor_scalar(cia, cflat, 4, None, ALU.logical_shift_right))
                        rlink(t, nc.vector.tensor_copy(cif[:, 0, :], cia))
                        rlink(t, nc.vector.tensor_scalar(cia, cflat, 15, None, ALU.bitwise_and))
                        rlink(t, nc.vector.tensor_copy(cif[:, 1, :], cia))

                def pick(t, half):
                    f4 = fidx.rearrange("p (h a) n -> p h a n", a=2)
                    oh = sc.rearrange("p s n -> p (s n)").rearrange("p (k j) -> p k j", j=TOPK)
                    rlink(t, nc.vector.tensor_tensor(oh, bc(cif[:, half, :].unsqueeze(2), [P, P, TOPK]),
                                                     bc(iota[:, :].unsqueeze(1), [P, P, TOPK]), ALU.is_equal))
                    oh4 = oh.rearrange("p (h k) j -> p h k j", h=PH)
                    rlink(t, nc.vector.tensor_tensor(oh4, oh4, bc(f4[:, :, half, :].unsqueeze(2), [P, PH, TOPK, TOPK]),
                                                     ALU.mult))
                    rlink(t, nc.vector.tensor_reduce(sel[:, half, :], oh, AX.X, ALU.add))

                def winners(t):
                    nc.vector.scalar_tensor_tensor(out=idx2[:, bass.ds((t % 2) * P, P)], in0=sel[:, 0, :],
                                                   scalar=float(NKEY), in1=sel[:, 1, :], op0=ALU.mult, op1=ALU.add)
                    nc.vector.tensor_tensor(ef, cval, bc(cval[:, :, 0:1], [P, PH, TOPK]), ALU.subtract
                                            ).then_inc(R["csub"], 1)
                    wait(dve, R["gexp"], t + 1)
                    rlink(t, nc.vector.tensor_reduce(ssum[:, 0:8], ef, AX.X, ALU.add))
                    rlink(t, nc.vector.reciprocal(small[:, 48:56], ssum[:, 0:8]))
                    rlink(t, nc.vector.tensor_tensor(
                        gate2[:, bass.ds((t % 2) * P, P)].rearrange("p (h n) -> p h n", h=PH),
                        ef, bc(small[:, 48:56].unsqueeze(2), [P, PH, TOPK]), ALU.mult))
                    assert rcount[0] == RLINKS, rcount[0]
                    rcount[0] = 0
                    dve.sem_inc(R["route_done"], 1)

                def turn(t, first=False, last=False):
                    keep_x(t)
                    half = TOPK // 2
                    route = {} if last else {
                        (4, half): lambda: top_keys(t + 1, 0), (5, 0): lambda: top_keys(t + 1, 1),
                        (5, half): lambda: top_sums(t + 1, 0), (6, 0): lambda: top_sums(t + 1, 1),
                        (6, half): lambda: top_sums(t + 1, 2), (7, 0): lambda: pick(t + 1, 0),
                        (7, half): lambda: (pick(t + 1, 1), winners(t + 1))}
                    if not first:
                        route[(1, half // 2)] = lambda: finish(t - 1)
                    for h in range(PH):
                        dot(t, h, {i: f for (hh, i), f in route.items() if hh == h})
                        weights(t, h)

                for part in range(2):
                    top_keys(0, part)
                for part in range(3):
                    top_sums(0, part)
                pick(0, 0)
                pick(0, 1)
                winners(0)
                turns(dve, lambda t: turn(t, first=True), turn, lambda t: turn(t, last=True))
                finish(TILES - 1)

        program(phase_norm)
        program(projection([RQ, RK, RV]))
        program(phase_retention)
        program(projection([RG, FQ, FK, FV]))
        recycle()
        program(phase_fox)
        program(phase_out)
        program(phase_peer)


def shape_constants():
    f = np.float32
    n = np.arange(P)
    pos = np.empty((P, TILES), np.float64)
    for t in range(PT):
        pos[:, t] = t * P + n
    pos[:, ST] = PAST + n % NS
    inv = (10000.0 ** (-np.arange(32, dtype=f) / 32)).astype(f)
    ang = (pos.astype(f)[:, :, None] * inv[None, None, :]).astype(f).astype(np.float64)
    lg = np.log1p(-(2.0 ** (-5.0 - np.arange(NH))))
    step = np.stack([n + 1.0, n % NS + 1.0])
    grown = lg[None, None, :] * step[:, :, None]
    dec = np.stack([np.exp(grown), np.exp(-grown) * HD ** -0.5])
    span = np.array([P, NS])
    sdec = np.empty((P, 2, PAIRS))
    for par in range(2):
        for r in range(PAIRS):
            sdec[64 * par:64 * par + 64, :, r] = np.exp(lg[2 * r + par] * span)[None, :]
    same = (n[:, None] // NS) == (n[None, :] // NS)
    later = n[:, None] <= n[None, :]
    causal = np.stack([later, later & same], axis=1)
    maskq = np.where(n[None, :] > n[:, None], BIG, 0.0)
    maskn = np.where(np.arange(NS)[None, :] > (n % NS)[:, None], BIG, 0.0)
    e8 = np.zeros((NH, NH, P))
    e8[np.arange(NH), np.arange(NH), :] = 1.0
    e64 = np.zeros((NB * NH, NB, P))
    for b in range(NB):
        for m in range(P):
            e64[b * NH + m // NS, b, m] = 1.0
    return {
        "c_ident": np.eye(P, dtype=f), 
        "c_causal": causal.astype(f), "c_masks": np.concatenate([maskq, maskn], axis=1).astype(f),
         "c_cos": np.cos(ang).astype(f),
        "c_nsin": (-np.sin(ang)).astype(f), "c_psin": np.sin(ang).astype(f),
        "c_dec": np.ascontiguousarray(dec.transpose(2, 0, 1, 3)).astype(f), "c_sdec": sdec.astype(f),
        "c_bind": (n[:, None] // NS == np.arange(NB)[None, :]).astype(f),
        "c_iota": np.broadcast_to(np.arange(TOPK, dtype=f), (P, TOPK)).copy(),
        "c_e8": e8.astype(f), "c_e64": e64.astype(f),
    }


_DIRECT = ["x_prompt", "x_sample", "cache_fox_k", "cache_fox_v", "state_ret", "norm1_g", "w_in", "b_f", "fox_qn_g",
           "fox_kn_g", "ret_out_g", "fox_out_g", "w_out", "norm2_g", "peer_wq", "peer_u", "peer_v"]
_OUTS = [("y_prompt", (1, NP_TOK, D)), ("y_sample", (NB, NS, D)),
         ("new_fox_k_p", (1, 1, NP_TOK, NH, HD)), ("new_fox_v_p", (1, 1, NP_TOK, NH, HD)),
         ("new_fox_logf_p", (1, 1, NP_TOK, NH)), ("new_state_ret_p", (1, 1, NH, HD, HD)),
         ("new_fox_k_s", (1, NB, NS, NH, HD)), ("new_fox_v_s", (1, NB, NS, NH, HD)),
         ("new_fox_logf_s", (1, NB, NS, NH)), ("new_state_ret_s", (1, NB, NH, HD, HD))]


def kernel(**inputs):
    import concourse.bacc as _bacc
    from concourse.bass_utils import run_bass_kernel_spmd as _run

    nc = _bacc.Bacc("TRN2", target_bir_lowering=False, num_devices=1)
    data = {n: np.ascontiguousarray(inputs[n]) for n in _DIRECT}
    data["cache_lf_t"] = np.ascontiguousarray(
        np.asarray(inputs["cache_fox_logf"])[0].transpose(0, 2, 1).reshape(NB * NH, PAST))
    data["keys_t"] = np.ascontiguousarray(
        np.asarray(inputs["peer_keys"])[0].transpose(3, 1, 0, 2).reshape(P, 2 * PH, NKEY))
    data["c_wff"] = np.ascontiguousarray(
        np.asarray(inputs["w_in"])[0, :, 7 * GW:].reshape(KC, P, NH).transpose(1, 0, 2))
    data.update(shape_constants())
    arrays, a = {}, {}
    for name, v in data.items():
        arrays[f"in_{name}"] = v
        a[name] = nc.dram_tensor(f"in_{name}", v.shape, mybir.dt.from_np(v.dtype), kind="ExternalInput").ap()
    for name, shape in _OUTS:
        a[name] = nc.dram_tensor(f"out_{name}", shape, F32, kind="ExternalOutput").ap()
    a["xn"] = nc.dram_tensor("xn_scratch", (TILES, P, D), F32, kind="Internal").ap()
    a["x1"] = nc.dram_tensor("x1_scratch", (TILES, P, D), F32, kind="Internal").ap()
    emit(nc, a)
    r = _run(nc, [arrays], core_ids=[0])
    return tuple(r.results[0][f"out_{name}"] for name, _ in _OUTS)
```

```python
import math

import numpy as np

import concourse.bass as bass
from concourse import mybir
from contextlib import ExitStack

F32 = mybir.dt.float32
BF16 = mybir.dt.bfloat16
U32 = mybir.dt.uint32
I32 = mybir.dt.int32
ALU = mybir.AluOpType
ACT = mybir.ActivationFunctionType
AX = mybir.AxisListType

P = 128
D = 1024
KC = D // P
NP_TOK, NB, NS, PAST = 1024, 8, 16, 256
TILES = (NP_TOK + NB * NS) // P
PT = NP_TOK // P
ST = PT
NH, HD = 8, 64
GW = NH * HD
PAIRS = NH // 2
EPS = 1e-6
BIG = 1e30
TOPK, NKEY, PH = 16, 128, 8
GELU_C = 2.0 * math.sqrt(2.0 / math.pi)


def emit(nc, a):
    ctx = ExitStack()
    with ctx:
        def sb(name, shape, dt=F32):
            return ctx.enter_context(nc.sbuf_tensor(name, shape, dt))

        def flat(name, n):
            return sb(name, [P, n])

        Hreg = flat("Hreg", KC * P * TILES)
        Wreg = flat("Wreg", 2 * KC * GW)
        Rreg = flat("Rreg", 4 * TILES * GW)
        mixo = sb("mixo", [P, TILES, 2 * GW])
        Xreg = flat("Xreg", 4384)
        hT = Hreg[:, :].rearrange("p (k n) -> p k n", k=KC)
        wbuf = Wreg[:, :].rearrange("p (s k c) -> p s k c", s=2, k=KC)
        quarter = TILES * GW
        qT = Rreg[:, 0:quarter].rearrange("p (r n) -> p r n", r=PAIRS)
        kT = Rreg[:, quarter:2 * quarter].rearrange("p (r n) -> p r n", r=PAIRS)
        vn = Rreg[:, 2 * quarter:3 * quarter].rearrange("p (t c) -> p t c", t=TILES)
        kn = Rreg[:, 3 * quarter:4 * quarter].rearrange("p (t c) -> p t c", t=TILES)

        ident = sb("ident", [P, P])
        identb = sb("identb", [P, P], BF16)
        causal = sb("causal", [P, 2, P])
        maskq = sb("maskq", [P, P], BF16)
        maskn = sb("maskn", [P, NS], BF16)
        cosn = mixo[:, 0, GW:GW + 32 * TILES].rearrange("p (t d) -> p t d", t=TILES)
        nsin = mixo[:, 1, GW:GW + 32 * TILES].rearrange("p (t d) -> p t d", t=TILES)
        psin = mixo[:, 2, GW:GW + 32 * TILES].rearrange("p (t d) -> p t d", t=TILES)
        gain_fq, gain_fk, gain_ret = (mixo[:, 3 + i, GW:] for i in range(3))
        grow1 = mixo[:, 7, :]
        dec = sb("dec", [P, 2, 2, NH])
        sdec = sb("sdec", [P, 2, PAIRS])
        bind = sb("bind", [P, NB])
        iota = sb("iota", [P, TOPK])
        nhalf = sb("nhalf", [P, NH])
        gain_fox = sb("gain_fox", [P, GW])
        grow = sb("grow", [P, D])
        bfb = sb("bfb", [P, NH])
        ffw = sb("ffw", [P, KC, NH])
        lgf = sb("lgf", [P, TILES, NH])
        lgfT = Hreg[0:NH, 7040:7040 + TILES * P]
        small = sb("small", [P, 64])

        def bc(ap, shape):
            return ap.to_broadcast(shape)

        held = ctx.enter_context(nc.semaphore("held"))

        def after(engine, semaphore, value):
            engine.wait_ge(semaphore, value)
            engine.sem_inc(held, 1)

        phases, used = [], []

        def recycle():
            nc.clear_and_free_semaphores(used)
            used.clear()
            nc.all_engine_barrier()

        def program(body):
            phases.append(body)
            with ExitStack() as ph:
                def sem(name):
                    used.append(nc.alloc_semaphore(f"{name}_{len(phases)}"))
                    return used[-1]

                def ps(name, shape):
                    return ph.enter_context(nc.psum_tensor(f"{name}_{len(phases)}", shape, F32))

                block = ph.enter_context(nc.Block())
                body(block, sem, ps)

        def phase_norm(block, sem, ps):
            const_in = sem("const_in")
            x_in = [sem(f"x_in{t}") for t in range(TILES)]
            sq_done, rs_done, xs_done = sem("sq_done"), sem("rs_done"), sem("xs_done")
            tr_done, ev_done, ev2_done = sem("tr_done"), sem("ev_done"), sem("ev2_done")
            pool_step, w_ahead = sem("pool_step"), sem("w_ahead")
            xt = Rreg[:, D:(TILES + 1) * D].rearrange("p (s d) -> p s d", s=TILES)
            xs = Xreg[:, 2 * D:4 * D].rearrange("p (s d) -> p s d", s=2)
            junk = Rreg[:, 0:D]
            tp = [ps(f"tp{i}", [P, 4, P]) for i in range(4)]
            masks = Xreg[:, 4 * D:4 * D + P + NS]
            loads = [(ident, a["c_ident"]), (causal, a["c_causal"]), (masks, a["c_masks"]), (cosn, a["c_cos"]), (nsin, a["c_nsin"]), (psin, a["c_psin"]),
                     (dec, a["c_dec"]), (sdec, a["c_sdec"]), (bind, a["c_bind"]), (iota, a["c_iota"])]
            grows = [(gain_fq, a["fox_qn_g"]), (gain_fk, a["fox_kn_g"]), (gain_ret, a["ret_out_g"]),
                     (gain_fox[:, :], a["fox_out_g"])]
            n_const = 16 * (len(loads) + len(grows) + 2)

            def x_rows(t):
                return a["x_prompt"][0, t * P:(t + 1) * P, :] if t < PT else \
                    a["x_sample"].rearrange("b t d -> (b t) d")

            @block.sync
            def _(sp):
                for t in range(TILES):
                    if t == 2:
                        sp.wait_ge(const_in, n_const)
                    sp.dma_start(xt[:, t, :], x_rows(t)).then_inc(x_in[t], 16)
                for g in (RQ, RK):
                    sp.dma_start(wbuf[:, g], a["w_in"][0, :, g * GW:(g + 1) * GW]
                                 .rearrange("(k p) c -> p k c", p=P)).then_inc(w_ahead, 16)
                sp.wait_ge(w_ahead, 32)

            @block.scalar
            def _(act):
                for dst, src in loads:
                    act.dma_start(dst[tuple(slice(None) for _ in dst.shape)], src).then_inc(const_in, 16)
                for dst, g in grows:
                    act.dma_start(dst, g.rearrange("a h d -> a (h d)").partition_broadcast(P)
                                  .rearrange("p a c -> p (a c)")).then_inc(const_in, 16)
                act.dma_start(grow1, a["norm1_g"].partition_broadcast(P)
                              .rearrange("p a c -> p (a c)")).then_inc(const_in, 16)
                act.dma_start(bfb[:, :], a["b_f"].partition_broadcast(P)
                              .rearrange("p a c -> p (a c)")).then_inc(const_in, 16)

                def evacuate(t):
                    act.wait_ge(tr_done, t + 1)
                    nc.scalar.copy(hT[:, 0:4, t * P:(t + 1) * P], tp[2 * (t % 2)][:, :, :]).then_inc(ev_done, 1)

                for t in range(TILES):
                    act.wait_ge(x_in[t], 16)
                    nc.scalar.activation(junk, xt[:, t, :], ACT.Square,
                                         accum_out=small[:, t:t + 1]).then_inc(sq_done, 1)
                    act.wait_ge(sq_done, t + 1)
                    if t >= 1:
                        evacuate(t - 1)
                evacuate(TILES - 1)

            @block.gpsimd
            def _(pool):
                nc.gpsimd.memset(nhalf[:, :], -0.5).then_inc(pool_step, 1)
                pool.wait_ge(pool_step, 1)
                for t in range(TILES):
                    pool.wait_ge(sq_done, t + 1)
                    nc.gpsimd.tensor_scalar(small[:, 16 + t:17 + t], small[:, t:t + 1], 1.0 / D, EPS,
                                            ALU.mult, ALU.add).then_inc(pool_step, 1)
                    pool.wait_ge(pool_step, t + 2)
                    nc.gpsimd.tensor_tensor(small[:, 32 + t:33 + t], small[:, 16 + t:17 + t], nhalf[:, 0:1],
                                            ALU.pow).then_inc(rs_done, 1)

            @block.vector
            def _(dve):
                dve.wait_ge(const_in, n_const)
                nc.vector.tensor_copy(identb[:, :], ident[:, :])
                nc.vector.tensor_copy(maskq[:, :], masks[:, 0:P])
                nc.vector.tensor_copy(maskn[:, :], masks[:, P:])
                for t in range(TILES + 1):
                    if t < TILES:
                        dve.wait_ge(rs_done, t + 1)
                        if t >= 2:
                            dve.wait_ge(tr_done, t - 1)
                        nc.vector.scalar_tensor_tensor(out=xs[:, t % 2, :], in0=xt[:, t, :],
                                                       scalar=small[:, 32 + t:33 + t], in1=grow1,
                                                       op0=ALU.mult, op1=ALU.mult).then_inc(xs_done, 1)
                    if t >= 1:
                        dve.wait_ge(tr_done, t)
                        nc.vector.tensor_copy(hT[:, 4:8, (t - 1) * P:t * P],
                                              tp[2 * ((t - 1) % 2) + 1][:, :, :]).then_inc(ev2_done, 1)

            @block.tensor
            def _(pe):
                pe.wait_ge(const_in, n_const)
                for t in range(TILES):
                    pe.wait_ge(xs_done, t + 1)
                    if t >= 2:
                        pe.wait_ge(ev_done, t - 1)
                        pe.wait_ge(ev2_done, t - 1)
                    for k in range(KC):
                        last = nc.tensor.transpose(tp[2 * (t % 2) + k // 4][:, k % 4, :],
                                                   xs[:, t % 2, k * P:(k + 1) * P], ident[:, :])
                    last.then_inc(tr_done, 1)

        RQ, RK, RV, RG, FQ, FK, FV = range(7)

        def projection(groups):
            def body(block, sem, ps):
                steps = [(g, t) for g in groups for t in range(TILES)]
                turned = [n for n, (g, _) in enumerate(steps) if g in (RQ, RK, FQ, FK)]
                order = {n: m for m, n in enumerate(turned)}
                normed = [n for n, (g, _) in enumerate(steps) if g in (RG, FQ, FK)]
                norder = {n: m for m, n in enumerate(normed)}
                w_in = [sem(f"w_in{i}") for i in range(2)]
                w_used, z_done = sem("w_used"), sem("z_done")
                z_free = [sem(f"z_free{i}") for i in range(3)]
                rot_done, tr_done, ev_done = sem("rot_done"), sem("tr_done"), sem("ev_done")
                link_sem, v_done = sem("link_sem"), sem("v_done")
                with_ff = FV in groups
                if with_ff:
                    sq_done, ss_done, rs_done = sem("sq_done"), sem("ss_done"), sem("rs_done")
                    pool_step, gate_exp, out_done = sem("pool_step"), sem("gate_exp"), sem("out_done")
                    ff_in, ff_done, ff_z, ff_abs = sem("ff_in"), sem("ff_done"), sem("ff_z"), sem("ff_abs")
                    ff_exp, ff_e1, ff_ln, ff_log = sem("ff_exp"), sem("ff_e1"), sem("ff_ln"), sem("ff_log")
                    ffT, ff_row, ff_cp = sem("ffT"), sem("ff_row"), sem("ff_cp")
                    ffr = Rreg[0:NH, quarter:quarter + TILES * P]
                z = [ps(f"z{i}", [P, GW]) for i in range(3)]
                tp = [ps(f"ztp{i}", [P, 4, P]) for i in range(2)]
                ffp = ps("ffp", [P, TILES, NH])
                ffpt = ps("ffpt", [NH, 2, 512])
                tmp = Xreg[:, 0:8 * GW].rearrange("p (s c) -> p s c", s=8)
                ffx = Xreg[:, 8 * GW:8 * GW + 4 * TILES * NH].rearrange("p (s t h) -> p s t h", s=4, t=TILES)

                def heads(ap):
                    return ap.rearrange("p (h d) -> p h d", h=NH)

                @block.sync
                def _(sp):
                    if with_ff:
                        sp.dma_start(ffw[:, :, :], a["c_wff"]).then_inc(ff_in, 16)
                    for gi, g in enumerate(groups):
                        if g in (RQ, RK):
                            continue
                        if gi >= 2:
                            sp.wait_ge(w_used, gi - 1)
                        sp.dma_start(wbuf[:, gi % 2], a["w_in"][0, :, g * GW:(g + 1) * GW]
                                     .rearrange("(k p) c -> p k c", p=P)).then_inc(w_in[gi % 2], 16)
                    outs = 0
                    for n, (g, t) in enumerate(steps):
                        if g == FK:
                            sp.wait_ge(rot_done, order[n] + 1)
                            src, dk = kn[:, t, :], "new_fox_k"
                        elif g == FV:
                            sp.wait_ge(v_done, t + 1)
                            src, dk = vn[:, t, :], "new_fox_v"
                        else:
                            continue
                        dst = a[dk + "_p"][0, 0, t * P:(t + 1) * P].rearrange("n h d -> n (h d)") if t < PT else \
                            a[dk + "_s"][0].rearrange("b n h d -> (b n) (h d)")
                        sp.dma_start(dst, src).then_inc(out_done, 16)
                        outs += 1
                    if with_ff:
                        sp.wait_ge(ff_log, 1)
                        sp.dma_start(a["new_fox_logf_p"][0, 0].rearrange("(t p) h -> p t h", p=P),
                                     lgf[:, 0:PT, :]).then_inc(out_done, 16)
                        sp.dma_start(a["new_fox_logf_s"][0].rearrange("b n h -> (b n) h"),
                                     lgf[:, ST, :]).then_inc(out_done, 16)
                        outs += 2
                    if outs:
                        sp.wait_ge(out_done, 16 * outs)

                @block.tensor
                def _(pe):
                    def turn(n):
                        m = order[n]
                        g, t = steps[n]
                        pe.wait_ge(rot_done, m + 1)
                        if m >= 2:
                            pe.wait_ge(ev_done, m - 1)
                        src = tmp[:, 6 + m % 2, :] if g in (RQ, FQ) else kn[:, t, :]
                        for r in range(PAIRS):
                            last = nc.tensor.transpose(tp[m % 2][:, r, :], src[:, r * P:(r + 1) * P], ident[:, :])
                        last.then_inc(tr_done, 1)

                    if with_ff:
                        pe.wait_ge(ff_in, 16)
                        for c in range(3):
                            w = min(512, TILES * P - 512 * c)
                            for k in range(KC):
                                last = nc.tensor.matmul(z[c][0:NH, 0:w], ffw[:, k, :], hT[:, k, 512 * c:512 * c + w],
                                                        start=(k == 0), stop=(k == KC - 1))
                            last.then_inc(ff_row, 1)
                        pe.wait_ge(ff_cp, 3)
                        for t in range(TILES):
                            last = nc.tensor.transpose(ffp[:, t, :], ffr[:, t * P:(t + 1) * P], ident[0:NH, 0:NH])
                        last.then_inc(ff_done, 1)
                    for n, (g, t) in enumerate(steps):
                        gi = n // TILES
                        if t == 0 and g not in (RQ, RK):
                            pe.wait_ge(w_in[gi % 2], 16 * len([x for x in groups[gi % 2:gi + 1:2]
                                                               if x not in (RQ, RK)]))
                        if n >= 3:
                            pe.wait_ge(z_free[n % 3], n // 3)
                        for k in range(KC):
                            last = nc.tensor.matmul(z[n % 3][:, :], hT[:, k, t * P:(t + 1) * P],
                                                    wbuf[:, gi % 2, k, :], start=(k == 0), stop=(k == KC - 1))
                        last.then_inc(z_done, 1)
                        if t == TILES - 1:
                            pe.wait_ge(z_done, n + 1)
                            pe.sem_inc(w_used, 1)
                        if n - 2 in order:
                            turn(n - 2)
                    for n in range(len(steps) - 2, len(steps)):
                        if n in order:
                            turn(n)
                    if with_ff:
                        pe.wait_ge(ff_log, 1)
                        for t in range(TILES):
                            if t == PT:
                                pe.wait_ge(ffT, 1)
                            last = nc.tensor.transpose(ffpt[:, (t // 4) % 2, (t % 4) * P:(t % 4 + 1) * P],
                                                       lgf[:, t, :], ident[:, :])
                            if t == PT - 1 or t == ST:
                                last.then_inc(tr_done, 1)

                @block.scalar
                def _(act):
                    def evacuate(n):
                        m = order[n]
                        g, t = steps[n]
                        act.wait_ge(tr_done, m + 1)
                        dst = qT if g in (RQ, FQ) else kT
                        nc.scalar.copy(dst[:, :, t * P:(t + 1) * P], tp[m % 2][:, :, :]).then_inc(ev_done, 1)

                    if with_ff:
                        for c in range(3):
                            w = min(512, TILES * P - 512 * c)
                            act.wait_ge(ff_row, c + 1)
                            nc.scalar.copy(ffr[:, 512 * c:512 * c + w], z[c][0:NH, 0:w]).then_inc(ff_cp, 1)
                        act.wait_ge(ff_z, 1)
                        nc.scalar.activation(ffx[:, 1], ffx[:, 0], ACT.Abs).then_inc(ff_abs, 1)
                        act.wait_ge(ff_abs, 1)
                        nc.scalar.activation(ffx[:, 2], ffx[:, 1], ACT.Exp, scale=-1.0).then_inc(ff_exp, 1)
                        act.wait_ge(ff_e1, 1)
                        nc.scalar.activation(ffx[:, 1], ffx[:, 3], ACT.Ln).then_inc(ff_ln, 1)
                    for n, (g, t) in enumerate(steps):
                        if g in (RV, FV):
                            act.wait_ge(z_done, n + 1)
                            nc.scalar.copy(vn[:, t, :], z[n % 3][:, :]).then_inc(z_free[n % 3], 1)
                            act.wait_ge(z_free[n % 3], n // 3 + 1)
                            act.sem_inc(v_done, 1)
                        if g in (FQ, FK):
                            m = norder[n]
                            act.wait_ge(z_done, n + 1)
                            if m >= 2:
                                act.wait_ge(ss_done, m - 1)
                            nc.scalar.activation(tmp[:, m % 2, :], z[n % 3][:, :], ACT.Square).then_inc(sq_done, 1)
                        if g == RG:
                            m = norder[n]
                            if m >= 2:
                                act.wait_ge(ss_done, m - 1)
                            nc.scalar.activation(tmp[:, m % 2, :], mixo[:, t, 0:GW], ACT.Square).then_inc(sq_done, 1)
                            act.wait_ge(z_done, n + 1)
                            if n >= 2:
                                act.wait_ge(z_free[(n - 2) % 3], (n - 2) // 3 + 1)
                            nc.scalar.activation(tmp[:, 2 + m % 2, :], z[n % 3][:, :], ACT.Exp,
                                                 scale=-1.0).then_inc(gate_exp, 1)
                        if n - 2 in order:
                            evacuate(n - 2)
                    for n in range(len(steps) - 2, len(steps)):
                        if n in order:
                            evacuate(n)
                    if with_ff:
                        act.wait_ge(tr_done, len(order) + 1)
                        nc.scalar.copy(lgfT[:, 0:NP_TOK], ffpt[:, :, :].rearrange("h a n -> h (a n)")).then_inc(ffT, 1)
                        act.wait_ge(tr_done, len(order) + 2)
                        nc.scalar.copy(lgfT[:, NP_TOK:], ffpt[:, 0, 0:P])

                @block.gpsimd
                def _(pool):
                    steps_done = 0
                    for m, n in enumerate(normed):
                        g, t = steps[n]
                        o = 8 * (m % 2)
                        pool.wait_ge(ss_done, m + 1)
                        nc.gpsimd.tensor_scalar(small[:, 16 + o:24 + o], small[:, o:o + 8], 1.0 / HD, EPS,
                                                ALU.mult, ALU.add).then_inc(pool_step, 1)
                        steps_done += 1
                        pool.wait_ge(pool_step, steps_done)
                        ins = nc.gpsimd.tensor_tensor(small[:, 32 + o:40 + o], small[:, 16 + o:24 + o],
                                                      nhalf[:, :], ALU.pow)
                        if g == FQ:
                            ins.then_inc(pool_step, 1)
                            steps_done += 1
                            pool.wait_ge(pool_step, steps_done)
                            ins = nc.gpsimd.tensor_scalar(small[:, 32 + o:40 + o], small[:, 32 + o:40 + o],
                                                          -(HD ** -0.5), None, ALU.mult)
                        ins.then_inc(rs_done, 1)

                @block.vector
                def _(dve):
                    count = [0]

                    def link(ins):
                        count[0] += 1
                        ins.then_inc(link_sem, 1)
                        dve.wait_ge(link_sem, count[0])

                    if with_ff:
                        dve.wait_ge(ff_done, 1)
                        nc.vector.tensor_tensor(ffx[:, 0], ffp[:, :, :], bc(bfb[:, :].unsqueeze(1), [P, TILES, NH]),
                                                ALU.add).then_inc(ff_z, 1)
                        dve.wait_ge(ff_exp, 1)
                        nc.vector.tensor_scalar_add(ffx[:, 3], ffx[:, 2], 1.0).then_inc(ff_e1, 1)
                        dve.wait_ge(ff_ln, 1)
                        nc.vector.scalar_tensor_tensor(out=lgf[:, :, :], in0=ffx[:, 0], scalar=0.0, in1=ffx[:, 1],
                                                       op0=ALU.min, op1=ALU.subtract).then_inc(ff_log, 1)
                    for n, (g, t) in enumerate(steps):
                        zn = z[n % 3][:, :]
                        kind = 0 if t < PT else 1
                        if g in (RQ, RK):
                            m = order[n]
                            dve.wait_ge(z_done, n + 1)
                            z4 = zn.rearrange("p (h a d) -> p h a d", h=NH, a=2)
                            A = tmp[:, 2, :].rearrange("p (h a d) -> p h a d", h=NH, a=2)
                            B = tmp[:, 3, :].rearrange("p (h a d) -> p h a d", h=NH, a=2)
                            cs = bc(cosn[:, t, :].unsqueeze(1).unsqueeze(1), [P, NH, 2, 32])
                            nc.vector.tensor_tensor(A, z4, cs, ALU.mult)
                            nc.vector.tensor_tensor(B[:, :, 0, :], z4[:, :, 1, :],
                                                    bc(nsin[:, t, :].unsqueeze(1), [P, NH, 32]), ALU.mult)
                            count[0] += 1
                            nc.vector.tensor_tensor(B[:, :, 1, :], z4[:, :, 0, :],
                                                    bc(psin[:, t, :].unsqueeze(1), [P, NH, 32]),
                                                    ALU.mult).then_inc(link_sem, 1)
                            dve.wait_ge(link_sem, count[0])
                            dve.sem_inc(z_free[n % 3], 1)
                            link(nc.vector.tensor_tensor(tmp[:, 4, :], tmp[:, 2, :], tmp[:, 3, :], ALU.add))
                            if g == RQ:
                                if m >= 2:
                                    dve.wait_ge(tr_done, m - 1)
                                dst = tmp[:, 6 + m % 2, :]
                            else:
                                dst = kn[:, t, :]
                            nc.vector.tensor_tensor(
                                heads(dst), heads(tmp[:, 4, :]),
                                bc(dec[:, 0 if g == RQ else 1, kind, :].unsqueeze(2), [P, NH, HD]),
                                ALU.mult).then_inc(rot_done, 1)
                        if g in (RG, FQ, FK):
                            m = norder[n]
                            o = 8 * (m % 2)
                            dve.wait_ge(sq_done, m + 1)
                            nc.vector.tensor_reduce(small[:, o:o + 8], heads(tmp[:, m % 2, :]), AX.X,
                                                    ALU.add).then_inc(ss_done, 1)
                            if g == RG:
                                dve.wait_ge(gate_exp, m + 1)
                                link(nc.vector.tensor_scalar_add(tmp[:, 4, :], tmp[:, 2 + m % 2, :], 1.0))
                                link(nc.vector.reciprocal(tmp[:, 5, :], tmp[:, 4, :]))
                                link(nc.vector.tensor_tensor(tmp[:, 4, :], zn, tmp[:, 5, :], ALU.mult))
                                dve.sem_inc(z_free[n % 3], 1)
                                link(nc.vector.tensor_tensor(tmp[:, 5, :], tmp[:, 4, :], gain_ret, ALU.mult))
                                link(nc.vector.tensor_tensor(tmp[:, 4, :], tmp[:, 5, :], mixo[:, t, 0:GW], ALU.mult))
                                dve.wait_ge(rs_done, m + 1)
                                link(nc.vector.tensor_tensor(heads(mixo[:, t, 0:GW]), heads(tmp[:, 4, :]),
                                                             bc(small[:, 32 + o:40 + o].unsqueeze(2), [P, NH, HD]),
                                                             ALU.mult))
                            else:
                                mt = order[n]
                                dve.wait_ge(rs_done, m + 1)
                                link(nc.vector.tensor_tensor(heads(tmp[:, 4, :]), heads(zn),
                                                             bc(small[:, 32 + o:40 + o].unsqueeze(2), [P, NH, HD]),
                                                             ALU.mult))
                                dve.sem_inc(z_free[n % 3], 1)
                                if g == FQ:
                                    if mt >= 2:
                                        dve.wait_ge(tr_done, mt - 1)
                                    dst = tmp[:, 6 + mt % 2, :]
                                else:
                                    dst = kn[:, t, :]
                                nc.vector.tensor_tensor(dst, tmp[:, 4, :], gain_fq if g == FQ else gain_fk,
                                                        ALU.mult).then_inc(rot_done, 1)
            return body

        def phase_retention(block, sem, ps):
            st = Wreg[:, 0:PAIRS * HD].rearrange("p (r e) -> p r e", r=PAIRS)
            stt = Wreg[:, 256:512].rearrange("p (r e) -> p r e", r=PAIRS)
            sT = Wreg[:, 512:512 + 2 * NH * P].rearrange("p (s q r l) -> p s q r l", s=2, q=2, r=PAIRS)
            s0 = Wreg[:, 2560:2560 + 2048].rearrange("p (r b e) -> p r b e", r=PAIRS, b=NB)
            vbd = Wreg[:, 4608:4608 + 2 * GW].rearrange("p (s b e) -> p s b e", s=2, b=NB)
            sadd = Wreg[:, 5632:5632 + 2048].rearrange("p (r b e) -> p r b e", r=PAIRS, b=NB)
            oT = Wreg[:, 7680:7680 + GW].rearrange("p (r l) -> p r l", r=PAIRS)
            sc = [ps(f"sc{i}", [P, 4, P]) for i in range(2)]
            op_all = [[ps(f"op{i}{j}", [P, GW]) for j in range(2)] for i in range(2)]
            op = [[b[:, 0:PAIRS * HD].rearrange("p (r e) -> p r e", r=PAIRS) for b in row] for row in op_all]
            up_all = ps("up", [P, GW])
            up = up_all[:, 0:PAIRS * HD].rearrange("p (r e) -> p r e", r=PAIRS)
            opT = ps("opT", [P, PAIRS, P])
            snew = [op_all[i][0][:, :].rearrange("p (b e) -> p b e", b=NB) for i in range(2)]
            sc_done, mask_done, o_done, oev = sem("sc_done"), sem("mask_done"), sem("o_done"), sem("oev")
            up_done, st_done, link_sem = sem("up_done"), sem("st_done"), sem("link_sem")
            s0_in, oT_done, oTc, vb_done = sem("s0_in"), sem("oT_done"), sem("oTc"), sem("vb_done")
            sn_done, sn_out, out_done, oTt = sem("sn_done"), sem("sn_out"), sem("out_done"), sem("oTt")

            @block.sync
            def _(sp):
                for par in range(2):
                    for r in range(PAIRS):
                        sp.dma_start(s0[64 * par:64 * par + 64, r],
                                     a["state_ret"][0, :, 2 * r + par].rearrange("b d e -> d b e")).then_inc(s0_in, 16)
                sp.wait_ge(st_done, PT)
                for par in range(2):
                    sp.dma_start(a["new_state_ret_p"][0, 0].rearrange("(r q) d e -> q d r e", q=2)[par],
                                 st[64 * par:64 * par + 64]).then_inc(out_done, 16)
                for r in range(PAIRS):
                    sp.wait_ge(sn_out, r + 1)
                    for par in range(2):
                        sp.dma_start(a["new_state_ret_s"][0, :, 2 * r + par].rearrange("b d e -> d b e"),
                                     sadd[64 * par:64 * par + 64, r]).then_inc(out_done, 16)
                sp.wait_ge(out_done, 16 * (2 + 2 * PAIRS))

            @block.tensor
            def _(pe):
                def scores(t):
                    for half in range(2):
                        if t >= 1:
                            pe.wait_ge(mask_done, 2 * (t - 1) + half + 1)
                        for r in range(PAIRS):
                            b0 = 64 * half
                            last = nc.tensor.matmul(sc[half][:, r, :], kT[b0:b0 + 64, r, t * P:(t + 1) * P],
                                                    qT[b0:b0 + 64, r, t * P:(t + 1) * P], start=True, stop=True)
                        last.then_inc(sc_done, 1)

                def outputs(t):
                    if t >= 2:
                        pe.wait_ge(oev, t - 1)
                    if t >= 1:
                        pe.wait_ge(st_done, t)
                    for h in range(NH):
                        if h < 2:
                            pe.wait_ge(mask_done, 2 * t + h + 1)
                        b0, r = 64 * (h % 2), h // 2
                        o = op[h % 2][t % 2][:, r, :]
                        last = nc.tensor.matmul(o, sT[:, t % 2, h % 2, r, :], vn[:, t, h * HD:(h + 1) * HD],
                                                start=True, stop=(t == 0))
                        if t:
                            last = nc.tensor.matmul(o, qT[b0:b0 + 64, r, t * P:(t + 1) * P],
                                                    st[b0:b0 + 64, r, :], start=False, stop=True)
                    last.then_inc(o_done, 1)
                    for h in range(NH):
                        b0, r = 64 * (h % 2), h // 2
                        last = nc.tensor.matmul(up[b0:b0 + 64, r, :], kn[:, t, h * HD:(h + 1) * HD],
                                                vn[:, t, h * HD:(h + 1) * HD], start=True, stop=True)
                    last.then_inc(up_done, 1)

                scores(0)
                for t in range(PT):
                    scores(t + 1)
                    outputs(t)
                pe.wait_ge(s0_in, 16 * NH)
                pe.wait_ge(mask_done, 2 * TILES)
                for h in range(NH):
                    b0, r = 64 * (h % 2), h // 2
                    nc.tensor.matmul(opT[b0:b0 + 64, r, :], vn[:, ST, h * HD:(h + 1) * HD], sT[:, ST % 2, h % 2, r, :],
                                     start=True, stop=False)
                    for b in range(NB):
                        c = NP_TOK + b * NS
                        last = nc.tensor.matmul(opT[b0:b0 + 64, r, b * NS:(b + 1) * NS], s0[b0:b0 + 64, r, b, :],
                                                qT[b0:b0 + 64, r, c:c + NS], start=False, stop=(b == NB - 1))
                last.then_inc(oT_done, 1)
                pe.wait_ge(oev, PT)
                for h in range(NH):
                    b0, r = 64 * (h % 2), h // 2
                    pe.wait_ge(vb_done, h + 1)
                    if h % 2 == 0 and r >= 2:
                        pe.wait_ge(sn_out, r - 1)
                    last = nc.tensor.matmul(snew[r % 2][b0:b0 + 64].rearrange("p b e -> p (b e)"),
                                            kn[:, ST, h * HD:(h + 1) * HD],
                                            vbd[:, h % 2].rearrange("p b e -> p (b e)"), start=True, stop=True)
                    last.then_inc(sn_done, 1)
                pe.wait_ge(oTc, 1)
                pe.wait_ge(st_done, PT)
                for r in range(PAIRS):
                    last = nc.tensor.transpose(up_all[:, r * P:(r + 1) * P], oT[:, r, :], ident[:, :])
                last.then_inc(oTt, 1)

            @block.vector
            def _(dve):
                count = [0]

                def link(ins):
                    count[0] += 1
                    ins.then_inc(link_sem, 1)
                    dve.wait_ge(link_sem, count[0])

                def mask(t):
                    for half in range(2):
                        dve.wait_ge(sc_done, 2 * t + half + 1)
                        if t >= 2:
                            dve.wait_ge(o_done, t - 1)
                        nc.vector.tensor_tensor(sT[:, t % 2, half], sc[half][:, :, :],
                                                bc(causal[:, 0 if t < PT else 1, :].unsqueeze(1), [P, 4, P]),
                                                ALU.mult).then_inc(mask_done, 1)

                for t in range(PT):
                    mask(t)
                    dve.wait_ge(up_done, t + 1)
                    sd = bc(sdec[:, 0, :].unsqueeze(2), [P, PAIRS, HD])
                    if t == 0:
                        nc.vector.tensor_tensor(st, up, sd, ALU.mult).then_inc(st_done, 1)
                    else:
                        link(nc.vector.tensor_tensor(stt, up, st, ALU.add))
                        nc.vector.tensor_tensor(st, stt, sd, ALU.mult).then_inc(st_done, 1)
                    dve.wait_ge(st_done, t + 1)
                mask(ST)
                dve.wait_ge(s0_in, 16 * NH)

                def spread(h):
                    if h >= 2:
                        dve.wait_ge(sn_done, h - 1)
                    nc.vector.tensor_tensor(vbd[:, h % 2],
                                            bc(vn[:, ST, h * HD:(h + 1) * HD].unsqueeze(1), [P, NB, HD]),
                                            bc(bind[:, :].unsqueeze(2), [P, NB, HD]), ALU.mult).then_inc(vb_done, 1)

                spread(0)
                spread(1)
                for r in range(PAIRS):
                    if r + 1 < PAIRS:
                        spread(2 * r + 2)
                        spread(2 * r + 3)
                    dve.wait_ge(sn_done, 2 * r + 2)
                    link(nc.vector.tensor_tensor(sadd[:, r], snew[r % 2], s0[:, r], ALU.add))
                    nc.vector.tensor_scalar(sadd[:, r], sadd[:, r], sdec[:, 1, r:r + 1], None,
                                            ALU.mult).then_inc(sn_out, 1)

            @block.scalar
            def _(act):
                for t in range(PT):
                    act.wait_ge(o_done, t + 1)
                    for par in range(2):
                        last = nc.scalar.copy(
                            mixo[:, t, 0:GW].rearrange("p (r q e) -> p q r e", q=2, e=HD)[:, par],
                            op[par][t % 2])
                    last.then_inc(oev, 1)
                act.wait_ge(oT_done, 1)
                nc.scalar.copy(oT, opT[:, :, :]).then_inc(oTc, 1)
                act.wait_ge(oTt, 1)
                nc.scalar.copy(mixo[:, ST, 0:GW], up_all[:, :])

        def phase_fox(block, sem, ps):
            cB = Hreg[:, 0:2 * NP_TOK].rearrange("p (s n) -> p s n", s=2)
            sN = Hreg[:, 2048:4096].rearrange("p (s n) -> p s n", s=2)
            pr = Hreg[:, 4096:6144].rearrange("p (s n) -> p s n", s=2)
            pT = Hreg[:, 6144:8192].rearrange("p (s j q) -> p s j q", s=2, j=8)
            ones = Hreg[:, 8192:9216]
            csum = Rreg[0:NH, 3 * quarter:3 * quarter + NP_TOK]
            e8 = Rreg[0:NH, 3 * quarter + 1024:3 * quarter + 2048].rearrange("p (h m) -> p h m", h=NH)
            e64 = Rreg[0:64, 3 * quarter + 2048:3 * quarter + 3072].rearrange("p (b m) -> p b m", b=NB)
            lfs = Rreg[0:64, 3 * quarter + 3072:3 * quarter + 3344]
            cs = Rreg[0:64, 3 * quarter + 3344:3 * quarter + 3616]
            mn = sb("mn", [P, 4, 3])
            ck = Wreg[:, 0:2048].rearrange("p (s j c) -> p s j c", s=2, j=2)
            cv = Wreg[:, 2048:4096].rearrange("p (s j c) -> p s j c", s=2, j=2)
            vnew = Wreg[0:NS, 4096:8192].rearrange("p (b c) -> p b c", b=NB)
            qbd = Xreg[:, 0:1024].rearrange("p (r b a q) -> p r b a q", r=PAIRS, b=NB, a=2)
            ckT = Xreg[:, 1024:2048].rearrange("p (r n) -> p r n", r=PAIRS)
            pn = Xreg[:, 2048:2048 + 272]
            pns = Xreg[:, 2320:2320 + 272]
            psT = Xreg[:, 2592:2592 + 384].rearrange("p (j m) -> p j m", j=3)
            foT = Xreg[:, 2976:2976 + 512].rearrange("p (r n) -> p r n", r=PAIRS)
            sp_ = [ps(f"s{i}", [P, NP_TOK]) for i in range(2)]
            tpp = ps("tpp", [P, 8, P])
            ov = ps("ov", [P, P])
            cbp = ps("cbp", [P, 512])

            oTs = Xreg[:, 1024:3072].rearrange("p (s i q) -> p s i q", s=2, i=PT)
            inv = lgf[:, 0:PT, :]
            otr_mm, ofin = sem("otr_mm"), sem("ofin")
            e_in, lf_in, vn_in = sem("e_in"), sem("lf_in"), sem("vn_in")
            ones_set, c_done, cs_done = sem("ones_set"), sem("c_done"), sem("cs_done")
            cb_mm, cb_ev = sem("cb_mm"), sem("cb_ev")
            s_done, ttr_done, exp_done, t_done = sem("s_done"), sem("ttr_done"), sem("exp_done"), sem("t_done")
            pta, ptb, pv_done, norm_done, rl_done = sem("pta"), sem("ptb"), sem("pv_done"), sem("norm_done"), sem("rl_done")
            ck_in, cv_in = [sem(f"ck_in{i}") for i in range(2)], [sem(f"cv_in{i}") for i in range(2)]
            qb_done, qz = sem("qb_done"), sem("qz")
            kt_mm, kt_ev, ss_done, smin, sexp, spn = (sem(x) for x in ("kt_mm", "kt_ev", "ss_done", "smin", "sexp", "spn"))
            st_mm, st_ev, so_mm, so_ev, srl, fT_mm = (sem(x) for x in ("st_mm", "st_ev", "so_mm", "so_ev", "srl", "fT_mm"))
            S2 = [sp_[1][:, 512 * i:512 * i + 272] for i in range(2)]
            NSTEP = NH * PT

            def wide_before(n):
                return 4 * (n // PT) + max(0, n % PT - 4)

            @block.sync
            def _(sp):
                sp.dma_start(e8, a["c_e8"]).then_inc(e_in, 16)
                sp.dma_start(e64, a["c_e64"]).then_inc(e_in, 16)
                sp.dma_start(lfs[:, 0:PAST], a["cache_lf_t"]).then_inc(lf_in, 16)
                for b in range(NB):
                    sp.dma_start(lfs[b * NH:(b + 1) * NH, PAST:PAST + NS],
                                 lgfT[:, NP_TOK + b * NS:NP_TOK + (b + 1) * NS]).then_inc(lf_in, 16)
                    sp.dma_start(vnew[:, b, :], vn[b * NS:(b + 1) * NS, ST, :]).then_inc(vn_in, 16)
                for b in range(NB):
                    if b >= 2:
                        sp.wait_ge(kt_mm, b - 1)
                    sp.dma_start(ck[:, b % 2], a["cache_fox_k"][0, b].rearrange("(j p) h d -> p j (h d)", p=P)
                                 ).then_inc(ck_in[b % 2], 16)
                    if b >= 2:
                        sp.wait_ge(so_mm, b - 1)
                    sp.dma_start(cv[:, b % 2], a["cache_fox_v"][0, b].rearrange("(j p) h d -> p j (h d)", p=P)
                                 ).then_inc(cv_in[b % 2], 16)

            @block.tensor
            def _(pe):
                def decay_rows(m):
                    h, half = m // 2, m % 2
                    if m >= 1:
                        pe.wait_ge(cb_ev, m)
                    if h >= 4:
                        pe.wait_ge(ofin, 2 * ((h - 2) // 2))
                    nc.tensor.matmul(cbp[:, :], e8[:, h, :], csum[:, 512 * half:512 * half + 512],
                                     start=True, stop=True).then_inc(cb_mm, 1)

                def scores(n):
                    h, i = n // PT, n % PT
                    b0, r = 64 * (h % 2), h // 2
                    if n >= 2:
                        pe.wait_ge(ttr_done, n - 1)
                    width = (i + 1) * P
                    for c in range(0, width, 512):
                        w = min(512, width - c)
                        final = c + w == width
                        nc.tensor.matmul(sp_[n % 2][:, c:c + w], qT[b0:b0 + 64, r, i * P:(i + 1) * P],
                                         kT[b0:b0 + 64, r, c:c + w], start=True, stop=not final)
                    nc.tensor.matmul(sp_[n % 2][:, i * P:width], identb[:, :], maskq[:, :],
                                     start=False, stop=True).then_inc(s_done, 1)

                def turn(n):
                    h, i = n // PT, n % PT
                    pe.wait_ge(exp_done, n + 1)
                    if n >= 1:
                        pe.wait_ge(pta, n)
                        pe.wait_ge(ptb, wide_before(n))
                    for j in range(i + 1):
                        last = nc.tensor.transpose(tpp[:, j, :], pr[:, n % 2, j * P:(j + 1) * P], ident[:, :])
                    last.then_inc(t_done, 1)

                def values(n):
                    h, i = n // PT, n % PT
                    pe.wait_ge(pta, n + 1)
                    pe.wait_ge(ptb, wide_before(n + 1))
                    if n >= 1:
                        pe.wait_ge(norm_done, n)
                    b0 = 64 * (h % 2)
                    for j in range(i + 1):
                        last = nc.tensor.matmul(ov[b0:b0 + 64, :], vn[:, j, h * HD:(h + 1) * HD], pT[:, n % 2, j, :],
                                                start=(j == 0), stop=(j == i))
                    last.then_inc(pv_done, 1)

                def turn_outputs(r, half):
                    pe.wait_ge(norm_done, PT * (2 * r + 2))
                    pe.wait_ge(cb_ev, min(4 * r + 8, 2 * NH))
                    if half:
                        pe.wait_ge(ofin, 2 * r + 1)
                    for q in range(4):
                        last = nc.tensor.transpose(cbp[:, q * P:(q + 1) * P], oTs[:, r % 2, 4 * half + q, :], ident[:, :])
                    last.then_inc(otr_mm, 1)

                pe.wait_ge(e_in, 32)
                pe.wait_ge(c_done, 1)
                decay_rows(0)
                decay_rows(1)
                for n in range(NSTEP + 3):
                    if n < NSTEP:
                        scores(n)
                        if n % PT in (3, 4) and n // PT < NH - 1:
                            decay_rows(2 * (n // PT) + n % PT - 1)
                    if 2 <= n < NSTEP + 2:
                        turn(n - 2)
                    if n >= 3:
                        values(n - 3)
                    if n // PT in (2, 4, 6) and n % PT in (5, 6):
                        turn_outputs(n // PT // 2 - 1, n % PT - 5)
                for half in range(2):
                    turn_outputs(PAIRS - 1, half)
                pe.wait_ge(cs_done, 1)
                pe.wait_ge(qb_done, 2)
                pe.wait_ge(vn_in, 16 * NB)
                kTp = sp_[0][:, :].rearrange("p (r n) -> p r n", r=PAIRS)
                pe.wait_ge(ttr_done, NSTEP)

                def sample_scores(b):
                    pe.wait_ge(ck_in[b % 2], 16 * (b // 2 + 1))
                    if b >= 1:
                        pe.wait_ge(kt_ev, b)
                    for r in range(PAIRS):
                        for j in range(2):
                            last = nc.tensor.transpose(kTp[:, r, j * P:(j + 1) * P], ck[:, b % 2, j, r * P:(r + 1) * P],
                                                       ident[:, :])
                    last.then_inc(kt_mm, 1)
                    S = S2[b % 2]
                    if b >= 2:
                        pe.wait_ge(sexp, b - 1)
                    nc.tensor.matmul(S, e64[:, b, :], cs, start=True, stop=False, skip_group_check=True)
                    nc.tensor.matmul(S[:, PAST:PAST + NS], identb[:, :], maskn[:, :], start=False, stop=False,
                                     skip_group_check=True)
                    pe.wait_ge(kt_ev, b + 1)
                    for r in range(PAIRS):
                        o = 32 * r
                        lhs = qbd[:, r, b].rearrange("p a q -> p (a q)")
                        nc.tensor.matmul(S[o:o + 32, 0:PAST], lhs, ckT[:, r, :], start=False, stop=False,
                                         skip_group_check=True)
                        last = nc.tensor.matmul(S[o:o + 32, PAST:PAST + NS], lhs,
                                                kT[:, r, NP_TOK + b * NS:NP_TOK + (b + 1) * NS],
                                                start=False, stop=True, skip_group_check=True)
                    last.then_inc(ss_done, 1)

                def sample_values(b):
                    pe.wait_ge(spn, b + 1)
                    if b >= 1:
                        pe.wait_ge(st_ev, 2 * b)
                    for j in range(2):
                        nc.tensor.transpose(tpp[:, j, :], pns[:, j * P:(j + 1) * P], ident[:, :])
                    nc.tensor.transpose(tpp[0:NS, 2, :], pns[:, PAST:PAST + NS], ident[:, :]).then_inc(st_mm, 1)
                    pe.wait_ge(cv_in[b % 2], 16 * (b // 2 + 1))
                    pe.wait_ge(st_ev, 2 * b + 2)
                    if b >= 1:
                        pe.wait_ge(so_ev, 2 * b)
                    for r in range(PAIRS):
                        o = cbp[:, 32 * r:32 * r + 32]
                        for j in range(2):
                            nc.tensor.matmul(o, cv[:, b % 2, j, r * P:(r + 1) * P], psT[:, j, 32 * r:32 * r + 32],
                                             start=(j == 0), stop=False)
                        last = nc.tensor.matmul(o, vnew[:, b, r * P:(r + 1) * P], psT[0:NS, 2, 32 * r:32 * r + 32],
                                                start=False, stop=True)
                    last.then_inc(so_mm, 1)

                sample_scores(0)
                for b in range(NB):
                    if b + 1 < NB:
                        sample_scores(b + 1)
                    sample_values(b)
                pe.wait_ge(so_ev, 2 * NB)
                for r in range(PAIRS):
                    last = nc.tensor.transpose(tpp[:, r, :], foT[:, r, :], ident[:, :])
                last.then_inc(fT_mm, 1)

            @block.scalar
            def _(act):
                def rows(m):
                    act.wait_ge(cb_mm, m + 1)
                    h, half = m // 2, m % 2
                    if h >= 2:
                        act.wait_ge(ttr_done, PT * (h - 1))
                    nc.scalar.copy(cB[:, h % 2, 512 * half:512 * half + 512], cbp[:, :]).then_inc(cb_ev, 1)

                act.wait_ge(lf_in, 16 * (NB + 1))
                rows(0)
                rows(1)
                for n in range(NSTEP + 2):
                    if n >= 2:
                        m = n - 2
                        act.wait_ge(t_done, m + 1)
                        j = min(4, m % PT + 1)
                        if m >= 2:
                            act.wait_ge(pv_done, m - 1)
                        nc.scalar.copy(pT[:, m % 2, 0:j, :], tpp[:, 0:j, :]).then_inc(pta, 1)
                    if n < NSTEP:
                        w = (n % PT + 1) * P
                        act.wait_ge(ttr_done, n + 1)
                        if n >= 4:
                            act.wait_ge(rl_done, n - 3)
                        nc.scalar.activation(pr[:, n % 2, 0:w], sN[:, n % 2, 0:w], ACT.Exp, bias=mn[:, n % 4, 0:1],
                                             scale=-1.0, accum_out=mn[:, n % 4, 1:2]).then_inc(exp_done, 1)
                        if n % PT in (3, 4) and n // PT < NH - 1:
                            rows(2 * (n // PT) + n % PT - 1)

                def copy_keys(b):
                    act.wait_ge(kt_mm, b + 1)
                    if b >= 1:
                        act.wait_ge(ss_done, b)
                    nc.scalar.copy(ckT, sp_[0][:, :].rearrange("p (r n) -> p r n", r=PAIRS)).then_inc(kt_ev, 1)

                def sample_exp(b):
                    act.wait_ge(smin, b + 1)
                    if b >= 1:
                        act.wait_ge(spn, b)
                    nc.scalar.activation(pn, S2[b % 2], ACT.Exp, bias=mn[:, 0, 0:1], scale=-1.0,
                                         accum_out=mn[:, 0, 1:2]).then_inc(sexp, 1)

                copy_keys(0)
                sample_exp(0)
                for b in range(NB):
                    if b + 1 < NB:
                        copy_keys(b + 1)
                    act.wait_ge(st_mm, b + 1)
                    if b >= 1:
                        act.wait_ge(so_mm, b)
                    nc.scalar.copy(psT[:, 0:2, :], tpp[:, 0:2, :]).then_inc(st_ev, 1)
                    nc.scalar.copy(psT[0:NS, 2, :], tpp[0:NS, 2, :]).then_inc(st_ev, 1)
                    if b + 1 < NB:
                        sample_exp(b + 1)
                act.wait_ge(fT_mm, 1)
                nc.scalar.copy(mixo[:, ST, GW:], tpp[:, 0:4, :].rearrange("p r e -> p (r e)"))

            @block.gpsimd
            def _(pool):
                nc.gpsimd.memset(ones, 1.0).then_inc(ones_set, 1)
                nc.gpsimd.memset(Xreg[:, 0:1024], 0.0).then_inc(qz, 1)

            @block.vector
            def _(dve):
                dve.wait_ge(ones_set, 1)
                nc.vector.tensor_tensor_scan(out=csum, data0=ones[0:NH, :], data1=lgfT[:, 0:NP_TOK],
                                             initial=0.0, op0=ALU.mult, op1=ALU.add).then_inc(c_done, 1)
                dve.wait_ge(lf_in, 16 * (NB + 1))
                nc.vector.tensor_tensor_scan(out=cs, data0=ones[0:64, 0:272], data1=lfs,
                                             initial=0.0, op0=ALU.mult, op1=ALU.add).then_inc(cs_done, 1)
                dve.wait_ge(qz, 1)
                for par in range(2):
                    o = 64 * par
                    for r in range(PAIRS):
                        last = nc.vector.tensor_copy(qbd[o:o + 64, r, :, par, :],
                                                     qT[o:o + 64, r, NP_TOK:].rearrange("p (b q) -> p b q", q=NS))
                    last.then_inc(qb_done, 1)

                def finish_outputs(r, half):
                    dve.wait_ge(otr_mm, 2 * r + half + 1)
                    dve.wait_ge(rl_done, PT * (2 * r + 2))
                    c = GW + 2 * r * HD
                    nc.vector.tensor_tensor(
                        mixo[:, 4 * half:4 * half + 4, c:c + 2 * HD].rearrange("p i (a d) -> p i a d", a=2),
                        cbp[:, :].rearrange("p (i a d) -> p i a d", i=4, a=2),
                        bc(inv[:, 4 * half:4 * half + 4, 2 * r:2 * r + 2].unsqueeze(3), [P, 4, 2, HD]),
                        ALU.mult).then_inc(ofin, 1)

                for n in range(NSTEP + 3):
                    if n < NSTEP:
                        h, w = n // PT, (n % PT + 1) * P
                        if n % PT == 0:
                            dve.wait_ge(cb_ev, 2 * h + 2)
                        dve.wait_ge(s_done, n + 1)
                        if n >= 2:
                            dve.wait_ge(exp_done, n - 1)
                        nc.vector.tensor_tensor_reduce(out=sN[:, n % 2, 0:w], in0=sp_[n % 2][:, 0:w],
                                                       in1=cB[:, h % 2, 0:w], scale=1.0, scalar=3e38,
                                                       op0=ALU.add, op1=ALU.min,
                                                       accum_out=mn[:, n % 4, 0:1]).then_inc(ttr_done, 1)
                    if 2 <= n < NSTEP + 2:
                        m = n - 2
                        dve.wait_ge(exp_done, m + 1)
                        nc.vector.reciprocal(inv[:, m % PT, m // PT:m // PT + 1],
                                             mn[:, m % 4, 1:2]).then_inc(rl_done, 1)
                        if m % PT >= 4:
                            j = m % PT + 1
                            dve.wait_ge(t_done, m + 1)
                            if m >= 2:
                                dve.wait_ge(pv_done, m - 1)
                            nc.vector.tensor_copy(pT[:, m % 2, 4:j, :], tpp[:, 4:j, :]).then_inc(ptb, 1)
                    if n >= 3:
                        m = n - 3
                        h, i = m // PT, m % PT
                        dve.wait_ge(pv_done, m + 1)
                        if h % 2 == 0 and h >= 4 and i == 0:
                            dve.wait_ge(otr_mm, h - 2)
                        b0 = 64 * (h % 2)
                        nc.vector.tensor_copy(oTs[b0:b0 + 64, (h // 2) % 2, i, :], ov[b0:b0 + 64, :]).then_inc(norm_done, 1)
                    if n // PT in (2, 4, 6) and n % PT in (5, 6):
                        finish_outputs(n // PT // 2 - 1, n % PT - 5)
                for half in range(2):
                    finish_outputs(PAIRS - 1, half)

                def sample_softmax(b):
                    dve.wait_ge(ss_done, b + 1)
                    nc.vector.tensor_reduce(mn[:, 0, 0:1], S2[b % 2], AX.X, ALU.min).then_inc(smin, 1)
                    dve.wait_ge(sexp, b + 1)
                    nc.vector.reciprocal(mn[:, 0, 2:3], mn[:, 0, 1:2]).then_inc(srl, 1)
                    dve.wait_ge(srl, b + 1)
                    if b >= 1:
                        dve.wait_ge(st_mm, b)
                    nc.vector.tensor_scalar(pns, pn, mn[:, 0, 2:3], None, ALU.mult).then_inc(spn, 1)

                sample_softmax(0)
                for b in range(NB):
                    if b + 1 < NB:
                        sample_softmax(b + 1)
                    dve.wait_ge(so_mm, b + 1)
                    for par in range(2):
                        o = 64 * par
                        nc.vector.tensor_copy(foT[o:o + 64, :, b * NS:(b + 1) * NS],
                                              cbp[o:o + 64, 0:P].rearrange("p (r a q) -> p r a q", r=PAIRS, a=2)
                                              [:, :, par, :]).then_inc(so_ev, 1)

        wout = Wreg[:, :].rearrange("p (k c) -> p k c", k=KC)
        NSEG = 2 * PH
        wq = Rreg[:, 0:KC * 2048].rearrange("p (k c) -> p k c", k=KC)
        keysT = Rreg[:, 16384:18432].rearrange("p (s n) -> p s n", s=NSEG)

        def phase_peer(block, sem, ps):
            NU = NV = 8
            NI, ND = 4, 4
            xns, xcur, xb = (Hreg[:, i * D:(i + 1) * D] for i in (0, 1, 3))
            xT = Hreg[:, 4096:5120].rearrange("p (k n) -> p k n", k=KC)
            qTs = Hreg[:, 5120:7168].rearrange("p (s n) -> p s n", s=NSEG)
            sc = Hreg[:, 7168:9216].rearrange("p (s n) -> p s n", s=NSEG)
            sc2 = qTs
            mflat = mixo[:, :, :].rearrange("p t c -> p (t c)")
            vb = mflat[:, 0:NV * D].rearrange("p (s d) -> p s d", s=NV)
            junk = mflat[:, NV * D:(NV + 1) * D]
            ub = Wreg[:, 0:NU * D].rearrange("p (s d) -> p s d", s=NU)
            idx2 = Xreg[:, 0:2 * P].bitcast(I32)
            gate2 = Xreg[:, 2 * P:4 * P]
            X0 = 4 * P
            vals = Xreg[:, X0:X0 + 256].rearrange("p (s n) -> p s n", s=NSEG)
            idx = Xreg[:, X0 + 256:X0 + 512].bitcast(U32).rearrange("p (s n) -> p s n", s=NSEG)
            fidx = Xreg[:, X0 + 512:X0 + 768].rearrange("p (s n) -> p s n", s=NSEG)
            cval = Xreg[:, X0 + 768:X0 + 896].rearrange("p (h n) -> p h n", h=PH)
            ci = Xreg[:, X0 + 896:X0 + 1024].bitcast(U32).rearrange("p (h n) -> p h n", h=PH)
            cia = Xreg[:, X0 + 1024:X0 + 1152].bitcast(U32)
            cif = Xreg[:, X0 + 1152:X0 + 1408].rearrange("p (a n) -> p a n", a=2)
            sel = Xreg[:, X0 + 1408:X0 + 1664].rearrange("p (a n) -> p a n", a=2)
            ef = Xreg[:, X0 + 1664:X0 + 1792].rearrange("p (h n) -> p h n", h=PH)
            ssum = Xreg[:, X0 + 1792:X0 + 1808]
            cand = Xreg[:, X0 + 1808:X0 + 3856].rearrange("p (h n) -> p h n", h=PH)
            islot = sb("islot", [P, NI, TOPK], I32)
            dots, gw = sb("dots", [P, 2, TOPK]), sb("gw", [P, 2, TOPK])
            g1, g2 = sb("g1", [P, TOPK]), sb("g2", [P, TOPK])
            diag = sb("diag", [P, ND, P])
            tp = ps("btp", [P, 8, P])
            qp = [ps(f"qp{i}", [P, 4, P]) for i in range(2)]
            spp = [ps(f"spp{i}", [P, 4, P]) for i in range(2)] + qp
            yp = ps("yp", [P, D])
            qflat = [b[:, :, :].rearrange("p a b -> p (a b)") for b in qp]
            qsb = cand.rearrange("p h n -> p (h n)")[:, 0:1024].rearrange("p (s c) -> p s c", s=2)
            QUERY_STEPS = [[("q", 0), ("q", 1), ("t", 0)], [("q", 2), ("t", 1), ("q", 3), ("t", 2), ("t", 3)]]
            xt = [Hreg[:, (1 + i) * D:(2 + i) * D] for i in range(2)]
            mT = [mixo[:, t, :].rearrange("p (k n) -> p k n", k=KC) for t in range(TILES)]
            xn = [mixo[:, t, :] for t in range(TILES)]
            sq = diag[:, :, :].rearrange("p a b -> p (a b)")
            oy = [[yp[:, 0:512], yp[:, 512:1024]],
                  [spp[i][:, :, :].rearrange("p a b -> p (a b)") for i in range(2)]]
            w_in, x_in, wq_in = [sem(f"w_in{k}") for k in range(KC)], [sem("x_in0"), sem("x_in1")], sem("wq_in")
            sq_done, ss_done, rs_done, mix_done = sem("sq_done"), sem("ss_done"), sem("rs_done"), sem("mix_done")
            t_mm, ev_a, ev_v, y_mm, x1_done = sem("t_mm"), sem("ev_a"), sem("ev_v"), sem("y_mm"), sem("x1_done")
            pstep, vlink, g2_in = sem("pstep"), sem("vlink"), sem("g2_in")
            xsq, xrs, xn_done = sem("xsq"), sem("xrs"), sem("xn_done")
            x1_out, xn_out = [sem("x1_out0"), sem("x1_out1")], [sem("xn_out0"), sem("xn_out1")]

            u_in = [sem(f"u_in{i}") for i in range(NU)]
            v_in = [sem(f"v_in{i}") for i in range(NV)]
            u_used, v_used, idx_done = sem("u_used"), sem("v_used"), sem("idx_done")
            gel1, gel2, gw_done, diag_done, elink = (sem(x) for x in ("gel1", "gel2", "gw_done", "diag_done", "elink"))
            xcopy, y_out, xb_in, out_done = sem("xcopy"), sem("y_out"), sem("xb_in"), sem("out_done")
            names = ("xn_in", "xt_mm", "xt_ev", "q_mm", "q_cp", "qt_mm", "q_ev", "s_mm", "s_ev",
                     "csub", "gexp", "rlink", "route_done")
            R = {n: sem("r_" + n) for n in names}
            ROUTE0 = 2
            RLINKS, ELINKS = 22, 6
            u_tab, v_tab = a["peer_u"][0], a["peer_v"][0]

            def turns(engine, first, inner, last):
                first(0)
                with engine.Fori(1, TILES - 1) as t:
                    inner(t)
                last(TILES - 1)

            def wait(engine, semaphore, value):
                if isinstance(value, int):
                    engine.wait_ge(semaphore, value)
                else:
                    after(engine, semaphore, value)

            @block.sync
            def _(sp):
                def load_route(t):
                    wait(sp, R["xt_mm"], t)
                    wait(sp, xcopy, t)
                    sp.dma_start(xns, a["xn"][bass.ds(t, 1)].rearrange("a p d -> (a p) d")).then_inc(R["xn_in"], 16)

                def store(t):
                    wait(sp, y_out, t + 1)
                    dst = a["y_sample"].rearrange("b t d -> (b t) d") if isinstance(t, int) and t == ST else \
                        a["y_prompt"][0, bass.ds(t * P, P), :]
                    sp.dma_start(dst, xb).then_inc(out_done, 16)
                    wait(sp, out_done, 16 * t + 16)

                def load_final(t):
                    sp.dma_start(xb, a["x1"][bass.ds(t, 1)].rearrange("a p d -> (a p) d")).then_inc(xb_in, 16)

                for k in range(KC):
                    sp.dma_start(wout[:, k, :], a["w_out"][0, k * P:(k + 1) * P, :]).then_inc(w_in[k], 16)
                for t in range(2):
                    sp.dma_start(xt[t], a["x_prompt"][0, t * P:(t + 1) * P, :]).then_inc(x_in[t], 16)
                sp.dma_start(grow[:, :], a["norm2_g"].partition_broadcast(P)
                             .rearrange("p a c -> p (a c)")).then_inc(g2_in, 16)
                for k in range(KC):
                    sp.dma_start(wq[:, k, :], a["peer_wq"][0, k * P:(k + 1) * P, :]).then_inc(wq_in, 16)
                sp.dma_start(keysT, a["keys_t"]).then_inc(wq_in, 16)
                for t in range(TILES):
                    sp.wait_ge(x1_done, t + 1)
                    sp.dma_start(a["x1"][t], xt[t % 2]).then_inc(x1_out[t % 2], 16)
                    sp.wait_ge(xn_done, t + 1)
                    sp.dma_start(a["xn"][t], xn[t]).then_inc(xn_out[t % 2], 16)
                    if t + 2 < TILES:
                        sp.wait_ge(x1_out[t % 2], 16 * (t // 2 + 1))
                        src = a["x_prompt"][0, (t + 2) * P:(t + 3) * P, :] if t + 2 < PT else \
                            a["x_sample"].rearrange("b t d -> (b t) d")
                        sp.dma_start(xt[t % 2], src).then_inc(x_in[t % 2], 16)
                    if t == 0:
                        sp.wait_ge(xn_out[0], 16)
                        sp.wait_ge(x1_out[0], 16)
                        sp.dma_start(xns, a["xn"][0]).then_inc(R["xn_in"], 16)
                        sp.dma_start(xb, a["x1"][0]).then_inc(xb_in, 16)
                for i in range(2):
                    sp.wait_ge(xn_out[i], 16 * (5 - i))
                    sp.wait_ge(x1_out[i], 16 * (5 - i))

                def turn0(t):
                    load_route(t + 1)

                def turn(t):
                    load_route(t + 1)
                    store(t - 1)
                    load_final(t)

                def turn_last(t):
                    store(t - 1)
                    load_final(t)
                    store(t)

                turns(sp, turn0, turn, turn_last)

            @block.gpsimd
            def _(pool):
                def load_numbers(t, h):
                    g = t * PH + h
                    if h == 0:
                        wait(pool, R["route_done"], t + 1)
                    if not (isinstance(g, int) and g < NI):
                        wait(pool, v_used, (g - NI + 1) * TOPK)
                    nc.gpsimd.tensor_copy(islot[:, h % NI, :],
                                          idx2[:, bass.ds((t % 2) * P + h * TOPK, TOPK)]).then_inc(idx_done, 1)
                    wait(pool, idx_done, g + 1)

                def gather_u(t, h, i):
                    g = t * PH + h
                    if not (isinstance(g, int) and g == 0 and i < NU):
                        wait(pool, u_used, g * TOPK + i - NU + 1)
                    nc.gpsimd.indirect_dma_start(
                        ub[:, i % NU, :], None, u_tab,
                        bass.IndirectOffsetOnAxis(ap=islot[:, h % NI, i:i + 1], axis=0)).then_inc(u_in[i % NU], 16)

                def gather_v(t, h, i):
                    g = t * PH + h
                    if not (isinstance(g, int) and g == 0 and i < NV):
                        wait(pool, v_used, g * TOPK + i - NV + 1)
                    nc.gpsimd.indirect_dma_start(
                        vb[:, i % NV, :], None, v_tab,
                        bass.IndirectOffsetOnAxis(ap=islot[:, h % NI, i:i + 1], axis=0)).then_inc(v_in[i % NV], 16)

                def turn(t, first=False, last=False):
                    for h in range(PH):
                        load_numbers(t, h)
                        for i in range(TOPK):
                            gather_u(t, h, i)
                            if h:
                                gather_v(t, h - 1, i)
                            elif not first:
                                gather_v(t - 1, PH - 1, i)

                steps_done = [0]

                def rsqrt(out, tmp, ssq, scale, half, done):
                    nc.gpsimd.tensor_scalar(tmp, ssq, scale, EPS, ALU.mult, ALU.add).then_inc(pstep, 1)
                    steps_done[0] += 1
                    pool.wait_ge(pstep, steps_done[0])
                    nc.gpsimd.tensor_tensor(out, tmp, half, ALU.pow).then_inc(done, 1)

                for t in range(TILES + 2):
                    if t >= 2:
                        pool.wait_ge(xsq, t - 1)
                        rsqrt(small[:, 60:61], small[:, 58:59], small[:, 56:57], 1.0 / D, nhalf[:, 0:1], xrs)
                    for m in (2 * t, 2 * t + 1):
                        if m < TILES:
                            o = 8 * (m % 2)
                            pool.wait_ge(ss_done, m + 1)
                            rsqrt(small[:, 32 + o:40 + o], small[:, 16 + o:24 + o], small[:, o:o + 8], 1.0 / HD,
                                  nhalf[:, :], rs_done)
                pool.wait_ge(y_mm, TILES)
                for i in range(2):
                    pool.wait_ge(xn_out[i], 16 * (5 - i))
                turns(pool, lambda t: turn(t, first=True), turn, turn)
                for i in range(TOPK):
                    gather_v(TILES - 1, PH - 1, i)

            @block.scalar
            def _(act):
                def evacuate_x(t):
                    wait(act, R["xt_mm"], t + 1)
                    nc.scalar.copy(xT[:, 0:4, :], tp[:, 0:4, :])
                    nc.scalar.copy(xT[:, 4:8, :], tp[:, 4:8, :]).then_inc(R["xt_ev"], 1)

                def copy_q(t, b):
                    wait(act, R["q_mm"], 4 * t + b + 1)
                    nc.scalar.copy(qsb[:, b % 2, :], qflat[b % 2]).then_inc(R["q_cp"], 1)

                def evacuate_q(t, b):
                    wait(act, R["qt_mm"], 4 * t + b + 1)
                    nc.scalar.copy(qTs[:, 4 * b:4 * b + 4, :], spp[b % 2][:, :, :]).then_inc(R["q_ev"], 1)

                def move_q(t, part):
                    for f, b in QUERY_STEPS[part]:
                        (copy_q if f == "q" else evacuate_q)(t, b)

                def evacuate_s(t, b):
                    wait(act, R["s_mm"], 4 * t + b + 1)
                    nc.scalar.copy(sc[:, 4 * b:4 * b + 4, :], spp[b][:, :, :]).then_inc(R["s_ev"], 1)

                def gate_exp(t):
                    wait(act, R["csub"], t + 1)
                    nc.scalar.activation(ef, ef, ACT.Exp).then_inc(R["gexp"], 1)

                def gelu_exp(t, h):
                    wait(act, gel1, t * PH + h + 1)
                    nc.scalar.activation(g2[:, :], g1[:, :], ACT.Exp, scale=-1.0).then_inc(gel2, 1)

                def diagonals(t, h):
                    g = t * PH + h
                    wait(act, gw_done, g + 1)
                    for i in range(TOPK):
                        if not (isinstance(g, int) and g == 0 and i < ND):
                            wait(act, v_used, g * TOPK + i - ND + 1)
                        nc.scalar.activation(diag[:, i % ND, :], ident[:, :], ACT.Copy,
                                             scale=gw[:, h % 2, i:i + 1]).then_inc(diag_done, 1)

                def turn(t, first=False, last=False):
                    for h in range(PH):
                        if h:
                            diagonals(t, h - 1)
                        elif not first:
                            diagonals(t - 1, PH - 1)
                        gelu_exp(t, h)
                        if not last:
                            if h == 0:
                                evacuate_x(t + 1)
                            elif h in (1, 2):
                                move_q(t + 1, h - 1)
                            elif h == 3:
                                for b in range(4):
                                    evacuate_s(t + 1, b)
                            elif h == 6:
                                gate_exp(t + 1)

                def square(t):
                    act.wait_ge(x1_done, t + 1)
                    if t >= 1:
                        act.wait_ge(xrs, t)
                    nc.scalar.activation(xn[t], xt[t % 2], ACT.Square, accum_out=small[:, 56:57]).then_inc(xsq, 1)

                for t in range(TILES + 2):
                    if 1 <= t <= TILES:
                        act.wait_ge(t_mm, t)
                        nc.scalar.copy(mT[t - 1][:, 0:4, :], tp[:, 0:4, :]).then_inc(ev_a, 1)
                    if t == ROUTE0 + 1:
                        evacuate_x(0)
                    if t == ROUTE0 + 3:
                        move_q(0, 0)
                        move_q(0, 1)
                        for b in range(4):
                            evacuate_s(0, b)
                    if t == TILES + 1:
                        gate_exp(0)
                    if t >= 2:
                        square(t - 2)
                    for m in (2 * t, 2 * t + 1):
                        if m < TILES:
                            if m >= 1:
                                act.wait_ge(ss_done, m)
                            nc.scalar.activation(sq, mixo[:, m, GW:], ACT.Square).then_inc(sq_done, 1)
                turns(act, lambda t: turn(t, first=True), turn, lambda t: turn(t, last=True))
                diagonals(TILES - 1, PH - 1)

            @block.tensor
            def _(pe):
                def turn_x(t, src=xns):
                    for k in range(KC):
                        last = nc.tensor.transpose(tp[:, k, :], src[:, k * P:(k + 1) * P], ident[:, :])
                    last.then_inc(R["xt_mm"], 1)

                def query(t, b):
                    if b == 0:
                        pe.wait_ge(R["xt_ev"], t + 1)
                    if b >= 2:
                        pe.wait_ge(R["q_cp"], 4 * t + b - 1)
                    elif not (isinstance(t, int) and t == 0):
                        pe.wait_ge(R["s_ev"], 4 * t)
                    for k in range(KC):
                        last = nc.tensor.matmul(qflat[b % 2], xT[:, k, :], wq[:, k, 512 * b:512 * b + 512],
                                                start=(k == 0), stop=(k == KC - 1))
                    last.then_inc(R["q_mm"], 1)

                def turn_q(t, b):
                    pe.wait_ge(R["q_cp"], 4 * t + b + 1)
                    if b >= 2:
                        pe.wait_ge(R["q_ev"], 4 * t + b - 1)
                    for i in range(4):
                        last = nc.tensor.transpose(spp[b % 2][:, i, :], qsb[:, b % 2, i * P:(i + 1) * P], ident[:, :])
                    last.then_inc(R["qt_mm"], 1)

                def queries(t, part):
                    for f, b in QUERY_STEPS[part]:
                        (query if f == "q" else turn_q)(t, b)

                def key_scores(t):
                    pe.wait_ge(R["q_ev"], 4 * t + 4)
                    for b in range(4):
                        for i in range(4):
                            s = 4 * b + i
                            last = nc.tensor.matmul(spp[b][:, i, :], qTs[:, s, :], keysT[:, s, :],
                                                    start=True, stop=True)
                        last.then_inc(R["s_mm"], 1)

                def add_v(t, h):
                    g = t * PH + h
                    if h == 0 and not (isinstance(t, int) and t == 0):
                        pe.wait_ge(y_out, t)
                    for i in range(TOPK):
                        pe.wait_ge(v_in[i % NV], 32 * g + 16 * (i // NV) + 16)
                        pe.wait_ge(diag_done, g * TOPK + i + 1)
                        for c in range(2):
                            last = nc.tensor.matmul(yp[:, 512 * c:512 * c + 512], diag[:, i % ND, :],
                                                    vb[:, i % NV, 512 * c:512 * c + 512],
                                                    start=(h == 0 and i == 0), stop=(h == PH - 1 and i == TOPK - 1))
                        last.then_inc(v_used, 1)

                def turn(t, first=False, last=False):
                    for h in range(PH):
                        if h:
                            add_v(t, h - 1)
                        elif not first:
                            add_v(t - 1, PH - 1)
                        if not last:
                            if h == 0:
                                pe.wait_ge(R["xn_in"], 16 * t + 32)
                                turn_x(t + 1)
                            elif h in (1, 2):
                                queries(t + 1, h - 1)
                            elif h == 3:
                                key_scores(t + 1)

                def turn_mix(t):
                    pe.wait_ge(mix_done, t + 1)
                    if t >= 1:
                        pe.wait_ge(ev_a, t)
                        pe.wait_ge(ev_v, t)
                    for k in range(KC):
                        last = nc.tensor.transpose(tp[:, k, :], mixo[:, t, k * P:(k + 1) * P], ident[:, :])
                    last.then_inc(t_mm, 1)

                turn_mix(0)
                for t in range(TILES):
                    pe.wait_ge(ev_a, t + 1)
                    pe.wait_ge(ev_v, t + 1)
                    if t == ROUTE0:
                        pe.wait_ge(xn_done, 1)
                        turn_x(0, xn[0])
                        pe.wait_ge(R["xt_ev"], 1)
                    if t + 1 < TILES:
                        turn_mix(t + 1)
                    if t == ROUTE0 + 1:
                        pe.wait_ge(wq_in, 16 * (KC + 1))
                        pe.wait_ge(x1_done, t - 1)
                        queries(0, 0)
                        queries(0, 1)
                        key_scores(0)
                        pe.wait_ge(R["s_ev"], 4)
                    if t >= 2:
                        pe.wait_ge(x1_done, t - 1)
                    for c in range(2):
                        for k in range(KC):
                            if t == 0 and c == 0:
                                pe.wait_ge(w_in[k], 16)
                            last = nc.tensor.matmul(oy[t % 2][c], mT[t][:, k, :], wout[:, k, 512 * c:512 * c + 512],
                                                    start=(k == 0), stop=(k == KC - 1))
                    last.then_inc(y_mm, 1)
                pe.wait_ge(x1_done, TILES)
                turns(pe, lambda t: turn(t, first=True), turn, lambda t: turn(t, last=True))
                add_v(TILES - 1, PH - 1)

            @block.vector
            def _(dve):
                def dot(t, h, between):
                    g = t * PH + h
                    for i in range(TOPK):
                        if i in between:
                            between[i]()
                        wait(dve, u_in[i % NU], 32 * g + 16 * (i // NU) + 16)
                        nc.vector.scalar_tensor_tensor(out=junk, in0=ub[:, i % NU, :], scalar=1.0, in1=xcur,
                                                       op0=ALU.mult, op1=ALU.mult,
                                                       accum_out=dots[:, h % 2, i:i + 1]).then_inc(u_used, 1)
                        wait(dve, u_used, g * TOPK + i + 1)

                def weights(t, h):
                    g = t * PH + h
                    x = dots[:, h % 2, :]
                    k = [0]

                    def link(ins):
                        k[0] += 1
                        ins.then_inc(elink, 1)
                        wait(dve, elink, ELINKS * g + k[0])

                    link(nc.vector.tensor_tensor(g1[:, :], x, x, ALU.mult))
                    link(nc.vector.tensor_scalar(g1[:, :], g1[:, :], GELU_C * 0.044715, GELU_C, ALU.mult, ALU.add))
                    link(nc.vector.tensor_tensor(g1[:, :], g1[:, :], x, ALU.mult))
                    nc.vector.tensor_scalar_max(g1[:, :], g1[:, :], -80.0).then_inc(gel1, 1)
                    wait(dve, gel2, g + 1)
                    link(nc.vector.tensor_scalar_add(g1[:, :], g2[:, :], 1.0))
                    link(nc.vector.reciprocal(g1[:, :], g1[:, :]))
                    link(nc.vector.tensor_tensor(g1[:, :], g1[:, :], x, ALU.mult))
                    if not (isinstance(g, int) and g < 2):
                        wait(dve, diag_done, (g - 1) * TOPK)
                    nc.vector.tensor_tensor(gw[:, h % 2, :], g1[:, :],
                                            gate2[:, bass.ds((t % 2) * P + h * TOPK, TOPK)],
                                            ALU.mult).then_inc(gw_done, 1)
                    assert k[0] == ELINKS

                def finish(t):
                    wait(dve, v_used, (t + 1) * P)
                    wait(dve, xb_in, 16 * t + 16)
                    nc.vector.tensor_tensor(xb, yp[:, :], xb, ALU.add).then_inc(y_out, 1)

                rcount = [0]

                def rlink(t, ins):
                    rcount[0] += 1
                    ins.then_inc(R["rlink"], 1)
                    wait(dve, R["rlink"], RLINKS * t + rcount[0])

                def keep_x(t):
                    wait(dve, R["xn_in"], 16 * t + 16)
                    nc.vector.tensor_copy(xcur, xns).then_inc(xcopy, 1)
                    wait(dve, xcopy, t + 1)

                def top_keys(t, part):
                    if part == 0:
                        wait(dve, R["s_ev"], 4 * t + 4)
                        for s in range(NSEG):
                            last = nc.vector.max(vals[:, s, 0:8], sc[:, s, :])
                        rlink(t, last)
                        for s in range(NSEG):
                            nc.vector.max_index(idx[:, s, 0:8], vals[:, s, 0:8], sc[:, s, :])
                            last = nc.vector.match_replace(sc2[:, s, :], vals[:, s, 0:8], sc[:, s, :], -3e38)
                        rlink(t, last)
                    else:
                        for s in range(NSEG):
                            last = nc.vector.max(vals[:, s, 8:16], sc2[:, s, :])
                        rlink(t, last)
                        for s in range(NSEG):
                            last = nc.vector.max_index(idx[:, s, 8:16], vals[:, s, 8:16], sc2[:, s, :])
                        rlink(t, last)

                def top_sums(t, part):
                    cand2 = sc2.rearrange("p (h a) n -> p h (a n)", a=2)
                    if part == 0:
                        v4 = vals.rearrange("p (h a) n -> p h a n", a=2)
                        nc.vector.tensor_copy(fidx, idx)
                        rlink(t, nc.vector.tensor_tensor(cand.rearrange("p h (i j) -> p h i j", i=TOPK),
                                                         bc(v4[:, :, 0, :].unsqueeze(3), [P, PH, TOPK, TOPK]),
                                                         bc(v4[:, :, 1, :].unsqueeze(2), [P, PH, TOPK, TOPK]),
                                                         ALU.add))
                        for h in range(PH):
                            last = nc.vector.max(cval[:, h, 0:8], cand[:, h, :])
                        rlink(t, last)
                    elif part == 1:
                        for h in range(PH):
                            nc.vector.max_index(ci[:, h, 0:8], cval[:, h, 0:8], cand[:, h, :])
                            last = nc.vector.match_replace(cand2[:, h, :], cval[:, h, 0:8], cand[:, h, :], -3e38)
                        rlink(t, last)
                        for h in range(PH):
                            last = nc.vector.max(cval[:, h, 8:16], cand2[:, h, :])
                        rlink(t, last)
                    else:
                        for h in range(PH):
                            last = nc.vector.max_index(ci[:, h, 8:16], cval[:, h, 8:16], cand2[:, h, :])
                        rlink(t, last)
                        cflat = ci.rearrange("p h n -> p (h n)")
                        rlink(t, nc.vector.tensor_scalar(cia, cflat, 4, None, ALU.logical_shift_right))
                        rlink(t, nc.vector.tensor_copy(cif[:, 0, :], cia))
                        rlink(t, nc.vector.tensor_scalar(cia, cflat, 15, None, ALU.bitwise_and))
                        rlink(t, nc.vector.tensor_copy(cif[:, 1, :], cia))

                def pick(t, half):
                    f4 = fidx.rearrange("p (h a) n -> p h a n", a=2)
                    oh = sc.rearrange("p s n -> p (s n)").rearrange("p (k j) -> p k j", j=TOPK)
                    rlink(t, nc.vector.tensor_tensor(oh, bc(cif[:, half, :].unsqueeze(2), [P, P, TOPK]),
                                                     bc(iota[:, :].unsqueeze(1), [P, P, TOPK]), ALU.is_equal))
                    oh4 = oh.rearrange("p (h k) j -> p h k j", h=PH)
                    rlink(t, nc.vector.tensor_tensor(oh4, oh4, bc(f4[:, :, half, :].unsqueeze(2), [P, PH, TOPK, TOPK]),
                                                     ALU.mult))
                    rlink(t, nc.vector.tensor_reduce(sel[:, half, :], oh, AX.X, ALU.add))

                def winners(t):
                    nc.vector.scalar_tensor_tensor(out=idx2[:, bass.ds((t % 2) * P, P)], in0=sel[:, 0, :],
                                                   scalar=float(NKEY), in1=sel[:, 1, :], op0=ALU.mult, op1=ALU.add)
                    nc.vector.tensor_tensor(ef, cval, bc(cval[:, :, 0:1], [P, PH, TOPK]), ALU.subtract
                                            ).then_inc(R["csub"], 1)
                    wait(dve, R["gexp"], t + 1)
                    rlink(t, nc.vector.tensor_reduce(ssum[:, 0:8], ef, AX.X, ALU.add))
                    rlink(t, nc.vector.reciprocal(small[:, 48:56], ssum[:, 0:8]))
                    rlink(t, nc.vector.tensor_tensor(
                        gate2[:, bass.ds((t % 2) * P, P)].rearrange("p (h n) -> p h n", h=PH),
                        ef, bc(small[:, 48:56].unsqueeze(2), [P, PH, TOPK]), ALU.mult))
                    assert rcount[0] == RLINKS, rcount[0]
                    rcount[0] = 0
                    dve.sem_inc(R["route_done"], 1)

                def turn(t, first=False, last=False):
                    keep_x(t)
                    half = TOPK // 2
                    route = {} if last else {
                        (4, half): lambda: top_keys(t + 1, 0), (5, 0): lambda: top_keys(t + 1, 1),
                        (5, half): lambda: top_sums(t + 1, 0), (6, 0): lambda: top_sums(t + 1, 1),
                        (6, half): lambda: top_sums(t + 1, 2), (7, 0): lambda: pick(t + 1, 0),
                        (7, half): lambda: (pick(t + 1, 1), winners(t + 1))}
                    if not first:
                        route[(1, half // 2)] = lambda: finish(t - 1)
                    for h in range(PH):
                        dot(t, h, {i: f for (hh, i), f in route.items() if hh == h})
                        weights(t, h)

                def heads(ap):
                    return ap.rearrange("p (h d) -> p h d", h=NH)

                def normalise(t):
                    o = 8 * (t % 2)
                    dve.wait_ge(sq_done, t + 1)
                    nc.vector.tensor_reduce(small[:, o:o + 8], heads(sq), AX.X, ALU.add).then_inc(ss_done, 1)
                    dve.wait_ge(rs_done, t + 1)
                    nc.vector.tensor_tensor(heads(mixo[:, t, GW:]), heads(mixo[:, t, GW:]),
                                            bc(small[:, 32 + o:40 + o].unsqueeze(2), [P, NH, HD]),
                                            ALU.mult).then_inc(vlink, 1)
                    dve.wait_ge(vlink, t + 1)
                    nc.vector.tensor_tensor(mixo[:, t, GW:], mixo[:, t, GW:], gain_fox[:, :],
                                            ALU.mult).then_inc(mix_done, 1)

                route0 = {5: lambda: top_keys(0, 0), 6: lambda: (top_keys(0, 1), top_sums(0, 0)),
                          7: lambda: (top_sums(0, 1), top_sums(0, 2)), 8: lambda: pick(0, 0),
                          9: lambda: (pick(0, 1), winners(0))}
                for t in range(TILES + 2):
                    if 1 <= t <= TILES:
                        dve.wait_ge(t_mm, t)
                        nc.vector.tensor_copy(mT[t - 1][:, 4:8, :], tp[:, 4:8, :]).then_inc(ev_v, 1)
                    if t >= 2:
                        m = t - 2
                        dve.wait_ge(y_mm, m + 1)
                        dve.wait_ge(x_in[m % 2], 16 * (m // 2 + 1))
                        for c in range(2):
                            last = nc.vector.tensor_tensor(xt[m % 2][:, 512 * c:512 * c + 512], oy[m % 2][c],
                                                           xt[m % 2][:, 512 * c:512 * c + 512], ALU.add)
                        last.then_inc(x1_done, 1)
                        dve.wait_ge(xrs, m + 1)
                        if m == 0:
                            dve.wait_ge(g2_in, 16)
                        nc.vector.scalar_tensor_tensor(out=xn[m], in0=xt[m % 2], scalar=small[:, 60:61],
                                                       in1=grow[:, :], op0=ALU.mult, op1=ALU.mult).then_inc(xn_done, 1)
                    for m in (2 * t, 2 * t + 1):
                        if m < TILES:
                            normalise(m)
                    if t in route0:
                        route0[t]()
                dve.wait_ge(xn_done, TILES)
                dve.wait_ge(x1_out[0], 16 * 5)
                turns(dve, lambda t: turn(t, first=True), turn, lambda t: turn(t, last=True))
                finish(TILES - 1)

        program(phase_norm)
        program(projection([RQ, RK, RV]))
        program(phase_retention)
        program(projection([RG, FQ, FK, FV]))
        recycle()
        program(phase_fox)
        program(phase_peer)


def shape_constants():
    f = np.float32
    n = np.arange(P)
    pos = np.empty((P, TILES), np.float64)
    for t in range(PT):
        pos[:, t] = t * P + n
    pos[:, ST] = PAST + n % NS
    inv = (10000.0 ** (-np.arange(32, dtype=f) / 32)).astype(f)
    ang = (pos.astype(f)[:, :, None] * inv[None, None, :]).astype(f).astype(np.float64)
    lg = np.log1p(-(2.0 ** (-5.0 - np.arange(NH))))
    step = np.stack([n + 1.0, n % NS + 1.0])
    grown = lg[None, None, :] * step[:, :, None]
    dec = np.stack([np.exp(grown), np.exp(-grown) * HD ** -0.5])
    span = np.array([P, NS])
    sdec = np.empty((P, 2, PAIRS))
    for par in range(2):
        for r in range(PAIRS):
            sdec[64 * par:64 * par + 64, :, r] = np.exp(lg[2 * r + par] * span)[None, :]
    same = (n[:, None] // NS) == (n[None, :] // NS)
    later = n[:, None] <= n[None, :]
    causal = np.stack([later, later & same], axis=1)
    maskq = np.where(n[None, :] > n[:, None], BIG, 0.0)
    maskn = np.where(np.arange(NS)[None, :] > (n % NS)[:, None], BIG, 0.0)
    e8 = np.zeros((NH, NH, P))
    e8[np.arange(NH), np.arange(NH), :] = 1.0
    e64 = np.zeros((NB * NH, NB, P))
    for b in range(NB):
        for m in range(P):
            e64[b * NH + m // NS, b, m] = 1.0
    return {
        "c_ident": np.eye(P, dtype=f), 
        "c_causal": causal.astype(f), "c_masks": np.concatenate([maskq, maskn], axis=1).astype(f),
         "c_cos": np.cos(ang).astype(f),
        "c_nsin": (-np.sin(ang)).astype(f), "c_psin": np.sin(ang).astype(f),
        "c_dec": np.ascontiguousarray(dec.transpose(2, 0, 1, 3)).astype(f), "c_sdec": sdec.astype(f),
        "c_bind": (n[:, None] // NS == np.arange(NB)[None, :]).astype(f),
        "c_iota": np.broadcast_to(np.arange(TOPK, dtype=f), (P, TOPK)).copy(),
        "c_e8": e8.astype(f), "c_e64": e64.astype(f),
    }


_DIRECT = ["x_prompt", "x_sample", "cache_fox_k", "cache_fox_v", "state_ret", "norm1_g", "w_in", "b_f", "fox_qn_g",
           "fox_kn_g", "ret_out_g", "fox_out_g", "w_out", "norm2_g", "peer_wq", "peer_u", "peer_v"]
_OUTS = [("y_prompt", (1, NP_TOK, D)), ("y_sample", (NB, NS, D)),
         ("new_fox_k_p", (1, 1, NP_TOK, NH, HD)), ("new_fox_v_p", (1, 1, NP_TOK, NH, HD)),
         ("new_fox_logf_p", (1, 1, NP_TOK, NH)), ("new_state_ret_p", (1, 1, NH, HD, HD)),
         ("new_fox_k_s", (1, NB, NS, NH, HD)), ("new_fox_v_s", (1, NB, NS, NH, HD)),
         ("new_fox_logf_s", (1, NB, NS, NH)), ("new_state_ret_s", (1, NB, NH, HD, HD))]


def kernel(**inputs):
    import concourse.bacc as _bacc
    from concourse.bass_utils import run_bass_kernel_spmd as _run

    nc = _bacc.Bacc("TRN2", target_bir_lowering=False, num_devices=1)
    data = {n: np.ascontiguousarray(inputs[n]) for n in _DIRECT}
    data["cache_lf_t"] = np.ascontiguousarray(
        np.asarray(inputs["cache_fox_logf"])[0].transpose(0, 2, 1).reshape(NB * NH, PAST))
    data["keys_t"] = np.ascontiguousarray(
        np.asarray(inputs["peer_keys"])[0].transpose(3, 1, 0, 2).reshape(P, 2 * PH, NKEY))
    data["c_wff"] = np.ascontiguousarray(
        np.asarray(inputs["w_in"])[0, :, 7 * GW:].reshape(KC, P, NH).transpose(1, 0, 2))
    data.update(shape_constants())
    arrays, a = {}, {}
    for name, v in data.items():
        arrays[f"in_{name}"] = v
        a[name] = nc.dram_tensor(f"in_{name}", v.shape, mybir.dt.from_np(v.dtype), kind="ExternalInput").ap()
    for name, shape in _OUTS:
        a[name] = nc.dram_tensor(f"out_{name}", shape, F32, kind="ExternalOutput").ap()
    a["xn"] = nc.dram_tensor("xn_scratch", (TILES, P, D), F32, kind="Internal").ap()
    a["x1"] = nc.dram_tensor("x1_scratch", (TILES, P, D), F32, kind="Internal").ap()
    emit(nc, a)
    r = _run(nc, [arrays], core_ids=[0])
    return tuple(r.results[0][f"out_{name}"] for name, _ in _OUTS)
```
